# Optimizing a Trainium2 kernel written in Bass

```python
import math
import jax, jax.numpy as jnp
from jax import lax
import numpy as np

D_MODEL = 1024
BATCH = 1
SEQ = 512
DEPTH = 2

HEAD_DIM = 64
BLOCK_Q = 128
NEG = -1e30
EPS = 1e-6
FORCE_BONUS = 1000.0

SB_HEADS = 4
SWA_HEADS = 4
SWA_KV_HEADS = 2
SWA_WINDOW = 128
NSA_HEADS = 4
NSA_KV_HEADS = 2
NSA_CMP_LEN = 32
NSA_CMP_STRIDE = 16
NSA_CMP_HIDDEN = 128
NSA_SEL_LEN = 64
NSA_TOPK = 16
NSA_WINDOW = 512
NSA_QBLOCK = 64
MLA_HEADS = 4
MLA_NOPE = 64
MLA_ROPE = 32
MLA_V = 64
MLA_Q_RANK = 192
MLA_KV_RANK = 128
ROPE_THETA = 10000.0
T5_BUCKETS = 32
T5_MAX_DIST = 1024
N_BIAS_HEADS = SWA_HEADS + NSA_HEADS
MOE_GROUPS = 4
MOE_EXPERTS_PER_GROUP = 8
MOE_EXPERTS = MOE_GROUPS * MOE_EXPERTS_PER_GROUP
MOE_HIDDEN = 256
MOE_TOPK = 2

IN_SPLITS = (SB_HEADS * HEAD_DIM, SB_HEADS * HEAD_DIM, SB_HEADS * HEAD_DIM,
             SWA_HEADS * HEAD_DIM, SWA_KV_HEADS * HEAD_DIM, SWA_KV_HEADS * HEAD_DIM,
             NSA_HEADS * HEAD_DIM,
             NSA_KV_HEADS * HEAD_DIM, NSA_KV_HEADS * HEAD_DIM,
             NSA_KV_HEADS * HEAD_DIM, NSA_KV_HEADS * HEAD_DIM,
             NSA_KV_HEADS * HEAD_DIM, NSA_KV_HEADS * HEAD_DIM,
             3 * NSA_HEADS,
             MLA_Q_RANK, MLA_KV_RANK, MLA_ROPE)
IN_COLS = (3 * SB_HEADS + SWA_HEADS + 2 * SWA_KV_HEADS + NSA_HEADS + 6 * NSA_KV_HEADS) * HEAD_DIM \
    + 3 * NSA_HEADS + MLA_Q_RANK + MLA_KV_RANK + MLA_ROPE
GROUP_WIDTH = 4 * HEAD_DIM
N_GROUPS_MIX = 4
MIX_WIDTH = N_GROUPS_MIX * GROUP_WIDTH

kernel_name = "hymba_style_sb_swa_nsa_mla_hmoe"

def rms_norm(x, g):
    xf = x.astype(jnp.float32)
    y = xf * lax.rsqrt(jnp.mean(xf * xf, axis=-1, keepdims=True) + EPS)
    return (y * g.astype(jnp.float32)).astype(x.dtype)

def t5_bucket(dist):
    n = jnp.maximum(dist, 0)
    max_exact = T5_BUCKETS // 2
    nf = jnp.maximum(n, 1).astype(jnp.float32)
    large = max_exact + (jnp.log(nf / max_exact) / math.log(T5_MAX_DIST / max_exact)
                         * (T5_BUCKETS - max_exact)).astype(jnp.int32)
    large = jnp.minimum(large, T5_BUCKETS - 1)
    return jnp.where(n < max_exact, n, large)

def masked_softmax(logits, mask, sink=None):
    l = jnp.where(mask, logits, NEG)
    m = jnp.max(l, axis=-1, keepdims=True)
    if sink is not None:
        m = jnp.maximum(m, sink)
    p = jnp.where(mask, jnp.exp(l - m), 0.0)
    denom = jnp.sum(p, axis=-1, keepdims=True)
    if sink is not None:
        denom = denom + jnp.exp(sink - m)
    return p / jnp.maximum(denom, 1e-30)

def rope(x, cos, sin):
    half = x.shape[-1] // 2
    xf = x.astype(jnp.float32)
    x1, x2 = xf[..., :half], xf[..., half:]
    c = cos[None, :, None, :]
    s = sin[None, :, None, :]
    return jnp.concatenate([x1 * c - x2 * s, x1 * s + x2 * c], axis=-1).astype(x.dtype)

def stick_breaking_attention(q, k, v):
    B, S, H, d = q.shape
    scale = d ** -0.5
    k_pos = jnp.arange(S)

    def block(i):
        start = i * BLOCK_Q
        qi = lax.dynamic_slice_in_dim(q, start, BLOCK_Q, axis=1)
        q_pos = start + jnp.arange(BLOCK_Q)
        mask = k_pos[None, :] < q_pos[:, None]
        z = jnp.einsum('bqhd,bkhd->bhqk', qi, k).astype(jnp.float32) * scale
        log_keep = jnp.where(mask, jax.nn.log_sigmoid(-z), 0.0)
        after = lax.cumsum(log_keep, axis=3, reverse=True) - log_keep
        a = jnp.where(mask, jnp.exp(jax.nn.log_sigmoid(z) + after), 0.0)
        return jnp.einsum('bhqk,bkhd->bqhd', a.astype(v.dtype), v)

    out = lax.map(block, jnp.arange(S // BLOCK_Q))
    return jnp.moveaxis(out, 0, 1).reshape(B, S, H, d)

def banded_attention(q, k, v, window, bias_tbl, sinks):
    B, S, H, d = q.shape
    Hk = k.shape[2]
    grp = H // Hk
    nprev = -(-(window - 1) // BLOCK_Q)
    pad = nprev * BLOCK_Q
    span = pad + BLOCK_Q
    kp = jnp.pad(k, ((0, 0), (pad, 0), (0, 0), (0, 0)))
    vp = jnp.pad(v, ((0, 0), (pad, 0), (0, 0), (0, 0)))
    qg = q.reshape(B, S, Hk, grp, d)
    tbl = bias_tbl.reshape(Hk, grp, T5_BUCKETS)
    snk = None if sinks is None else sinks.reshape(Hk, grp, 1, 1).astype(jnp.float32)
    scale = d ** -0.5

    def block(i):
        start = i * BLOCK_Q
        qi = lax.dynamic_slice_in_dim(qg, start, BLOCK_Q, axis=1)
        ki = lax.dynamic_slice_in_dim(kp, start, span, axis=1)
        vi = lax.dynamic_slice_in_dim(vp, start, span, axis=1)
        q_pos = start + jnp.arange(BLOCK_Q)
        k_pos = start - pad + jnp.arange(span)
        dist = q_pos[:, None] - k_pos[None, :]
        mask = (dist >= 0) & (dist < window) & (k_pos[None, :] >= 0)
        logits = jnp.einsum('bqhgd,bkhd->bhgqk', qi, ki).astype(jnp.float32) * scale
        logits = logits + tbl[:, :, t5_bucket(dist)].astype(jnp.float32)
        p = masked_softmax(logits, mask, snk)
        return jnp.einsum('bhgqk,bkhd->bqhgd', p.astype(v.dtype), vi)

    out = lax.map(block, jnp.arange(S // BLOCK_Q))
    return jnp.moveaxis(out, 0, 1).reshape(B, S, H, d)

def causal_attention(q, k, v):
    B, S, H, dk = q.shape
    dv = v.shape[-1]
    scale = dk ** -0.5
    k_pos = jnp.arange(S)

    def block(i):
        start = i * BLOCK_Q
        qi = lax.dynamic_slice_in_dim(q, start, BLOCK_Q, axis=1)
        q_pos = start + jnp.arange(BLOCK_Q)
        mask = k_pos[None, :] <= q_pos[:, None]
        logits = jnp.einsum('bqhd,bkhd->bhqk', qi, k).astype(jnp.float32) * scale
        p = masked_softmax(logits, mask)
        return jnp.einsum('bhqk,bkhd->bqhd', p.astype(v.dtype), v)

    out = lax.map(block, jnp.arange(S // BLOCK_Q))
    return jnp.moveaxis(out, 0, 1).reshape(B, S, H, dv)

def nsa_compress(x, pos, w1, w2):
    B, S, Hk, d = x.shape
    n_cat = NSA_CMP_LEN // NSA_CMP_STRIDE
    nb = S // NSA_CMP_STRIDE
    nc = nb - n_cat + 1
    xb = x.reshape(B, nb, NSA_CMP_STRIDE, Hk, d)
    win = jnp.concatenate([xb[:, j:j + nc] for j in range(n_cat)], axis=2)
    win = win + pos[None, None, :, None, :]
    h = jax.nn.gelu(jnp.einsum('bnlhd,ldf->bnhf', win, w1))
    return jnp.einsum('bnhf,fe->bnhe', h, w2)

def nsa_attention(q, k_cmp, v_cmp, k_slc, v_slc, k_win, v_win, gates, bias_tbl):
    B, S, H, d = q.shape
    Hk = k_slc.shape[2]
    grp = H // Hk
    nc = k_cmp.shape[1]
    n_sel = S // NSA_SEL_LEN
    topk = min(NSA_TOPK, n_sel)
    span_sel = topk * NSA_SEL_LEN
    scale = d ** -0.5
    tbl = bias_tbl.reshape(Hk, grp, T5_BUCKETS)
    qg = q.reshape(B, S, Hk, grp, d)
    cmp_start = jnp.arange(nc) * NSA_CMP_STRIDE
    cmp_end = cmp_start + NSA_CMP_LEN - 1
    sel_idx = jnp.arange(n_sel)
    sel_start = sel_idx * NSA_SEL_LEN
    overlap = ((cmp_start[:, None] < sel_start[None, :] + NSA_SEL_LEN)
               & (cmp_end[:, None] >= sel_start[None, :])).astype(jnp.float32)
    ks_blk = k_slc.reshape(B, n_sel, NSA_SEL_LEN, Hk, d).transpose(0, 3, 1, 2, 4)
    vs_blk = v_slc.reshape(B, n_sel, NSA_SEL_LEN, Hk, d).transpose(0, 3, 1, 2, 4)
    b_ix = jnp.arange(B)[:, None, None, None]
    h_ix = jnp.arange(Hk)[None, :, None, None]
    hh = jnp.arange(Hk)[:, None, None, None, None]
    gg = jnp.arange(grp)[None, :, None, None, None]
    tok_off = jnp.arange(NSA_SEL_LEN)

    def block(i):
        start = i * NSA_QBLOCK
        qi = lax.dynamic_slice_in_dim(qg, start, NSA_QBLOCK, axis=1)
        q_pos = start + jnp.arange(NSA_QBLOCK)
        dist_c = q_pos[:, None] - cmp_end[None, :]
        mask_c = dist_c >= 0
        lc = jnp.einsum('bqhgd,bnhd->bhgqn', qi, k_cmp).astype(jnp.float32) * scale
        lc = lc + tbl[:, :, t5_bucket(dist_c)].astype(jnp.float32)
        pc = masked_softmax(lc, mask_c)
        o_c = jnp.einsum('bhgqn,bnhd->bqhgd', pc.astype(v_cmp.dtype), v_cmp)
        imp = jnp.einsum('bhgqn,nj->bhqj', pc, overlap)
        cur = q_pos // NSA_SEL_LEN
        forced = ((sel_idx[None, :] == 0) | (sel_idx[None, :] == cur[:, None])
                  | (sel_idx[None, :] == cur[:, None] - 1))
        valid = sel_start[None, :] <= q_pos[:, None]
        score = jnp.where(valid, imp + jnp.where(forced, FORCE_BONUS, 0.0), NEG)
        _, idx = lax.top_k(score, topk)
        ksel = ks_blk[b_ix, h_ix, idx]
        vsel = vs_blk[b_ix, h_ix, idx]
        key_pos = idx[..., None] * NSA_SEL_LEN + tok_off
        dist_s = q_pos[None, None, :, None, None] - key_pos
        ls = jnp.einsum('bqhgd,bhqkld->bhgqkl', qi, ksel).astype(jnp.float32) * scale
        ls = ls + tbl[hh, gg, t5_bucket(dist_s)[:, :, None]].astype(jnp.float32)
        ls = ls.reshape(B, Hk, grp, NSA_QBLOCK, span_sel)
        mask_s = (dist_s >= 0).reshape(B, Hk, 1, NSA_QBLOCK, span_sel)
        ps = masked_softmax(ls, mask_s)
        o_s = jnp.einsum('bhgqm,bhqmd->bqhgd', ps.astype(v_slc.dtype),
                         vsel.reshape(B, Hk, NSA_QBLOCK, span_sel, d))
        return o_c, o_s

    o_c, o_s = lax.map(block, jnp.arange(S // NSA_QBLOCK))
    o_c = jnp.moveaxis(o_c, 0, 1).reshape(B, S, H, d)
    o_s = jnp.moveaxis(o_s, 0, 1).reshape(B, S, H, d)
    o_w = banded_attention(q, k_win, v_win, NSA_WINDOW, bias_tbl, None)
    return (gates[:, :, 0, :, None] * o_c + gates[:, :, 1, :, None] * o_s
            + gates[:, :, 2, :, None] * o_w)

def mla_attention(c_q, c_kv, k_pe, q_lat_g, w_q_up, kv_lat_g, w_kv_up, q_g, k_g, cos, sin):
    B, S, _ = c_q.shape
    q = (rms_norm(c_q, q_lat_g) @ w_q_up).reshape(B, S, MLA_HEADS, MLA_NOPE + MLA_ROPE)
    kv = (rms_norm(c_kv, kv_lat_g) @ w_kv_up).reshape(B, S, MLA_HEADS, MLA_NOPE + MLA_V)
    k_nope, v = kv[..., :MLA_NOPE], kv[..., MLA_NOPE:]
    k = jnp.concatenate([k_nope, jnp.broadcast_to(k_pe[:, :, None, :], (B, S, MLA_HEADS, MLA_ROPE))], axis=-1)
    q = rms_norm(q, q_g)
    k = rms_norm(k, k_g)
    q = jnp.concatenate([q[..., :MLA_NOPE], rope(q[..., MLA_NOPE:], cos, sin)], axis=-1)
    k = jnp.concatenate([k[..., :MLA_NOPE], rope(k[..., MLA_NOPE:], cos, sin)], axis=-1)
    return causal_attention(q, k, v)

def mixer(h, rel_bias, cos, sin, w_in, swa_q_norm, swa_k_norm, swa_sinks, nsa_q_norm,
          nsa_k_norm, nsa_cmp_pos, nsa_cmp_w1, nsa_cmp_w2, mla_q_lat_norm, mla_w_q_up,
          mla_kv_lat_norm, mla_w_kv_up, mla_q_norm, mla_k_norm, out_norm, w_out):
    B, S, _ = h.shape
    proj = h @ w_in
    parts = []
    off = 0
    for n in IN_SPLITS:
        parts.append(proj[..., off:off + n])
        off += n
    (sb_q, sb_k, sb_v, swa_q, swa_k, swa_v, nsa_q, nsa_kc, nsa_vc, nsa_ks, nsa_vs,
     nsa_kw, nsa_vw, nsa_g, mla_cq, mla_ckv, mla_kpe) = parts

    def heads(t):
        return t.reshape(B, S, -1, HEAD_DIM)

    o_a = stick_breaking_attention(heads(sb_q), heads(sb_k), heads(sb_v))
    o_b = banded_attention(rms_norm(heads(swa_q), swa_q_norm), rms_norm(heads(swa_k), swa_k_norm),
                           heads(swa_v), SWA_WINDOW, rel_bias[:, :SWA_HEADS].T, swa_sinks)
    k_cmp = rms_norm(nsa_compress(heads(nsa_kc), nsa_cmp_pos[0], nsa_cmp_w1[0], nsa_cmp_w2[0]), nsa_k_norm[0])
    v_cmp = nsa_compress(heads(nsa_vc), nsa_cmp_pos[1], nsa_cmp_w1[1], nsa_cmp_w2[1])
    gates = jax.nn.sigmoid(nsa_g.reshape(B, S, 3, NSA_HEADS))
    o_c = nsa_attention(rms_norm(heads(nsa_q), nsa_q_norm), k_cmp, v_cmp,
                        rms_norm(heads(nsa_ks), nsa_k_norm[1]), heads(nsa_vs),
                        rms_norm(heads(nsa_kw), nsa_k_norm[2]), heads(nsa_vw),
                        gates, rel_bias[:, SWA_HEADS:].T)
    o_d = mla_attention(mla_cq, mla_ckv, mla_kpe, mla_q_lat_norm, mla_w_q_up, mla_kv_lat_norm,
                        mla_w_kv_up, mla_q_norm, mla_k_norm, cos, sin)
    o = jnp.stack([o_a.reshape(B, S, GROUP_WIDTH), o_b.reshape(B, S, GROUP_WIDTH),
                   o_c.reshape(B, S, GROUP_WIDTH), o_d.reshape(B, S, GROUP_WIDTH)], axis=2)
    o = rms_norm(o, out_norm.reshape(N_GROUPS_MIX, GROUP_WIDTH)).reshape(B, S, MIX_WIDTH)
    return o @ w_out

def hier_moe(h, w_group, b_group, w_expert, b_expert, w_gate, w_up, w_down):
    B, S, D = h.shape
    t = h.reshape(B * S, D)
    g_logits = (t @ w_group).astype(jnp.float32) + b_group.astype(jnp.float32)
    g_prob = jax.nn.softmax(g_logits, axis=-1)
    g_star = jnp.argmax(g_logits, axis=-1)
    g_w = jnp.max(g_prob, axis=-1, keepdims=True)
    e_logits = ((t @ w_expert).astype(jnp.float32) + b_expert.astype(jnp.float32)
                ).reshape(-1, MOE_GROUPS, MOE_EXPERTS_PER_GROUP)
    e_in = e_logits[jnp.arange(t.shape[0]), g_star]
    e_prob = jax.nn.softmax(e_in, axis=-1)
    top_p, top_i = lax.top_k(e_prob, MOE_TOPK)
    top_w = top_p / jnp.sum(top_p, axis=-1, keepdims=True) * g_w
    expert_id = g_star[:, None] * MOE_EXPERTS_PER_GROUP + top_i
    combine = jnp.sum(jax.nn.one_hot(expert_id, MOE_EXPERTS, dtype=jnp.float32)
                      * top_w[..., None], axis=1).astype(t.dtype)
    y = jnp.zeros_like(t)
    for e in range(MOE_EXPERTS):
        a = jax.nn.silu(t @ w_gate[e]) * (t @ w_up[e])
        y = y + combine[:, e:e + 1] * (a @ w_down[e])
    return y.reshape(B, S, D)

def setup_inputs(seed: int = 0) -> dict:
    key = jax.random.key(seed)
    ks = jax.random.split(key, 28)
    f32 = jnp.float32
    L = DEPTH

    def nrm(k, shape, scale):
        return jax.random.normal(k, shape, f32) * scale

    def gain(k, shape):
        return 1.0 + 0.02 * jax.random.normal(k, shape, f32)

    return {
        "x": nrm(ks[0], (BATCH, SEQ, D_MODEL), 1.0),
        "rel_bias": nrm(ks[1], (T5_BUCKETS, N_BIAS_HEADS), 0.5),
        "attn_norm": gain(ks[2], (L, D_MODEL)),
        "w_in": nrm(ks[3], (L, D_MODEL, IN_COLS), D_MODEL ** -0.5),
        "swa_q_norm": gain(ks[4], (L, HEAD_DIM)),
        "swa_k_norm": gain(ks[5], (L, HEAD_DIM)),
        "swa_sinks": nrm(ks[6], (L, SWA_HEADS), 0.5),
        "nsa_q_norm": gain(ks[7], (L, HEAD_DIM)),
        "nsa_k_norm": gain(ks[8], (L, 3, HEAD_DIM)),
        "nsa_cmp_pos": nrm(ks[9], (L, 2, NSA_CMP_LEN, HEAD_DIM), 0.1),
        "nsa_cmp_w1": nrm(ks[10], (L, 2, NSA_CMP_LEN, HEAD_DIM, NSA_CMP_HIDDEN), (NSA_CMP_LEN * HEAD_DIM) ** -0.5),
        "nsa_cmp_w2": nrm(ks[11], (L, 2, NSA_CMP_HIDDEN, HEAD_DIM), NSA_CMP_HIDDEN ** -0.5),
        "mla_q_lat_norm": gain(ks[12], (L, MLA_Q_RANK)),
        "mla_w_q_up": nrm(ks[13], (L, MLA_Q_RANK, MLA_HEADS * (MLA_NOPE + MLA_ROPE)), MLA_Q_RANK ** -0.5),
        "mla_kv_lat_norm": gain(ks[14], (L, MLA_KV_RANK)),
        "mla_w_kv_up": nrm(ks[15], (L, MLA_KV_RANK, MLA_HEADS * (MLA_NOPE + MLA_V)), MLA_KV_RANK ** -0.5),
        "mla_q_norm": gain(ks[16], (L, MLA_NOPE + MLA_ROPE)),
        "mla_k_norm": gain(ks[17], (L, MLA_NOPE + MLA_ROPE)),
        "out_norm": gain(ks[18], (L, MIX_WIDTH)),
        "w_out": nrm(ks[19], (L, MIX_WIDTH, D_MODEL), MIX_WIDTH ** -0.5),
        "ffn_norm": gain(ks[20], (L, D_MODEL)),
        "moe_w_group": nrm(ks[21], (L, D_MODEL, MOE_GROUPS), D_MODEL ** -0.5),
        "moe_b_group": nrm(ks[22], (L, MOE_GROUPS), 0.01),
        "moe_w_expert": nrm(ks[23], (L, D_MODEL, MOE_EXPERTS), D_MODEL ** -0.5),
        "moe_b_expert": nrm(ks[24], (L, MOE_EXPERTS), 0.01),
        "moe_w_gate": nrm(ks[25], (L, MOE_EXPERTS, D_MODEL, MOE_HIDDEN), D_MODEL ** -0.5),
        "moe_w_up": nrm(ks[26], (L, MOE_EXPERTS, D_MODEL, MOE_HIDDEN), D_MODEL ** -0.5),
        "moe_w_down": nrm(ks[27], (L, MOE_EXPERTS, MOE_HIDDEN, D_MODEL), MOE_HIDDEN ** -0.5),
    }

def reference(x, rel_bias, attn_norm, w_in, swa_q_norm, swa_k_norm, swa_sinks, nsa_q_norm,
              nsa_k_norm, nsa_cmp_pos, nsa_cmp_w1, nsa_cmp_w2, mla_q_lat_norm, mla_w_q_up,
              mla_kv_lat_norm, mla_w_kv_up, mla_q_norm, mla_k_norm, out_norm, w_out, ffn_norm,
              moe_w_group, moe_b_group, moe_w_expert, moe_b_expert, moe_w_gate, moe_w_up,
              moe_w_down):
    S = x.shape[1]
    pos = jnp.arange(S, dtype=jnp.float32)
    inv_freq = ROPE_THETA ** (-jnp.arange(0, MLA_ROPE, 2, dtype=jnp.float32) / MLA_ROPE)
    ang = pos[:, None] * inv_freq[None, :]
    cos, sin = jnp.cos(ang), jnp.sin(ang)
    for l in range(DEPTH):
        h = rms_norm(x, attn_norm[l])
        x = x + mixer(h, rel_bias, cos, sin, w_in[l], swa_q_norm[l], swa_k_norm[l], swa_sinks[l],
                      nsa_q_norm[l], nsa_k_norm[l], nsa_cmp_pos[l], nsa_cmp_w1[l], nsa_cmp_w2[l],
                      mla_q_lat_norm[l], mla_w_q_up[l], mla_kv_lat_norm[l], mla_w_kv_up[l],
                      mla_q_norm[l], mla_k_norm[l], out_norm[l], w_out[l])
        h = rms_norm(x, ffn_norm[l])
        x = x + hier_moe(h, moe_w_group[l], moe_b_group[l], moe_w_expert[l], moe_b_expert[l],
                         moe_w_gate[l], moe_w_up[l], moe_w_down[l])
    return x


_drawn_inputs = setup_inputs


def setup_inputs(seed=0):
    import zlib

    import numpy as np

    out = dict(_drawn_inputs(seed))
    spreads = {}
    factors = {'swa_q_norm': 2.814,
     'swa_k_norm': 3.238,
     'swa_sinks': 3.195,
     'nsa_q_norm': 4.976,
     'nsa_k_norm': 4.754,
     'mla_q_lat_norm': 3.276,
     'mla_k_norm': 2.918,
     'moe_b_group': 3.033,
     'moe_b_expert': 4.817}
    for name, (base, spread) in spreads.items():
        noise = np.random.default_rng([zlib.crc32(name.encode()), seed]).standard_normal(out[name].shape)
        drawn = base * np.exp(spread * noise) if base else spread * noise
        out[name] = __import__('jax').numpy.asarray(drawn.astype(out[name].dtype))
    for name, factor in factors.items():
        out[name] = (out[name] * factor).astype(out[name].dtype)
    return out
```

```python
import math
from contextlib import ExitStack

import numpy as np

import concourse.bass as bass
from concourse import mybir

ALU = mybir.AluOpType
ACT = mybir.ActivationFunctionType
AX = mybir.AxisListType
F32 = mybir.dt.float32
I32 = mybir.dt.int32
U32 = mybir.dt.uint32

P = 128
T = 512
NT = T // P
D = 1024
KC = D // P
L = 2
HD = 64
EPS = 1e-6
BIG = 1e30

SBQ, SBK, SBV = 0, 256, 512
SWQ, SWK, SWV = 768, 1024, 1152
NQ, NKC, NVC, NKS, NVS, NKW, NVW, NG = 1280, 1536, 1664, 1792, 1920, 2048, 2176, 2304
MCQ, MCKV, MKPE, COLS = 2316, 2508, 2636, 2668
WCH = 512
CHUNKS = [(c, min(WCH, COLS - c)) for c in range(0, COLS, WCH)]

QR, KVR, NOPE, ROPE = 192, 128, 64, 32
MQK = NOPE + ROPE
HALF = ROPE // 2
CMP_L, CMP_S, CMP_H = 32, 16, 128
NCMP = T // CMP_S - 1
BUCKETS = 32

NGRP, EPG, NE = 4, 8, 32
FH = 256
S = 64
NOVER = 2 * T // S - 1
NTILE = NE + NOVER
NSLOT = NTILE * S

UN = 896
TN = UN + P - 1
US = 256
TS = US + P - 1

C_ID, C_TRI, C_CM, C_SM, C_COS, C_SIN, C_IM, C_E64, C_E, C_K = np.cumsum([0, P, P, T, T, 64, 64, NE, NE, NE]).tolist()
NCON = C_K + 16

SL_A, SL_B, SL_C, SL_D, SL_X = 0, 8, 14, 22, 30
NSL = 34


def t5_bucket(n):
    n = np.maximum(n, 0)
    half = BUCKETS // 2
    nf = np.maximum(n, 1).astype(np.float32)
    large = half + (np.log(nf / np.float32(half)) / np.float32(math.log(1024 / half)) * np.float32(BUCKETS - half)).astype(np.int32)
    return np.where(n < half, n, np.minimum(large, BUCKETS - 1))


def constants():
    c = np.zeros((P, NCON), np.float32)
    p = np.arange(P)[:, None]
    c[:, C_ID:C_ID + P] = np.eye(P)
    c[:, C_TRI:C_TRI + P] = p < np.arange(P)[None]
    dist = p + 384 - np.arange(T)[None]
    c[:, C_CM:C_CM + T] = np.where(dist >= 0, 0, BIG)
    c[:, C_SM:C_SM + T] = np.where(dist > 0, 0, -BIG)
    inv = (np.float32(10000.0) ** (-np.arange(0, ROPE, 2, dtype=np.float32) / np.float32(ROPE))).astype(np.float32)
    ang = (np.arange(T, dtype=np.float32)[:, None] * inv[None]).astype(np.float32).reshape(NT, P, HALF)
    c[:, C_COS:C_COS + 64] = np.cos(ang).transpose(1, 0, 2).reshape(P, 64)
    c[:, C_SIN:C_SIN + 64] = np.sin(ang).transpose(1, 0, 2).reshape(P, 64)
    c[:, C_IM:C_IM + NE] = np.arange(NE) - 1000
    c[:, C_E64:C_E64 + NE] = np.arange(NE) * S
    c[:, C_E:C_E + NE] = np.arange(NE)
    c[:, C_K:C_K + 16] = np.arange(16)
    m = np.zeros((BUCKETS + 1, TN + TS), np.float32)
    dn = T - 1 - np.arange(TN)
    ds = US - 1 - np.arange(TS)
    m[t5_bucket(dn), np.arange(TN)] = 1
    m[t5_bucket(ds), TN + np.arange(TS)] = 1
    m[BUCKETS, :TN] = np.where(dn >= 0, 0, -BIG)
    m[BUCKETS, TN:] = np.where((ds >= 0) & (ds < P), 0, -BIG)
    return c, m


def build(nc, a, consts, bias_map, out, bias_rows, xs_dram, ys_dram):
    with ExitStack() as ctx:
        def sb(name, shape, dt=F32):
            return ctx.enter_context(nc.sbuf_tensor(name, shape, dt))

        def sem(name):
            return ctx.enter_context(nc.semaphore(name))

        con = sb("con", [P, NCON])
        ones = sb("ones", [P, P])
        neghalf = sb("neghalf", [P, 64])
        x = sb("x", [P, NT, D])
        xo = sb("xo", [P, NT * D])
        hT = sb("hT", [P, NT * D])
        big = sb("big", [P, NT * COLS + NSL * T])
        sq = sb("sq", [P, 3584])
        gn = sb("gn", [P, 4, UN])
        gs = sb("gs", [P, 4, US])
        relx = sb("relx", [BUCKETS + 1, 8])
        g_attn, g_out, g_ffn = sb("g_attn", [P, KC]), sb("g_out", [P, KC]), sb("g_ffn", [P, KC])
        g64 = sb("g64", [HD, 6])
        g_lq, g_lkv, g_qk = sb("g_lq", [MQK, 2]), sb("g_lkv", [KVR, 1]), sb("g_qk", [P, 2, MQK])
        sink, nsink = sb("sink", [P, 4]), sb("nsink", [P, 4])
        cpos, cposT = sb("cpos", [2 * CMP_L, HD]), sb("cposT", [HD, 2 * CMP_L])
        w_cmp2 = sb("w_cmp2", [P, 2, HD])
        rbias, w_rt = sb("rbias", [P, 36]), sb("w_rt", [P, KC, 36])
        ss, rs = sb("ss", [P, 64]), sb("rs", [P, 64])
        gates = sb("gates", [P, NT, 12])
        hcmp = sb("hcmp", [P, 2, 2, 32])
        kcmp, vcmp = sb("kcmp", [NCMP, 2, HD]), sb("vcmp", [NCMP, 2, HD])
        kcmpT = sb("kcmpT", [HD, 2, 32])
        csq, css = sb("csq", [NCMP, 2, HD]), sb("css", [NCMP, 4])
        mrow, den = sb("mrow", [P, 96]), sb("den", [P, 96])
        den2, esink = sb("den2", [P, 4]), sb("esink", [P, 4 * NT])
        g64q = sb("g64q", [HD, 2])
        otmp = sb("otmp", [P, NT, HD])
        lg = sb("lg", [P, NT, 36])
        rsm = sb("rsm", [P, 12, NT])
        goh, gex = sb("goh", [P, NT, NGRP]), sb("gex", [P, NT, NGRP])
        row, rowi = sb("row", [P, 6, NE]), sb("rowi", [P, NE], I32)
        slotf, sloti = sb("slotf", [P, 2, NT]), sb("sloti", [P, 2, NT], U32)
        overi = sb("overi", [1, 16], I32)
        overf = sb("overf", [1, 16])
        rt = sq[:, 1024:1024 + 10 * NT * NE].rearrange("p (a t e) -> p a t e", a=10, t=NT)
        over = sq[0:1, 0:2 * 16 * NE].rearrange("p (a k e) -> p a k e", a=2, k=16)
        sg = hT[:, 3072:3072 + 4 * S].rearrange("p (i c) -> p i c", i=2)
        aT = hT[:, 3072 + 4 * S:3072 + 8 * S].rearrange("p (i c s) -> p i c s", i=2, c=2)

        ps = ctx.enter_context(nc.psum_tensor("ps", [P, 8, 512], F32))

        ident = con[:, C_ID:C_ID + P]
        hTc = hT[:, :].rearrange("p (k t) -> p k t", k=KC)
        xoc = xo[:, :].rearrange("p (t d) -> p t d", t=NT)
        proj = big[:, 0:NT * COLS].rearrange("p (t c) -> p t c", t=NT)
        heads = big[:, NT * COLS:].rearrange("p (s t) -> p s t", s=NSL)
        base = NT * COLS
        win = [big[:, base + i * KC * WCH:base + (i + 1) * KC * WCH].rearrange("p (k n) -> p k n", k=KC) for i in range(2)]
        bmap = big[0:BUCKETS + 1, base + 20 * T:base + 23 * T]
        w_qup = big[0:MQK, base + (SL_D + 3) * T:base + (SL_D + 3) * T + 2 * 384].rearrange("p (c n) -> p c n", c=2)
        w_kvup = heads[:, SL_D + 5, :]
        w1 = [xo[0:HD, 0:CMP_L * CMP_H].rearrange("p (l f) -> p l f", l=CMP_L),
              big[0:HD, base + SL_D * T:base + (SL_D + 8) * T].rearrange("p (l f) -> p l f", l=CMP_L)]
        w_o = big[:, 0:KC * D].rearrange("p (k n) -> p k n", k=KC)
        RING0 = KC * D
        EW = 3 * KC * FH
        ring_g, ring_u, ring_d = [], [], []
        for s in range(2):
            b = RING0 + s * EW
            ring_g.append(big[:, b:b + KC * FH].rearrange("p (k f) -> p k f", k=KC))
            ring_u.append(big[:, b + KC * FH:b + 2 * KC * FH].rearrange("p (k f) -> p k f", k=KC))
            ring_d.append(big[:, b + 2 * KC * FH:b + EW].rearrange("p (c n) -> p c n", c=2))
        yg = [big[:, i * D:(i + 1) * D] for i in range(8)]
        sqh = sq[:, :].rearrange("p (t c) -> p t c", t=NT)
        dqk = sq[:, 0:NT * 8 * MQK].rearrange("p (t h c) -> p t h c", t=NT, h=8)
        dsq = hT[:, 0:NT * 8 * MQK].rearrange("p (t h c) -> p t h c", t=NT, h=8)
        dtm = [hT[:, i * 512:(i + 1) * 512].rearrange("p (t h c) -> p t h c", t=NT, h=8) for i in range(4)]
        lgt = [hT[:, i * T:(i + 1) * T] for i in range(3)]
        prb = [hT[:, (3 + i) * T:(4 + i) * T] for i in range(2)]
        prT = [hT[:, (5 + i) * T:(6 + i) * T] for i in range(2)]
        keep = [sq[:, i * T:(i + 1) * T] for i in range(2)]
        left = [sq[:, 1024 + i * 520:1024 + i * 520 + T + 1] for i in range(2)]
        xe = [hT[0:S, i * D:(i + 1) * D] for i in range(2)]
        xeT = [hT[:, 2048 + i * T:2048 + (i + 1) * T].rearrange("p (k s) -> p k s", k=KC) for i in range(2)]
        ye = [sq[0:S, i * D:(i + 1) * D] for i in range(2)]

        setup_in, setup_dve, bias_mm, bias_neg, bias_out, bias_in, zeros_rdy, zeroed, layer_open, entered, scat, gath, out_done = [
            sem(n) for n in "setup_in setup_dve bias_mm bias_neg bias_out bias_in zeros_rdy zeroed layer_open entered scat gath out_done".split()]
        per_layer = ("sp_done pe_done act_done dve_done params win_a win_b w1_in w1v_in wout_in dve_step sum_rdy ms_rdy rs_rdy xn_rdy "
                     "tr_act tr_dve ev_act ev_dve pj_mm pj_ev_act pj_ev_dve norms_rdy up_mm up_ev_act up_ev_dve "
                     "cmp_mm cmp_ev cmp_out cmp_n cmpT_mm cmpT_ev dqk_rdy sq_rdy scores logits probs_sm sig probs_sb "
                     "probT probT_ev pv head_out esink_rdy o_rdy wo_mm wo_ev lg_mm rt_in rt_exp assign pos_mm slots_rdy "
                     "wg0 wg1 wu0 wu1 wd0 wd1 xe0 xe1 xeT_mm xeT_ev gu_mm silu_rdy a_rdy dn_mm y_act y_dve "
                     "yst0 yst1 f_in f_step f_loop f_T f_Tev f_gu f_silu f_a f_dn f_yact f_ydve f_st f_end comb").split()
        s_ = {n: sem(n) for n in per_layer}

        def after(ins, s, n=1):
            return ins.then_inc(s_[s], n)

        block = ctx.enter_context(nc.Block())

        def enter(eng, l):
            eng.wait_ge(layer_open, l + 1)
            eng.sem_inc(entered, 1)

        def params(l):
            def of(name):
                return a[name][bass.ds(l, 1)]
            return [
                (g_attn[:, :], of("attn_norm").rearrange("o (p k) -> p (o k)", k=KC)),
                (g_out[:, :], of("out_norm").rearrange("o (p k) -> p (o k)", k=KC)),
                (g_ffn[:, :], of("ffn_norm").rearrange("o (p k) -> p (o k)", k=KC)),
                (g64[:, 0:1], of("swa_q_norm").rearrange("o p -> p o")),
                (g64[:, 1:2], of("swa_k_norm").rearrange("o p -> p o")),
                (g64[:, 2:3], of("nsa_q_norm").rearrange("o p -> p o")),
                (g64[:, 3:4], of("nsa_k_norm")[:, 0].rearrange("o p -> p o")),
                (g64[:, 4:5], of("nsa_k_norm")[:, 1].rearrange("o p -> p o")),
                (g64[:, 5:6], of("nsa_k_norm")[:, 2].rearrange("o p -> p o")),
                (g_lq[:, :], of("mla_q_lat_norm").rearrange("o (p k) -> p (o k)", k=2)),
                (g_lkv[:, :], of("mla_kv_lat_norm").rearrange("o p -> p o")),
                (g_qk[:, 0, :], of("mla_q_norm").broadcast_to([P, MQK])),
                (g_qk[:, 1, :], of("mla_k_norm").broadcast_to([P, MQK])),
                (sink[:, :], of("swa_sinks").broadcast_to([P, 4])),
                (cpos[:, :], of("nsa_cmp_pos").rearrange("o c l d -> (o c l) d")),
                (w_cmp2[:, :, :], of("nsa_cmp_w2").rearrange("o c f d -> f (o c) d")),
                (rbias[:, 0:NGRP], of("moe_b_group").broadcast_to([P, NGRP])),
                (rbias[:, NGRP:], of("moe_b_expert").broadcast_to([P, NE])),
                (w_rt[:, :, 0:NGRP], of("moe_w_group").rearrange("o (p k) n -> p (o k) n", k=KC)),
                (w_rt[:, :, NGRP:], of("moe_w_expert").rearrange("o (p k) n -> p (o k) n", k=KC)),
                (w_qup, of("mla_w_q_up").rearrange("o (p c) n -> p (o c) n", c=2)),
                (w_kvup, of("mla_w_kv_up").rearrange("o p n -> p (o n)")),
            ]
        ALL_PARAMS = 16 * len(params(0))

        abc = ([(SBQ + h * HD, SL_A + h, 1.0) for h in range(4)] + [(SBK + h * HD, SL_A + 4 + h, 1.0) for h in range(4)]
               + [(SWQ + h * HD, SL_B + h, g64q[:, 0:1]) for h in range(4)] + [(SWK + h * HD, SL_B + 4 + h, g64[:, 1:2]) for h in range(2)]
               + [(NQ + h * HD, SL_C + h, g64q[:, 1:2]) for h in range(4)] + [(NKS + h * HD, SL_C + 4 + h, g64[:, 4:5]) for h in range(2)]
               + [(NKW + h * HD, SL_C + 6 + h, g64[:, 5:6]) for h in range(2)])
        G_X = (0, 0)
        G_POS = (4, 4)
        G_LAT = (5, 4)
        G_KC = (7, 5)
        G_ABC = (7, 7)
        G_VC = (18, 18)
        G_D = (18, 20)
        G_O = (22, 24)
        G_H = (26, 28)
        G_END = (30, 32)

        units = [(kind, h, i, {"B": P * min(i + 1, 2), "cmp": NCMP}.get(kind, P * (i + 1)))
                 for kind in ("A", "B", "cmp", "slc", "win", "D") for h in range(4) for i in range(NT)]
        NU = len(units)
        NSB = 4 * NT

        def q_of(kind, h, i):
            c = slice(i * P, (i + 1) * P)
            if kind == "A":
                return heads[0:HD, SL_A + h, c]
            if kind == "B":
                return heads[0:HD, SL_B + h, c]
            if kind == "D":
                return heads[0:MQK, SL_D + h, c]
            return heads[0:HD, SL_C + h, c]

        def k_of(kind, h, i, n):
            if kind == "A":
                return heads[0:HD, SL_A + 4 + h, 0:n]
            if kind == "B":
                return heads[0:HD, SL_B + 4 + h // 2, (i + 1) * P - n:(i + 1) * P]
            if kind == "cmp":
                return kcmpT[:, h // 2, 0:NCMP]
            if kind == "slc":
                return heads[0:HD, SL_C + 4 + h // 2, 0:n]
            if kind == "win":
                return heads[0:HD, SL_C + 6 + h // 2, 0:n]
            return heads[0:MQK, SL_D + 4 + h, 0:n]

        def v_of(kind, h, t):
            if kind == "A":
                return proj[:, t, SBV + h * HD:SBV + (h + 1) * HD]
            if kind == "B":
                return proj[:, t, SWV + (h // 2) * HD:SWV + (h // 2 + 1) * HD]
            if kind == "slc":
                return proj[:, t, NVS + (h // 2) * HD:NVS + (h // 2 + 1) * HD]
            if kind == "win":
                return proj[:, t, NVW + (h // 2) * HD:NVW + (h // 2 + 1) * HD]
            return proj[:, t, h * HD:(h + 1) * HD]

        def bias_of(kind, h, i, n):
            if kind == "B":
                return gs[:, h, US - n:US]
            if kind == "D":
                return con[:, C_CM + T - n:C_CM + T]
            if kind == "A":
                return con[:, C_SM + T - n:C_SM + T]
            if kind == "cmp":
                u0 = P * (NT - 1 - i) + CMP_L - 1
                return gn[:, h, u0:u0 + CMP_S * (NCMP - 1) + 1:CMP_S]
            return gn[:, h, P * (NT - 1 - i):P * (NT - 1 - i) + n]

        def blocks_of(kind, i, n):
            if kind == "cmp":
                return [(0, NCMP, 0)]
            first = i + 1 - n // P
            return [(b * P, P, first + b) for b in range(n // P)]

        @block.sync
        def _(sp):
            sp.dma_start(con[:, :], consts).then_inc(setup_in, 16)
            sp.dma_start(relx[0:BUCKETS, :], a["rel_bias"]).then_inc(setup_in, 16)
            sp.dma_start(bmap[:, 0:TN + TS], bias_map).then_inc(setup_in, 16)
            sp.dma_start(x[:, :, :], a["x"].rearrange("b (t p) d -> p (b t) d", p=P)).then_inc(setup_in, 16)
            sp.wait_ge(bias_neg, 3)
            W = TN + TS
            for h in range(4):
                sp.dma_start(bias_rows[h:h + 1, :, 0:TN], sq[4 + h:5 + h, 0:TN].unsqueeze(1).broadcast_to([1, P, TN])).then_inc(bias_out, 16)
                sp.dma_start(bias_rows[h:h + 1, :, TN:], sq[h:h + 1, TN:TN + TS].unsqueeze(1).broadcast_to([1, P, TS])).then_inc(bias_out, 16)
            sp.wait_ge(bias_out, 128)
            for h in range(4):
                sp.dma_start(gn[:, h, :], bass.AP(bias_rows.tensor, h * P * W + P - 1, [[W - 1, P], [1, UN]])).then_inc(bias_in, 16)
                sp.dma_start(gs[:, h, :], bass.AP(bias_rows.tensor, h * P * W + TN + P - 1, [[W - 1, P], [1, US]])).then_inc(bias_in, 16)
            with sp.Fori(0, L) as l:
                def load(dst, src, s):
                    sp.dma_start(dst, src).then_inc(s_[s], 16)

                def load_win(c):
                    c0, n = CHUNKS[c]
                    load(win[c % 2][:, :, 0:n], a["w_in"][bass.ds(l, 1)].rearrange("o (p k) n -> p (o k) n", k=KC)[:, :, c0:c0 + n],
                         ("win_a", "win_b")[c % 2])
                enter(sp, l)
                load_win(0)
                load_win(1)
                for dst, src in params(l):
                    load(dst, src, "params")
                for c in range(2, len(CHUNKS)):
                    sp.wait_ge(s_["pj_mm"], NT * (c - 1))
                    load_win(c)
                load(w1[0], a["nsa_cmp_w1"][bass.ds(l, 1), 0].rearrange("o l d f -> d (o l) f"), "w1_in")
                sp.wait_ge(s_["up_mm"], NT)
                load(w1[1], a["nsa_cmp_w1"][bass.ds(l, 1), 1].rearrange("o l d f -> d (o l) f"), "w1v_in")
                sp.wait_ge(s_["pv"], NU)
                load(w_o, a["w_out"][bass.ds(l, 1)].rearrange("o (p k) n -> p (o k) n", k=KC), "wout_in")

                def gate_up_of(e):
                    return [a[n][bass.ds(l, 1), bass.ds(e, 1)].rearrange("a b (p k) f -> p (a b k) f", k=KC)
                            for n in ("moe_w_gate", "moe_w_up")]

                def down_of(e):
                    return a["moe_w_down"][bass.ds(l, 1), bass.ds(e, 1)].rearrange("a b (p c) n -> p (a b c) n", c=2)
                for s in range(2):
                    g, u = gate_up_of(s)
                    load(ring_g[s], g, f"wg{s}")
                    load(ring_u[s], u, f"wu{s}")
                    load(ring_d[s], down_of(s), f"wd{s}")
                sp.wait_ge(scat, 16 * 2 * NT * l + 16 * 2 * NT)
                sp.wait_ge(s_["lg_mm"], 1)
                for s in range(2):
                    load(xe[s], xs_dram[s * S:(s + 1) * S, :], f"xe{s}")
                with sp.Fori(0, NE // 2 - 1) as i:
                    for s in range(2):
                        g, u = gate_up_of(2 * i + 2 + s)
                        sp.wait_ge(s_["xeT_mm"], 2 * i + s + 1)
                        load(xe[s], xs_dram[bass.ds((2 * i + 2 + s) * S, S), :], f"xe{s}")
                        sp.wait_ge(s_["gu_mm"], 2 * i + s + 1)
                        load(ring_g[s], g, f"wg{s}")
                        load(ring_u[s], u, f"wu{s}")
                        sp.wait_ge(s_["dn_mm"], 2 * i + s + 1)
                        load(ring_d[s], down_of(2 * i + 2 + s), f"wd{s}")
                sp.wait_ge(s_["xeT_mm"], NE - 1)
                load(xe[0], xs_dram[NE * S:(NE + 1) * S, :], "xe0")
                sp.wait_ge(s_["dn_mm"], NE)
                sp.wait_ge(s_["xeT_mm"], NE + 1)
                n_over = sp.value_load(overi[0:1, 15:16], min_val=0, max_val=NOVER)
                with sp.If(n_over > 0):
                    with sp.Fori(0, n_over) as k:
                        e = sp.value_load(overi[0:1, bass.ds(k, 1)], min_val=0, max_val=NE - 1)
                        g, u = gate_up_of(e)
                        load(ring_g[0], g, "f_in")
                        load(ring_u[0], u, "f_in")
                        load(ring_d[0], down_of(e), "f_in")
                        load(xe[0], xs_dram[bass.ds(k * S + NE * S, S), :], "f_in")
                        sp.wait_ge(s_["f_end"], k + 1)
                        sp.sem_inc(s_["f_loop"], 1)
                after(sp.drain(), "sp_done")
            sp.wait_ge(layer_open, L + 1)
            sp.dma_start(out.rearrange("b (t p) d -> p (b t) d", p=P), x[:, :, :]).then_inc(out_done, 16)
            sp.wait_ge(out_done, 16)

        @block.tensor
        def _(pe):
            mm = nc.tensor.matmul

            def transposes(srcs, rows, n, on, kp=P):
                tr, ev, bank = (("tr_act", "ev_act", 4), ("tr_dve", "ev_dve", 5))[on]
                if n:
                    pe.wait_ge(s_[ev], n)
                for i, src in enumerate(srcs):
                    ins = nc.tensor.transpose(ps[0:rows, bank, i * kp:(i + 1) * kp], src, con[0:kp, C_ID:C_ID + kp])
                after(ins, tr)

            pe.wait_ge(setup_in, 64)
            pe.wait_ge(setup_dve, 1)
            for c in range(3):
                n = min(512, TN + TS - c * 512)
                mm(ps[0:8, c, 0:n], relx[:, :], bmap[:, c * 512:c * 512 + n], start=True, stop=True).then_inc(bias_mm, 1)
            pe.wait_ge(bias_neg, 3)
            with pe.Fori(0, L) as l:
                enter(pe, l)
                pe.wait_ge(s_["xn_rdy"], NT)
                for k in range(KC):
                    transposes([xoc[:, t, k::KC] for t in range(NT)], P, G_X[k % 2] + k // 2, k % 2)
                pe.wait_ge(s_["params"], ALL_PARAMS)
                transposes([cpos[:, :]], HD, G_POS[0], 0, kp=HD)
                pe.wait_ge(s_["ev_act"], G_POS[0])
                pe.wait_ge(s_["ev_dve"], G_POS[1])
                for c, (c0, n) in enumerate(CHUNKS):
                    pe.wait_ge(s_[("win_a", "win_b")[c % 2]], 16 * (c // 2 + 1))
                    for t in range(NT):
                        if c:
                            pe.wait_ge(s_[("pj_ev_act", "pj_ev_dve")[t % 2]], 2 * (c - 1) + t // 2 + 1)
                        for k in range(KC):
                            ins = mm(ps[:, t, 0:n], hTc[:, k, t * P:(t + 1) * P], win[c % 2][:, k, 0:n], start=k == 0, stop=k == KC - 1)
                        after(ins, "pj_mm")
                pe.wait_ge(s_["norms_rdy"], 1)
                for c in range(2):
                    transposes([proj[:, t, MCQ + c:MCQ + QR:2] for t in range(NT)], MQK, G_LAT[c], c)
                transposes([proj[:, t, MCKV:MCKV + KVR] for t in range(NT)], KVR, G_LAT[0] + 1, 0)
                for h in range(2):
                    transposes([proj[:, t, NKC + h * HD:NKC + (h + 1) * HD] for t in range(NT)], HD, G_KC[1] + h, 1)
                for j, (col, _, _) in enumerate(abc):
                    transposes([proj[:, t, col:col + HD] for t in range(NT)], HD, G_ABC[j % 2] + j // 2, j % 2)
                for t in range(NT):
                    if t >= 2:
                        pe.wait_ge(s_["up_ev_act"], t - 1)
                        pe.wait_ge(s_["up_ev_dve"], t - 1)
                    for c in range(2):
                        mm(ps[:, 2 * (t % 2), 0:384], heads[0:MQK, SL_D + c, t * P:(t + 1) * P], w_qup[:, c, :], start=c == 0, stop=c == 1)
                    after(mm(ps[:, 2 * (t % 2) + 1, :], heads[:, SL_D + 2, t * P:(t + 1) * P], w_kvup, start=True, stop=True), "up_mm")
                for c in range(2):
                    if c == 1:
                        for h in range(2):
                            transposes([proj[:, t, NVC + h * HD:NVC + (h + 1) * HD] for t in range(NT)], HD, G_VC[1] + h, 1)
                    pe.wait_ge(s_["ev_dve"], (G_VC, G_D)[c][1])
                    pe.wait_ge(s_[("w1_in", "w1v_in")[c]], 16)
                    for j in range(CMP_L):
                        slot = SL_X + 2 * (j // CMP_S)
                        src = heads[0:HD, slot:slot + 2, j:j + CMP_S * (NCMP - 1) + 1:CMP_S]
                        ins = mm(ps[:, 6 + c, 0:2 * NCMP], w1[c][:, j, :], src, start=j == 0, stop=j == CMP_L - 1)
                    after(ins, "cmp_mm")
                pe.wait_ge(s_["cmp_ev"], 2)
                pe.wait_ge(s_["up_ev_act"], NT)
                pe.wait_ge(s_["up_ev_dve"], NT)
                for c in range(2):
                    for h in range(2):
                        ins = mm(ps[0:NCMP, c, h * HD:(h + 1) * HD], hcmp[:, c, h, 0:NCMP], w_cmp2[:, c, :], start=True, stop=True)
                after(ins, "cmp_out")
                pe.wait_ge(s_["dqk_rdy"], 1)
                for h in range(8):
                    transposes([dqk[:, t, h, :] for t in range(NT)], MQK, G_D[h % 2] + h // 2, h % 2)
                pe.wait_ge(s_["cmp_n"], 1)
                for h in range(2):
                    ins = nc.tensor.transpose(ps[0:HD, 2, h * 32:h * 32 + NCMP], kcmp[:, h, :], con[0:NCMP, C_ID:C_ID + NCMP])
                after(ins, "cmpT_mm")
                pe.wait_ge(s_["ev_act"], G_O[0])
                pe.wait_ge(s_["ev_dve"], G_O[1])
                pe.wait_ge(s_["cmpT_ev"], 1)

                def scores(u):
                    kind, h, i, n = units[u]
                    if u >= 3:
                        pe.wait_ge(s_["logits"], u - 2)
                    after(mm(ps[:, u % 3, 0:n], q_of(kind, h, i), k_of(kind, h, i, n), start=True, stop=True), "scores")

                def turn(u):
                    kind, h, i, n = units[u]
                    if kind == "A":
                        pe.wait_ge(s_["probs_sb"], u + 1)
                    else:
                        pe.wait_ge(s_["probs_sm"], u + 1 - NSB)
                    if u >= 2:
                        pe.wait_ge(s_["probT_ev"], u - 1)
                    for c0, w, _ in blocks_of(kind, i, n):
                        ins = nc.tensor.transpose(ps[0:w, 3 + u % 2, c0:c0 + P], prb[u % 2][:, c0:c0 + w], ident)
                    after(ins, "probT")

                def values(u):
                    kind, h, i, n = units[u]
                    g = u // NT
                    if i == 0 and g >= 2:
                        pe.wait_ge(s_["head_out"], g - 1)
                    pe.wait_ge(s_["probT_ev"], u + 1)
                    bl = blocks_of(kind, i, n)
                    for j, (c0, w, kt) in enumerate(bl):
                        v = vcmp[:, h // 2, :] if kind == "cmp" else v_of(kind, h, kt)
                        ins = mm(ps[:, 5 + g % 2, i * HD:(i + 1) * HD], prT[u % 2][0:w, c0:c0 + P], v, start=j == 0, stop=j == len(bl) - 1)
                    after(ins, "pv")
                for u in range(-2, NU + 1):
                    if u + 2 < NU:
                        scores(u + 2)
                    if 0 <= u < NU:
                        turn(u)
                    if u >= 1:
                        values(u - 1)
                pe.wait_ge(s_["o_rdy"], 1)
                for k in range(KC):
                    transposes([xoc[:, t, k::KC] for t in range(NT)], P, G_O[k % 2] + k // 2, k % 2)
                pe.wait_ge(s_["ev_act"], G_H[0])
                pe.wait_ge(s_["ev_dve"], G_H[1])
                pe.wait_ge(s_["wout_in"], 16)
                for j in range(2 * NT):
                    if j >= 4:
                        pe.wait_ge(s_["wo_ev"], j - 3)
                    for k in range(KC):
                        ins = mm(ps[:, j % 4, :], hTc[:, k, j // 2 * P:(j // 2 + 1) * P], w_o[:, k, j % 2 * 512:(j % 2 + 1) * 512], start=k == 0, stop=k == KC - 1)
                    after(ins, "wo_mm")
                pe.wait_ge(s_["xn_rdy"], 2 * NT)
                for k in range(KC):
                    transposes([xoc[:, t, k::KC] for t in range(NT)], P, G_H[k % 2] + k // 2, k % 2)
                pe.wait_ge(s_["ev_act"], G_END[0])
                pe.wait_ge(s_["ev_dve"], G_END[1])
                for t in range(NT):
                    for k in range(KC):
                        ins = mm(ps[:, 0, t * 36:(t + 1) * 36], hTc[:, k, t * P:(t + 1) * P], w_rt[:, k, :], start=k == 0, stop=k == KC - 1)
                after(ins, "lg_mm")
                pe.wait_ge(s_["assign"], 1)
                for t in range(NT):
                    mm(ps[:, 1, t * NE:(t + 1) * NE], con[:, C_TRI:C_TRI + P], rt[:, 9, t, :], start=True, stop=t == 0)
                    for b in range(t):
                        mm(ps[:, 1, t * NE:(t + 1) * NE], ones[:, :], rt[:, 9, b, :], start=False, stop=b == t - 1)
                for t in range(NT):
                    ins = mm(ps[:, 2, 0:NE], ones[:, :], rt[:, 9, t, :], start=t == 0, stop=t == NT - 1)
                after(ins, "pos_mm")

                def turn_x(s):
                    for k in range(KC):
                        ins = nc.tensor.transpose(ps[:, 4 + s, k * S:(k + 1) * S], xe[s][:, k::KC], con[0:S, C_ID:C_ID + S])
                    return ins

                def gate_up(s):
                    for m in range(4):
                        w = (ring_g, ring_u)[m // 2][s]
                        for k in range(KC):
                            ins = mm(ps[:, 2 + s, m * S:(m + 1) * S], w[:, k, m % 2::2], xeT[s][:, k, :], start=k == 0, stop=k == KC - 1)
                    return ins

                def down(s):
                    for hf in range(2):
                        for c in range(2):
                            ins = mm(ps[0:S, (0, 6)[s] + hf, :], aT[:, s, c, :], ring_d[s][:, c, hf * 512:(hf + 1) * 512], start=c == 0, stop=c == 1)
                    return ins

                def expert(e, q, s, first):
                    pe.wait_ge(s_[f"wg{s}"], 16 * q + 16)
                    pe.wait_ge(s_[f"wu{s}"], 16 * q + 16)
                    pe.wait_ge(s_["xeT_ev"], e + 1)
                    pe.wait_ge(s_[f"xe{1 - s}"], 16 * q + 16 + 16 * s)
                    after(gate_up(s), "gu_mm")
                    after(turn_x(1 - s), "xeT_mm")
                    if not first:
                        pe.wait_ge(s_["y_act"], e - 1)
                        pe.wait_ge(s_["y_dve"], e - 1)
                    pe.wait_ge(s_[f"wd{s}"], 16 * q + 16)
                    pe.wait_ge(s_["a_rdy"], e + 1)
                    after(down(s), "dn_mm")
                pe.wait_ge(s_["xe0"], 16)
                after(turn_x(0), "xeT_mm")
                pe.wait_ge(s_["slots_rdy"], 1)
                for s in range(2):
                    expert(s, 0, s, True)
                with pe.Fori(1, NE // 2) as i:
                    for s in range(2):
                        expert(2 * i + s, i, s, False)
                n_over = pe.value_load(overi[0:1, 15:16], min_val=0, max_val=NOVER)
                pe.wait_ge(s_["xeT_ev"], NE + 1)
                pe.wait_ge(s_["y_act"], NE)
                pe.wait_ge(s_["y_dve"], NE)
                with pe.If(n_over > 0):
                    with pe.Fori(0, n_over) as k:
                        pe.wait_ge(s_["f_in"], 64 * k + 64)
                        pe.sem_inc(s_["f_step"], 1)
                        after(turn_x(0), "f_T")
                        pe.wait_ge(s_["f_Tev"], k + 1)
                        after(gate_up(0), "f_gu")
                        pe.wait_ge(s_["f_a"], k + 1)
                        after(down(0), "f_dn")
                        pe.wait_ge(s_["f_end"], k + 1)
                after(pe.drain(), "pe_done")

        @block.scalar
        def _(act):
            def A(out_, in_, f, **kw):
                return nc.scalar.activation(out_, in_, f, **kw)

            def copy_out(n, dst, src, scale=1.0):
                act.wait_ge(s_["tr_act"], n + 1)
                after(A(dst, src, ACT.Identity, scale=scale), "ev_act")

            def sums_x(rounds):
                for t in range(NT):
                    ins = A(hT[:, t * D:(t + 1) * D], x[:, t, :], ACT.Square, accum_out=ss[:, t:t + 1])
                after(ins, "sum_rdy")
            act.wait_ge(setup_in, 64)
            with act.Fori(0, L) as l:
                enter(act, l)
                sums_x(1)
                act.wait_ge(s_["params"], ALL_PARAMS)
                for k in range(0, KC, 2):
                    copy_out(G_X[0] + k // 2, hTc[:, k, :], ps[:, 4, :], g_attn[:, k:k + 1])
                copy_out(G_POS[0], cposT[:, :], ps[0:HD, 4, 0:HD])
                for c, (c0, n) in enumerate(CHUNKS):
                    for t in (0, 2):
                        act.wait_ge(s_["pj_mm"], NT * c + t + 1)
                        after(A(proj[:, t, c0:c0 + n], ps[:, t, 0:n], ACT.Identity), "pj_ev_act")
                act.wait_ge(s_["pj_ev_dve"], 2 * len(CHUNKS))
                act.wait_ge(s_["pj_ev_act"], 2 * len(CHUNKS))
                for dst, c0, n in ((0, SWQ, 384), (384, NQ, 256), (640, NKS, 128), (768, NKW, 128)):
                    A(sqh[:, :, dst:dst + n], proj[:, :, c0:c0 + n], ACT.Square)
                for t in range(NT):
                    A(hT[:, t * 192:t * 192 + QR], proj[:, t, MCQ:MCQ + QR], ACT.Square, accum_out=ss[:, 56 + t:57 + t])
                    ins = A(hT[:, 1024 + t * 128:1024 + t * 128 + KVR], proj[:, t, MCKV:MCKV + KVR], ACT.Square, accum_out=ss[:, 60 + t:61 + t])
                after(ins, "sum_rdy")
                copy_out(G_LAT[0], heads[0:MQK, SL_D, :], ps[0:MQK, 4, :], g_lq[:, 0:1])
                copy_out(G_LAT[0] + 1, heads[:, SL_D + 2, :], ps[:, 4, :], g_lkv[:, 0:1])
                for j, (_, slot, scale) in enumerate(abc):
                    if j % 2 == 0:
                        copy_out(G_ABC[0] + j // 2, heads[0:HD, slot, :], ps[0:HD, 4, :], scale)
                for t in range(NT):
                    act.wait_ge(s_["up_mm"], t + 1)
                    after(A(dqk[:, t, 0:4, :], ps[:, 2 * (t % 2), 0:384].rearrange("p (h c) -> p h c", h=4), ACT.Identity), "up_ev_act")
                act.wait_ge(s_["up_ev_act"], NT)
                act.wait_ge(s_["up_ev_dve"], NT + 1)
                after(A(dsq, dqk, ACT.Square), "sum_rdy")
                for c in range(2):
                    act.wait_ge(s_["cmp_mm"], c + 1)
                    after(A(hcmp[:, c, :, 0:NCMP], ps[:, 6 + c, 0:2 * NCMP].rearrange("p (h n) -> p h n", h=2), ACT.Gelu_apprx_tanh), "cmp_ev")
                for h in (0, 2, 4, 6):
                    copy_out(G_D[0] + h // 2, heads[0:MQK, SL_D + h, :], ps[0:MQK, 4, :], -(MQK ** -0.5) if h < 4 else 1.0)
                A(gates[:, :, :], proj[:, :, NG:NG + 12], ACT.Sigmoid)

                def probs(u):
                    kind, h, i, n = units[u]
                    act.wait_ge(s_["logits"], u + 1)
                    if u >= 2:
                        act.wait_ge(s_["probT"], u - 1)
                    if kind == "A":
                        if u >= 2:
                            act.wait_ge(s_["probs_sb"], u - 1)
                        A(prb[u % 2][:, 0:n], lgt[u % 3][:, 0:n], ACT.Sigmoid, scale=HD ** -0.5)
                        after(A(keep[u % 2][:, 0:n], lgt[u % 3][:, 0:n], ACT.Sigmoid, scale=-(HD ** -0.5)), "sig")
                        return
                    after(A(prb[u % 2][:, 0:n], lgt[u % 3][:, 0:n], ACT.Exp, bias=mrow[:, u:u + 1], scale=-1.0, accum_out=den[:, u:u + 1]), "probs_sm")
                    if kind == "B" and i == NT - 1:
                        after(A(esink[:, h * NT:(h + 1) * NT], mrow[:, u - 3:u + 1], ACT.Exp, bias=sink[:, h:h + 1]), "esink_rdy")

                def copy_probs(u):
                    kind, h, i, n = units[u]
                    w, m = (NCMP, P) if kind == "cmp" else (P, n)
                    act.wait_ge(s_["probT"], u + 1)
                    if u >= 2:
                        act.wait_ge(s_["pv"], u - 1)
                    after(A(prT[u % 2][0:w, 0:m], ps[0:w, 3 + u % 2, 0:m], ACT.Identity), "probT_ev")
                for u in range(-1, NU):
                    if u + 1 < NU:
                        probs(u + 1)
                    if u >= 0:
                        copy_probs(u)
                act.wait_ge(s_["head_out"], NU // NT)
                for t in range(NT):
                    for g in range(4):
                        c = t * D + g * 256
                        ins = A(hT[:, c:c + 256], xo[:, c:c + 256], ACT.Square, accum_out=ss[:, 4 * t + g:4 * t + g + 1])
                after(ins, "sum_rdy")
                for k in range(0, KC, 2):
                    copy_out(G_O[0] + k // 2, hTc[:, k, :], ps[:, 4, :], g_out[:, k:k + 1])
                act.wait_ge(s_["wo_ev"], 2 * NT)
                sums_x(2)
                for k in range(0, KC, 2):
                    copy_out(G_H[0] + k // 2, hTc[:, k, :], ps[:, 4, :], g_ffn[:, k:k + 1])
                act.wait_ge(s_["rt_in"], 1)
                after(A(gex[:, :, :], gex[:, :, :], ACT.Exp), "rt_exp")
                act.wait_ge(s_["rt_in"], 2)
                after(A(rsm[:, 6, :], rsm[:, 6, :], ACT.Exp), "rt_exp")

                def expert(e, q, s, first):
                    act.wait_ge(s_["gu_mm"], e + 1)
                    after(A(sg[:, s, :], ps[:, 2 + s, 0:2 * S], ACT.Silu), "silu_rdy")
                    if not first:
                        act.wait_ge(s_[f"yst{s}"], 16 * q)
                    act.wait_ge(s_["dn_mm"], e + 1)
                    after(A(ye[s][:, 0:512], ps[0:S, (0, 6)[s], :], ACT.Identity), "y_act")
                    act.wait_ge(s_["y_act"], e + 1)
                    act.wait_ge(s_["y_dve"], e + 1)
                    after(act.dma_start(ys_dram[bass.ds(e * S, S), :], ye[s]), f"yst{s}", 16)
                for s in range(2):
                    expert(s, 0, s, True)
                with act.Fori(1, NE // 2) as i:
                    for s in range(2):
                        expert(2 * i + s, i, s, False)
                n_over = act.value_load(overi[0:1, 15:16], min_val=0, max_val=NOVER)
                act.wait_ge(s_["yst0"], 16 * NE // 2)
                with act.If(n_over > 0):
                    with act.Fori(0, n_over) as k:
                        act.wait_ge(s_["f_gu"], k + 1)
                        after(A(sg[:, 0, :], ps[:, 2, 0:2 * S], ACT.Silu), "f_silu")
                        act.wait_ge(s_["f_dn"], k + 1)
                        after(A(ye[0][:, 0:512], ps[0:S, 0, :], ACT.Identity), "f_yact")
                        act.wait_ge(s_["f_yact"], k + 1)
                        act.wait_ge(s_["f_ydve"], k + 1)
                        after(act.dma_start(ys_dram[bass.ds(k * S + NE * S, S), :], ye[0]), "f_st", 16)
                        act.wait_ge(s_["f_st"], 16 * k + 16)
                        act.sem_inc(s_["f_end"], 1)
                after(act.drain(), "act_done")

        @block.vector
        def _(dve):
            V = nc.vector
            steps = [0]

            def link(ins):
                steps[0] += 1
                after(ins, "dve_step")
                dve.wait_ge(s_["dve_step"], steps[0])

            def copy_out(n, dst, src, scale=1.0):
                dve.wait_ge(s_["tr_dve"], n + 1)
                after(V.tensor_scalar(dst, src, scale, None, ALU.mult), "ev_dve")

            def mean(dst, src, width):
                return V.tensor_scalar(dst, src, 1.0 / width, EPS, ALU.mult, ALU.add)

            def norm_x(rounds, n):
                dve.wait_ge(s_["sum_rdy"], rounds)
                after(mean(ss[:, 0:NT], ss[:, 0:NT], D), "ms_rdy")
                dve.wait_ge(s_["rs_rdy"], rounds)
                for t in range(NT):
                    after(V.tensor_scalar(xoc[:, t, :], x[:, t, :], rs[:, t:t + 1], None, ALU.mult), "xn_rdy")

            def bc(ap, shape):
                return ap.broadcast_to(shape)

            V.memset(relx[BUCKETS:BUCKETS + 1, :], 1.0)
            V.memset(ones[:, :], 1.0)
            V.memset(neghalf[:, :], -0.5).then_inc(setup_dve, 1)
            for c in range(3):
                n = min(512, TN + TS - c * 512)
                dve.wait_ge(bias_mm, c + 1)
                V.tensor_scalar(sq[0:8, c * 512:c * 512 + n], ps[0:8, c, 0:n], -1.0, None, ALU.mult).then_inc(bias_neg, 1)
            dve.wait_ge(setup_in, 64)
            dve.wait_ge(bias_in, 128)
            with dve.Fori(0, L) as l:
                steps[0] = 0
                enter(dve, l)
                norm_x(1, 0)
                dve.wait_ge(s_["params"], ALL_PARAMS)
                link(V.tensor_scalar(g64q[:, 0:1], g64[:, 0:1], -(HD ** -0.5), None, ALU.mult))
                link(V.tensor_scalar(g64q[:, 1:2], g64[:, 2:3], -(HD ** -0.5), None, ALU.mult))
                link(V.tensor_scalar(nsink[:, :], sink[:, :], -1.0, None, ALU.mult))
                for k in range(1, KC, 2):
                    copy_out(G_X[1] + k // 2, hTc[:, k, :], ps[:, 5, :], g_attn[:, k:k + 1])
                for c, (c0, n) in enumerate(CHUNKS):
                    for t in (1, 3):
                        dve.wait_ge(s_["pj_mm"], NT * c + t + 1)
                        after(V.tensor_copy(proj[:, t, c0:c0 + n], ps[:, t, 0:n]), "pj_ev_dve")
                dve.wait_ge(s_["sum_rdy"], 2)
                link(V.tensor_reduce(ss[:, 0:56].rearrange("p (t h) -> p t h", t=NT), sqh.rearrange("p t (h c) -> p t h c", c=HD), AX.X, ALU.add))
                mean(ss[:, 0:56], ss[:, 0:56], HD)
                mean(ss[:, 56:60], ss[:, 56:60], QR)
                after(mean(ss[:, 60:64], ss[:, 60:64], KVR), "ms_rdy")
                dve.wait_ge(s_["rs_rdy"], 2)
                dve.wait_ge(s_["pj_ev_dve"], 2 * len(CHUNKS))
                for c0, n, r in ((MCQ, QR, 56), (MCKV, KVR, 60)):
                    v = proj[:, :, c0:c0 + n]
                    V.tensor_tensor(v, v, bc(rs[:, r:r + NT].unsqueeze(2), [P, NT, n]), ALU.mult)
                rsh = rs[:, 0:56].rearrange("p (t h) -> p t h", t=NT)
                for c0, nh, h0 in ((SWQ, 6, 0), (NQ, 4, 6), (NKS, 2, 10), (NKW, 2, 12)):
                    v = proj[:, :, c0:c0 + nh * HD].rearrange("p t (h c) -> p t h c", c=HD)
                    ins = V.tensor_tensor(v, v, bc(rsh[:, :, h0:h0 + nh].unsqueeze(3), [P, NT, nh, HD]), ALU.mult)
                after(ins, "norms_rdy")

                def positions(n, h):
                    dve.wait_ge(s_["tr_dve"], n + 1)
                    src = ps[0:HD, 5, :].rearrange("p (b r) -> p b r", r=CMP_S)
                    c0 = 0 if n < G_VC[1] else CMP_L
                    for half in range(2):
                        dst = heads[0:HD, SL_X + 2 * half + h, :].rearrange("p (b r) -> p b r", r=CMP_S)
                        pos = cposT[:, c0 + half * CMP_S:c0 + (half + 1) * CMP_S].unsqueeze(1)
                        ins = V.tensor_tensor(dst, src, bc(pos, [HD, T // CMP_S, CMP_S]), ALU.add)
                    after(ins, "ev_dve")
                copy_out(G_LAT[1], heads[0:MQK, SL_D + 1, :], ps[0:MQK, 5, :], g_lq[:, 1:2])
                dve.wait_ge(s_["ev_act"], G_LAT[0])
                for h in range(2):
                    positions(G_KC[1] + h, h)
                for j, (_, slot, scale) in enumerate(abc):
                    if j % 2:
                        copy_out(G_ABC[1] + j // 2, heads[0:HD, slot, :], ps[0:HD, 5, :], scale)
                link(V.tensor_copy(dqk[:, :, 4:8, NOPE:], bc(proj[:, :, MKPE:MKPE + ROPE].unsqueeze(2), [P, NT, 4, ROPE])))
                for t in range(NT):
                    dve.wait_ge(s_["up_mm"], t + 1)
                    kv = ps[:, 2 * (t % 2) + 1, :].rearrange("p (h c) -> p h c", h=4)
                    V.tensor_copy(proj[:, t, 0:256].rearrange("p (h c) -> p h c", h=4), kv[:, :, NOPE:])
                    after(V.tensor_copy(dqk[:, t, 4:8, 0:NOPE], kv[:, :, 0:NOPE]), "up_ev_dve")
                after(V.memset(den2[:, :], 1.0), "up_ev_dve")
                dve.wait_ge(s_["cmp_mm"], 1)
                for h in range(2):
                    positions(G_VC[1] + h, h)
                dve.wait_ge(s_["sum_rdy"], 3)
                link(V.tensor_reduce(ss[:, 0:32].rearrange("p (t h) -> p t h", t=NT), dsq, AX.X, ALU.add))
                after(mean(ss[:, 0:32], ss[:, 0:32], MQK), "ms_rdy")
                dve.wait_ge(s_["rs_rdy"], 3)
                link(V.tensor_tensor(dqk, dqk, bc(rs[:, 0:32].rearrange("p (t h) -> p t h", t=NT).unsqueeze(3), [P, NT, 8, MQK]), ALU.mult))
                for j in range(2):
                    ins = V.tensor_tensor(dqk[:, :, 4 * j:4 * j + 4, :], dqk[:, :, 4 * j:4 * j + 4, :],
                                          bc(g_qk[:, j, :].unsqueeze(1).unsqueeze(1), [P, NT, 4, MQK]), ALU.mult)
                link(ins)
                x1, x2 = dqk[:, :, :, NOPE:NOPE + HALF], dqk[:, :, :, NOPE + HALF:]
                cos, sin = [bc(con[:, c:c + 64].rearrange("p (t f) -> p t f", t=NT).unsqueeze(2), [P, NT, 8, HALF]) for c in (C_COS, C_SIN)]
                V.tensor_tensor(dtm[0], x1, cos, ALU.mult)
                V.tensor_tensor(dtm[1], x2, sin, ALU.mult)
                V.tensor_tensor(dtm[2], x1, sin, ALU.mult)
                link(V.tensor_tensor(dtm[3], x2, cos, ALU.mult))
                V.tensor_tensor(x1, dtm[0], dtm[1], ALU.subtract)
                after(V.tensor_tensor(x2, dtm[2], dtm[3], ALU.add), "dqk_rdy")
                dve.wait_ge(s_["cmp_out"], 1)
                V.tensor_copy(vcmp[:, :, :], ps[0:NCMP, 1, 0:2 * HD].rearrange("p (h c) -> p h c", h=2))
                link(V.tensor_copy(kcmp[:, :, :], ps[0:NCMP, 0, 0:2 * HD].rearrange("p (h c) -> p h c", h=2)))
                link(V.tensor_tensor(csq[:, :, :], kcmp[:, :, :], kcmp[:, :, :], ALU.mult))
                link(V.tensor_reduce(css[:, 0:2], csq[:, :, :], AX.X, ALU.add))
                after(mean(css[:, 0:2], css[:, 0:2], HD), "ms_rdy")
                dve.wait_ge(s_["rs_rdy"], 4)
                after(V.tensor_tensor(kcmp[:, :, :], kcmp[:, :, :], bc(css[:, 2:4].unsqueeze(2), [NCMP, 2, HD]), ALU.mult), "cmp_n")
                for h in (1, 3, 5, 7):
                    copy_out(G_D[1] + h // 2, heads[0:MQK, SL_D + h, :], ps[0:MQK, 5, :], -(MQK ** -0.5) if h < 4 else 1.0)
                dve.wait_ge(s_["cmpT_mm"], 1)
                after(V.tensor_scalar(kcmpT[:, :, 0:NCMP], ps[0:HD, 2, 0:64].rearrange("p (h n) -> p h n", h=2)[:, :, 0:NCMP], g64[:, 3:4], None, ALU.mult), "cmpT_ev")
                for s in range(2):
                    link(V.memset(left[s][:, T:T + 1], 1.0))

                def logits(u):
                    kind, h, i, n = units[u]
                    dve.wait_ge(s_["scores"], u + 1)
                    if u >= 3:
                        if units[u - 3][0] == "A":
                            dve.wait_ge(s_["sig"], u - 2)
                        else:
                            dve.wait_ge(s_["probs_sm"], u - 2 - NSB)
                    if kind == "A":
                        after(V.tensor_tensor(lgt[u % 3][:, 0:n], ps[:, u % 3, 0:n], bias_of(kind, h, i, n), ALU.add), "logits")
                        return
                    start = nsink[:, h:h + 1] if kind == "B" else 1e20
                    after(V.tensor_tensor_reduce(out=lgt[u % 3][:, 0:n], in0=ps[:, u % 3, 0:n], in1=bias_of(kind, h, i, n), scale=1.0,
                                                 scalar=start, op0=ALU.add, op1=ALU.min, accum_out=mrow[:, u:u + 1]), "logits")

                def stick(u):
                    kind, h, i, n = units[u]
                    dve.wait_ge(s_["sig"], u + 1)
                    link(V.tensor_tensor_scan(left[u % 2][:, T - n:T][:, ::-1], keep[u % 2][:, 0:n][:, ::-1], keep[u % 2][:, 0:n][:, ::-1], 1.0, ALU.mult, ALU.bypass))
                    after(V.tensor_tensor(prb[u % 2][:, 0:n], prb[u % 2][:, 0:n], left[u % 2][:, T - n + 1:T + 1], ALU.mult), "probs_sb")

                def head_out(g):
                    kind, h = units[g * NT][:2]
                    dve.wait_ge(s_["pv"], NT * g + NT)
                    grp = {"A": 0, "B": 1, "D": 3}.get(kind, 2)
                    src = ps[:, 5 + g % 2, 0:NT * HD].rearrange("p (t c) -> p t c", t=NT)
                    dst = xoc[:, :, grp * 256 + h * HD:grp * 256 + (h + 1) * HD]
                    if kind == "A":
                        after(V.tensor_copy(dst, src), "head_out")
                        return
                    d4 = den[:, NT * g:NT * g + NT]
                    if kind == "B":
                        dve.wait_ge(s_["esink_rdy"], h + 1)
                        link(V.tensor_tensor(d4, d4, esink[:, h * NT:(h + 1) * NT], ALU.add))
                    link(V.tensor_scalar(d4, d4, 1e-30, None, ALU.max))
                    link(V.reciprocal(den2[:, :], d4))
                    if grp == 2:
                        b = ("cmp", "slc", "win").index(kind)
                        link(V.tensor_tensor(den2[:, :], den2[:, :], gates[:, :, 4 * b + h], ALU.mult))
                    f = bc(den2[:, :].unsqueeze(2), [P, NT, HD])
                    if kind in ("slc", "win"):
                        link(V.tensor_tensor(otmp[:, :, :], src, f, ALU.mult))
                        after(V.tensor_tensor(dst, dst, otmp[:, :, :], ALU.add), "head_out")
                        dve.wait_ge(s_["head_out"], g + 1)
                    else:
                        after(V.tensor_tensor(dst, src, f, ALU.mult), "head_out")
                        dve.wait_ge(s_["head_out"], g + 1)
                for u in range(-2, NU + 1):
                    if u + 2 < NU:
                        logits(u + 2)
                    if 0 <= u + 1 < NSB:
                        stick(u + 1)
                    if u >= 1 and u % NT == 0:
                        head_out(u // NT - 1)
                dve.wait_ge(s_["sum_rdy"], 4)
                after(mean(ss[:, 0:16], ss[:, 0:16], 256), "ms_rdy")
                dve.wait_ge(s_["rs_rdy"], 5)
                og = xo[:, :].rearrange("p (g c) -> p g c", c=256)
                after(V.tensor_tensor(og, og, bc(rs[:, 0:16].unsqueeze(2), [P, 16, 256]), ALU.mult), "o_rdy")
                for k in range(1, KC, 2):
                    copy_out(G_O[1] + k // 2, hTc[:, k, :], ps[:, 5, :], g_out[:, k:k + 1])
                for j in range(2 * NT):
                    dve.wait_ge(s_["wo_mm"], j + 1)
                    xs = x[:, j // 2, j % 2 * 512:(j % 2 + 1) * 512]
                    after(V.tensor_tensor(xs, xs, ps[:, j % 4, :], ALU.add), "wo_ev")
                dve.wait_ge(s_["sum_rdy"], 5)
                after(mean(ss[:, 0:NT], ss[:, 0:NT], D), "ms_rdy")
                dve.wait_ge(s_["rs_rdy"], 6)
                for t in range(NT):
                    after(V.tensor_scalar(xoc[:, t, :], x[:, t, :], rs[:, t:t + 1], None, ALU.mult), "xn_rdy")
                for k in range(1, KC, 2):
                    copy_out(G_H[1] + k // 2, hTc[:, k, :], ps[:, 5, :], g_ffn[:, k:k + 1])
                TE = [P, NT, NE]
                dve.wait_ge(s_["lg_mm"], 1)
                link(V.tensor_tensor(lg[:, :, :], ps[:, 0, 0:NT * 36].rearrange("p (t n) -> p t n", t=NT), bc(rbias[:, :].unsqueeze(1), [P, NT, 36]), ALU.add))
                gl, el = lg[:, :, 0:NGRP], lg[:, :, NGRP:]

                def r(i):
                    return rsm[:, i, :]

                def b3(ap, n):
                    return bc(ap.unsqueeze(2), [P, NT, n])

                def c3(c, n):
                    return bc(con[:, c:c + n].unsqueeze(1), [P, NT, n])

                def first_best(dst, src, best, at, n):
                    link(V.tensor_reduce(best, src, AX.X, ALU.max))
                    link(V.tensor_tensor(dst, src, b3(best, n), ALU.is_equal))
                    link(V.scalar_tensor_tensor(dst, dst, -1000.0, c3(C_E, n), ALU.mult, ALU.add))
                    link(V.tensor_reduce(at, dst, AX.X, ALU.min))
                    link(V.tensor_tensor(dst, c3(C_IM, n), b3(at, n), ALU.is_equal))
                first_best(goh[:, :, :], gl, r(0), r(1), NGRP)
                after(V.tensor_tensor(gex[:, :, :], gl, b3(r(0), NGRP), ALU.subtract), "rt_in")
                link(V.tensor_scalar(goh[:, :, :], goh[:, :, :], BIG, -BIG, ALU.mult, ALU.add))
                em, oh1, em2, oh2, both, slot, ovf, pick = [rt[:, i] for i in (0, 1, 2, 3, 9, 4, 5, 6)]
                link(V.tensor_tensor(em.rearrange("p t (g e) -> p t g e", g=NGRP), el.rearrange("p t (g e) -> p t g e", g=NGRP),
                                     bc(goh[:, :, :].unsqueeze(3), [P, NT, NGRP, EPG]), ALU.add))
                first_best(oh1, em, r(2), r(3), NE)
                link(V.scalar_tensor_tensor(em2, oh1, -2 * BIG, em, ALU.mult, ALU.add))
                first_best(oh2, em2, r(4), r(5), NE)
                after(V.tensor_tensor(both, oh1, oh2, ALU.add), "assign")
                after(V.tensor_tensor(r(6), r(4), r(2), ALU.subtract), "rt_in")
                dve.wait_ge(s_["rt_exp"], 2)
                V.tensor_scalar(r(7), r(6), 1.0, None, ALU.add)
                link(V.tensor_reduce(r(8), gex[:, :, :], AX.X, ALU.add))
                link(V.tensor_tensor(r(7), r(7), r(8), ALU.mult))
                link(V.reciprocal(r(9), r(7)))
                link(V.tensor_tensor(r(10), r(9), r(6), ALU.mult))
                dve.wait_ge(s_["pos_mm"], 1)
                w = [row[:, i, :] for i in range(6)]
                link(V.tensor_scalar(w[0], ps[:, 2, 0:NE], float(S - 1), None, ALU.add))
                link(V.tensor_copy(rowi[:, :], w[0]))
                link(V.tensor_scalar(rowi[:, :], rowi[:, :], 6, None, ALU.arith_shift_right))
                link(V.tensor_copy(w[1], rowi[:, :]))
                link(V.tensor_scalar(w[1], w[1], -1.0, 0.0, ALU.add, ALU.max))
                link(V.tensor_tensor_scan(w[2], w[1], w[1], 0.0, ALU.add, ALU.bypass))
                link(V.tensor_tensor(w[3], w[2], w[1], ALU.subtract))
                link(V.tensor_scalar(w[4], w[3], float(S), float(S * (NE - 1)), ALU.mult, ALU.add))
                link(V.tensor_tensor(w[4], w[4], con[:, C_E64:C_E64 + NE], ALU.subtract))
                pos = ps[:, 1, 0:NT * NE].rearrange("p (t e) -> p t e", t=NT)
                link(V.tensor_tensor(slot, pos, c3(C_E64, NE), ALU.add))
                link(V.tensor_scalar(ovf, pos, float(S), None, ALU.is_ge))
                link(V.tensor_tensor(ovf, ovf, bc(w[4].unsqueeze(1), TE), ALU.mult))
                link(V.tensor_tensor(slot, slot, ovf, ALU.add))
                for j, oh in enumerate((oh1, oh2)):
                    link(V.tensor_tensor(pick, oh, slot, ALU.mult))
                    link(V.tensor_reduce(slotf[:, j, :], pick, AX.X, ALU.add))
                link(V.tensor_copy(sloti[:, :, :], slotf[:, :, :]))
                TK = [1, 16, NE]
                kk = bc(con[0:1, C_K:C_K + 16].unsqueeze(2), TK)
                link(V.tensor_tensor(over[:, 0], kk, bc(w[3][0:1].unsqueeze(1), TK), ALU.is_ge))
                link(V.tensor_tensor(over[:, 1], kk, bc(w[2][0:1].unsqueeze(1), TK), ALU.is_lt))
                link(V.tensor_tensor(over[:, 0], over[:, 0], over[:, 1], ALU.mult))
                link(V.tensor_tensor(over[:, 0], over[:, 0], bc(con[0:1, C_E:C_E + NE].unsqueeze(1), TK), ALU.mult))
                link(V.tensor_reduce(overf[:, :], over[:, 0], AX.X, ALU.add))
                link(V.tensor_copy(overf[:, 15:16], w[2][0:1, NE - 1:NE]))
                after(V.tensor_copy(overi[:, :], overf[:, :]), "slots_rdy")

                def take_x(s):
                    return V.tensor_tensor(xeT[s], ps[:, 4 + s, :].rearrange("p (k s) -> p k s", k=KC),
                                           bc(g_ffn[:, :].unsqueeze(2), [P, KC, S]), ALU.mult)

                def gate(s):
                    return V.tensor_tensor(aT[:, s].rearrange("p c s -> p (c s)"), sg[:, s, :], ps[:, 2 + s, 2 * S:4 * S], ALU.mult)

                def expert(e, q, s, first):
                    dve.wait_ge(s_["xeT_mm"], e + 2)
                    after(take_x(1 - s), "xeT_ev")
                    dve.wait_ge(s_["silu_rdy"], e + 1)
                    after(gate(s), "a_rdy")
                    if not first:
                        dve.wait_ge(s_[f"yst{s}"], 16 * q)
                    dve.wait_ge(s_["dn_mm"], e + 1)
                    after(V.tensor_copy(ye[s][:, 512:D], ps[0:S, (1, 7)[s], :]), "y_dve")
                dve.wait_ge(s_["xeT_mm"], 1)
                after(take_x(0), "xeT_ev")
                for s in range(2):
                    expert(s, 0, s, True)
                with dve.Fori(1, NE // 2) as i:
                    for s in range(2):
                        expert(2 * i + s, i, s, False)
                n_over = dve.value_load(overi[0:1, 15:16], min_val=0, max_val=NOVER)
                dve.wait_ge(s_["yst0"], 16 * NE // 2)
                with dve.If(n_over > 0):
                    with dve.Fori(0, n_over) as k:
                        dve.wait_ge(s_["f_T"], k + 1)
                        after(take_x(0), "f_Tev")
                        dve.wait_ge(s_["f_silu"], k + 1)
                        after(gate(0), "f_a")
                        dve.wait_ge(s_["f_dn"], k + 1)
                        after(V.tensor_copy(ye[0][:, 512:D], ps[0:S, 1, :]), "f_ydve")
                        dve.wait_ge(s_["f_end"], k + 1)
                for t in range(NT):
                    for j in range(2):
                        c = 2 * t + j
                        dve.wait_ge(gath, 16 * 2 * NT * l + 16 * 2 * NT)
                        after(V.scalar_tensor_tensor(x[:, t, :], yg[c], rsm[:, 9 + j, t:t + 1], x[:, t, :], ALU.mult, ALU.add), "comb")
                        dve.wait_ge(s_["comb"], c + 1)
                after(dve.drain(), "dve_done")

        @block.gpsimd
        def _(pool):
            G = nc.gpsimd

            def rsqrt(n, dst, src, rows, cols):
                pool.wait_ge(s_["ms_rdy"], n)
                after(G.tensor_tensor(dst, src, neghalf[0:rows, 0:cols], ALU.pow), "rs_rdy")
            G.memset(hT[:, :], 0.0).then_inc(zeros_rdy, 1)
            pool.wait_ge(zeros_rdy, 1)
            n = NSLOT // P
            for i in range(0, n, 4):
                k = min(4, n - i)
                pool.dma_start(xs_dram[i * P:(i + k) * P, :].rearrange("(p r) d -> p (r d)", p=P), hT[:, 0:k * D]).then_inc(zeroed, 16)
            m0 = NE * S
            rest = NSLOT - m0
            zr = rest // P
            for i in range(0, zr, 4):
                k = min(4, zr - i)
                pool.dma_start(ys_dram[m0 + i * P:m0 + (i + k) * P, :].rearrange("(p r) d -> p (r d)", p=P), hT[:, 0:k * D]).then_inc(zeroed, 16)
            if rest % P:
                pool.dma_start(ys_dram[m0 + zr * P:, :], hT[0:rest % P, 0:D]).then_inc(zeroed, 16)
            if NSLOT % P:
                pool.dma_start(xs_dram[n * P:, :], hT[0:NSLOT % P, 0:D]).then_inc(zeroed, 16)
            n_zero = -(-n // 4) - (-zr // 4) + bool(rest % P) + bool(NSLOT % P)
            pool.wait_ge(zeroed, 16 * n_zero)
            pool.wait_ge(setup_dve, 1)
            pool.sem_inc(layer_open, 1)
            with pool.Fori(0, L) as l:
                for n, cols in ((1, NT), (2, 64), (3, 32)):
                    rsqrt(n, rs[:, 0:cols], ss[:, 0:cols], P, cols)
                rsqrt(4, css[:, 2:4], css[:, 0:2], NCMP, 2)
                rsqrt(5, rs[:, 0:16], ss[:, 0:16], P, 16)
                rsqrt(6, rs[:, 0:NT], ss[:, 0:NT], P, NT)
                pool.wait_ge(s_["slots_rdy"], 1)
                for t in range(NT):
                    for j in range(2):
                        pool.indirect_dma_start(xs_dram, bass.IndirectOffsetOnAxis(ap=sloti[:, j, t:t + 1], axis=0), xoc[:, t, :], None).then_inc(scat, 16)
                for s in range(2):
                    pool.wait_ge(s_[f"yst{s}"], 16 * NE // 2)
                n_over = pool.value_load(overi[0:1, 15:16], min_val=0, max_val=NOVER)
                with pool.If(n_over > 0):
                    pool.wait_ge(s_["f_end"], n_over)
                for t in range(NT):
                    for j in range(2):
                        pool.indirect_dma_start(yg[2 * t + j], None, ys_dram, bass.IndirectOffsetOnAxis(ap=sloti[:, j, t:t + 1], axis=0)).then_inc(gath, 16)
                pool.wait_ge(s_["comb"], 2 * NT)
                for n in per_layer[:4]:
                    pool.wait_ge(s_[n], 1)
                for n in per_layer[4:] + per_layer[:4]:
                    pool.sem_clear(s_[n])
                pool.sem_inc(layer_open, 1)
    return nc


_INS = ["x", "rel_bias", "attn_norm", "w_in", "swa_q_norm", "swa_k_norm", "swa_sinks", "nsa_q_norm", "nsa_k_norm",
        "nsa_cmp_pos", "nsa_cmp_w1", "nsa_cmp_w2", "mla_q_lat_norm", "mla_w_q_up", "mla_kv_lat_norm", "mla_w_kv_up",
        "mla_q_norm", "mla_k_norm", "out_norm", "w_out", "ffn_norm", "moe_w_group", "moe_b_group", "moe_w_expert",
        "moe_b_expert", "moe_w_gate", "moe_w_up", "moe_w_down"]


def kernel(**inputs):
    import concourse.bacc as _bacc
    from concourse.bass_utils import run_bass_kernel_spmd as _run

    nc = _bacc.Bacc("TRN2", target_bir_lowering=False, num_devices=1)
    arrays, args = {}, {}

    def put(name, v):
        v = np.ascontiguousarray(v)
        arrays["in_" + name] = v
        return nc.dram_tensor("in_" + name, v.shape, mybir.dt.from_np(v.dtype), kind="ExternalInput").ap()
    for name in _INS:
        args[name] = put(name, inputs[name])
    c, m = constants()
    out = nc.dram_tensor("out_0", (1, T, D), F32, kind="ExternalOutput").ap()
    rows = nc.dram_tensor("bias_rows", (4, P, TN + TS), F32, kind="Internal").ap()
    xs = nc.dram_tensor("expert_in", (NSLOT, D), F32, kind="Internal").ap()
    ys = nc.dram_tensor("expert_out", (NSLOT, D), F32, kind="Internal").ap()
    build(nc, args, put("consts", c), put("bias_map", m), out, rows, xs, ys)
    r = _run(nc, [arrays], core_ids=[0])
    return r.results[0]["out_0"]
```

```python
import math
from contextlib import ExitStack

import numpy as np

import concourse.bass as bass
from concourse import mybir

ALU = mybir.AluOpType
ACT = mybir.ActivationFunctionType
AX = mybir.AxisListType
F32 = mybir.dt.float32
I32 = mybir.dt.int32
U32 = mybir.dt.uint32

P = 128
T = 512
NT = T // P
D = 1024
KC = D // P
L = 2
HD = 64
EPS = 1e-6
BIG = 1e30

SBQ, SBK, SBV = 0, 256, 512
SWQ, SWK, SWV = 768, 1024, 1152
NQ, NKC, NVC, NKS, NVS, NKW, NVW, NG = 1280, 1536, 1664, 1792, 1920, 2048, 2176, 2304
MCQ, MCKV, MKPE, COLS = 2316, 2508, 2636, 2668
WCH = 384
CHUNKS = [(c, min(WCH, COLS - c)) for c in range(0, COLS, WCH)]

QR, KVR, NOPE, ROPE = 192, 128, 64, 32
MQK = NOPE + ROPE
HALF = ROPE // 2
CMP_L, CMP_S, CMP_H = 32, 16, 128
NCMP = T // CMP_S - 1
BUCKETS = 32

NGRP, EPG, NE = 4, 8, 32
FH = 256
S = 64
NOVER = 2 * T // S - 1
NTILE = NE + NOVER
NSLOT = NTILE * S

UN = 896
TN = UN + P - 1
US = 256
TS = US + P - 1

C_ID, C_TRI, C_CM, C_SM, C_COS, C_SIN, C_IM, C_E64, C_E, C_K = np.cumsum([0, P, P, T, T, 64, 64, NE, NE, NE]).tolist()
NCON = C_K + 16

SL_A, SL_B, SL_C, SL_D, SL_X = 0, 8, 14, 22, 30
SL_L = 27
NSL = 34


def t5_bucket(n):
    n = np.maximum(n, 0)
    half = BUCKETS // 2
    nf = np.maximum(n, 1).astype(np.float32)
    large = half + (np.log(nf / np.float32(half)) / np.float32(math.log(1024 / half)) * np.float32(BUCKETS - half)).astype(np.int32)
    return np.where(n < half, n, np.minimum(large, BUCKETS - 1))


def constants():
    c = np.zeros((P, NCON), np.float32)
    p = np.arange(P)[:, None]
    c[:, C_ID:C_ID + P] = np.eye(P)
    c[:, C_TRI:C_TRI + P] = p < np.arange(P)[None]
    dist = p + 384 - np.arange(T)[None]
    c[:, C_CM:C_CM + T] = np.where(dist >= 0, 0, BIG)
    c[:, C_SM:C_SM + T] = np.where(dist > 0, 0, -BIG)
    inv = (np.float32(10000.0) ** (-np.arange(0, ROPE, 2, dtype=np.float32) / np.float32(ROPE))).astype(np.float32)
    ang = (np.arange(T, dtype=np.float32)[:, None] * inv[None]).astype(np.float32).reshape(NT, P, HALF)
    c[:, C_COS:C_COS + 64] = np.cos(ang).transpose(1, 0, 2).reshape(P, 64)
    c[:, C_SIN:C_SIN + 64] = np.sin(ang).transpose(1, 0, 2).reshape(P, 64)
    c[:, C_IM:C_IM + NE] = np.arange(NE) - 1000
    c[:, C_E64:C_E64 + NE] = np.arange(NE) * S
    c[:, C_E:C_E + NE] = np.arange(NE)
    c[:, C_K:C_K + 16] = np.arange(16)
    m = np.zeros((BUCKETS + 1, TN + TS), np.float32)
    dn = T - 1 - np.arange(TN)
    ds = US - 1 - np.arange(TS)
    m[t5_bucket(dn), np.arange(TN)] = 1
    m[t5_bucket(ds), TN + np.arange(TS)] = 1
    m[BUCKETS, :TN] = np.where(dn >= 0, 0, -BIG)
    m[BUCKETS, TN:] = np.where((ds >= 0) & (ds < P), 0, -BIG)
    return c, m


def build(nc, a, consts, bias_map, out, bias_rows, xs_dram, ys_dram):
    with ExitStack() as ctx:
        def sb(name, shape, dt=F32):
            return ctx.enter_context(nc.sbuf_tensor(name, shape, dt))

        def sem(name):
            return ctx.enter_context(nc.semaphore(name))

        con = sb("con", [P, NCON])
        ones = sb("ones", [P, P])
        neghalf = sb("neghalf", [P, 64])
        x = sb("x", [P, NT, D])
        xo = sb("xo", [P, NT * D])
        hT = sb("hT", [P, NT * D])
        big = sb("big", [P, NT * COLS + NSL * T])
        sq = sb("sq", [P, 3584])
        gn = sb("gn", [P, 4, UN])
        gs = sb("gs", [P, 4, US])
        relx = sb("relx", [BUCKETS + 1, 8])
        g_attn, g_out, g_ffn = sb("g_attn", [P, KC]), sb("g_out", [P, KC]), sb("g_ffn", [P, KC])
        g64 = sb("g64", [HD, 6])
        g_lq, g_lkv, g_qk = sb("g_lq", [MQK, 2]), sb("g_lkv", [KVR, 1]), sb("g_qk", [P, 2, MQK])
        sink, nsink = sb("sink", [P, 4]), sb("nsink", [P, 4])
        cpos, cposT = sb("cpos", [CMP_L, P]), sb("cposT", [P, CMP_L])
        zero = sb("zero", [P, 256])
        w_cmp2 = sb("w_cmp2", [P, 2, HD])
        rbias, w_rt = sb("rbias", [P, 36]), sb("w_rt", [P, KC, 36])
        ss, rs = sb("ss", [P, 64]), sb("rs", [P, 64])
        gates = sb("gates", [P, NT, 12])
        hcmp = sb("hcmp", [P, 2, 2, 32])
        kcmp, vcmp = sb("kcmp", [NCMP, 2, HD]), sb("vcmp", [NCMP, 2, HD])
        kcmpT = sb("kcmpT", [HD, 2, 32])
        csq, css = sb("csq", [NCMP, 2, HD]), sb("css", [NCMP, 4])
        mrow, den = sb("mrow", [P, 96]), sb("den", [P, 96])
        den2, esink = sb("den2", [P, 4]), sb("esink", [P, 4 * NT])
        g64q = sb("g64q", [HD, 2])
        otmp = sb("otmp", [P, NT, HD])
        lg = sb("lg", [P, NT, 36])
        rsm = sb("rsm", [P, 12, NT])
        goh, gex = sb("goh", [P, NT, NGRP]), sb("gex", [P, NT, NGRP])
        row, rowi = sb("row", [P, 6, NE]), sb("rowi", [P, NE], I32)
        slotf, sloti = sb("slotf", [P, 2, NT]), sb("sloti", [P, 2, NT], U32)
        overi = sb("overi", [1, 16], I32)
        overf = sb("overf", [1, 16])
        rt = sq[:, 1024:1024 + 10 * NT * NE].rearrange("p (a t e) -> p a t e", a=10, t=NT)
        over = sq[0:1, 0:2 * 16 * NE].rearrange("p (a k e) -> p a k e", a=2, k=16)
        sg = hT[0:S, 3072:3072 + 2 * FH].rearrange("p (i f) -> p i f", i=2)
        aT = hT[:, 3072 + 2 * FH:3072 + 2 * FH + 4 * S].rearrange("p (i c s) -> p i c s", i=2, c=2)

        ps = ctx.enter_context(nc.psum_tensor("ps", [P, 8, 512], F32))

        ident = con[:, C_ID:C_ID + P]
        hTc = hT[:, :].rearrange("p (k t) -> p k t", k=KC)
        xoc = xo[:, :].rearrange("p (t d) -> p t d", t=NT)
        proj = big[:, 0:NT * COLS].rearrange("p (t c) -> p t c", t=NT)
        heads = big[:, NT * COLS:].rearrange("p (s t) -> p s t", s=NSL)
        base = NT * COLS
        win = [big[:, base + SL_D * T + i * KC * WCH:base + SL_D * T + (i + 1) * KC * WCH].rearrange("p (k n) -> p k n", k=KC) for i in range(2)]
        bmap = big[0:BUCKETS + 1, base + 16 * T:base + 19 * T]
        w_qup = sq[0:MQK, 1536:1536 + 2 * 384].rearrange("p (c n) -> p c n", c=2)
        w_kvup = sq[:, 2304:2304 + 512]
        vlat = sq[:, 0:NT * 256].rearrange("p (t c) -> p t c", t=NT)
        w1 = xo[:, :].rearrange("p (l f) -> p l f", l=CMP_L)
        EW = 3 * KC * FH
        w_o = big[:, EW:EW + KC * D].rearrange("p (k n) -> p k n", k=KC)
        ring_g, ring_u, ring_d, ring_gu = [], [], [], []
        for b in (0, EW + KC * D, 2 * EW + KC * D, EW):
            ring_g.append(big[:, b:b + KC * FH].rearrange("p (k f) -> p k f", k=KC))
            ring_gu.append(big[:, b:b + 2 * KC * FH].rearrange("p (g k f) -> p g k f", g=2, k=KC))
            ring_u.append(big[:, b + KC * FH:b + 2 * KC * FH].rearrange("p (k f) -> p k f", k=KC))
            ring_d.append(big[:, b + 2 * KC * FH:b + EW].rearrange("p (c n) -> p c n", c=2))
        yg = [big[:, i * D:(i + 1) * D] for i in range(8)]
        sqh = sq[:, 0:NT * WCH].rearrange("p (t c) -> p t c", t=NT)
        dqk = [proj[:, :, c:c + 4 * MQK].rearrange("p t (h c) -> p t h c", h=4) for c in (0, 2 * WCH)]
        dtm = [b.rearrange("p (t h c) -> p t h c", t=NT, h=4) for b in
               (big[:, base + (SL_D + 5) * T:base + (SL_D + 5) * T + 256], big[:, base + (SL_D + 5) * T + 256:base + (SL_D + 6) * T],
                big[:, base + (SL_D + 6) * T:base + (SL_D + 6) * T + 256], big[:, base + (SL_D + 6) * T + 256:base + (SL_D + 7) * T])]
        lgt = [hT[:, i * T:(i + 1) * T] for i in range(3)]
        prb = [hT[:, (3 + i) * T:(4 + i) * T] for i in range(2)]
        prT = [hT[:, (5 + i) * T:(6 + i) * T] for i in range(2)]
        keep = [heads[:, SL_D + i, :] for i in range(2)]
        left = [big[:, base + (SL_D + 2) * T + i * 520:base + (SL_D + 2) * T + i * 520 + T + 1] for i in range(2)]
        xe = [hT[0:S, i * D:(i + 1) * D] for i in range(2)]
        xeT = [hT[:, 2048 + i * T:2048 + (i + 1) * T].rearrange("p (k s) -> p k s", k=KC) for i in range(2)]
        ye = [sq[0:S, i * D:(i + 1) * D] for i in range(2)]

        kept = ("bias_map_in x_in setup_dve bias_mm bias_neg bias_out bias_in zeros_rdy zeroed layer_open entered "
                "scat gath out_done").split()
        (bias_map_in, x_in, setup_dve, bias_mm, bias_neg, bias_out, bias_in, zeros_rdy, zeroed, layer_open, entered,
         scat, gath, out_done) = [sem(n) for n in kept]
        per_layer = ("sp_done pe_done act_done dve_done params win_a win_b w1_in wout_in dve_step sum_rdy ms_rdy rs_rdy xn_rdy "
                     "tr_act tr_dve ev_act ev_dve pj_mm pj_ev_act pj_ev_dve norms_rdy up_mm up_ev_act up_ev_dve "
                     "cmp_mm cmp_ev cmp_out cmp_n cmpT_mm cmpT_ev rope_step dqk_rdy lat_T lat_ev sq_used scores logits probs_sm sig probs_sb "
                     "probT probT_ev pv head_out esink_rdy o_rdy wo_mm wo_ev lg_mm rt_in rt_exp assign pos_mm slots_rdy "
                     "wg0 wg1 wg2 wg3 wu0 wu1 wu2 wu3 wd0 wd1 wd2 wd3 xe0 xe1 xeT_mm xeT_ev gu_mm silu_rdy a_rdy aT_mm aT_ev dn_mm y_act y_dve "
                     "yst0 yst1 f_in f_step f_loop f_T f_Tev f_gu f_silu f_a f_aT f_aTev f_dn f_yact f_ydve f_st f_end comb").split()
        s_ = {n: sem(n) for n in per_layer}

        def after(ins, s, n=1):
            return ins.then_inc(s_[s], n)

        block = ctx.enter_context(nc.Block())

        def enter(eng, l):
            eng.wait_ge(layer_open, l + 1)
            eng.sem_inc(entered, 1)

        def params(l):
            def of(name):
                return a[name][bass.ds(l, 1)]
            return [
                (g_attn[:, :], of("attn_norm").rearrange("o (p k) -> p (o k)", k=KC)),
                (g_out[:, :], of("out_norm").rearrange("o (p k) -> p (o k)", k=KC)),
                (g_ffn[:, :], of("ffn_norm").rearrange("o (p k) -> p (o k)", k=KC)),
                (g64[:, 0:1], of("swa_q_norm").rearrange("o p -> p o")),
                (g64[:, 1:2], of("swa_k_norm").rearrange("o p -> p o")),
                (g64[:, 2:3], of("nsa_q_norm").rearrange("o p -> p o")),
                (g64[:, 3:4], of("nsa_k_norm")[:, 0].rearrange("o p -> p o")),
                (g64[:, 4:5], of("nsa_k_norm")[:, 1].rearrange("o p -> p o")),
                (g64[:, 5:6], of("nsa_k_norm")[:, 2].rearrange("o p -> p o")),
                (g_lq[:, :], of("mla_q_lat_norm").rearrange("o (p k) -> p (o k)", k=2)),
                (g_lkv[:, :], of("mla_kv_lat_norm").rearrange("o p -> p o")),
                (g_qk[:, 0, :], of("mla_q_norm").broadcast_to([P, MQK])),
                (g_qk[:, 1, :], of("mla_k_norm").broadcast_to([P, MQK])),
                (sink[:, :], of("swa_sinks").broadcast_to([P, 4])),
                (cpos[:, 0:HD], of("nsa_cmp_pos")[:, 0].rearrange("o l d -> (o l) d")),
                (cpos[:, HD:], of("nsa_cmp_pos")[:, 1].rearrange("o l d -> (o l) d")),
                (w_cmp2[:, :, :], of("nsa_cmp_w2").rearrange("o c f d -> f (o c) d")),
                (rbias[:, 0:NGRP], of("moe_b_group").broadcast_to([P, NGRP])),
                (rbias[:, NGRP:], of("moe_b_expert").broadcast_to([P, NE])),
                (w_rt[:, :, 0:NGRP], of("moe_w_group").rearrange("o (p k) n -> p (o k) n", k=KC)),
                (w_rt[:, :, NGRP:], of("moe_w_expert").rearrange("o (p k) n -> p (o k) n", k=KC)),
                (w_qup, of("mla_w_q_up").rearrange("o (p c) n -> p (o c) n", c=2)),
                (w_kvup, of("mla_w_kv_up").rearrange("o p n -> p (o n)")),
            ]
        ALL_PARAMS = 16 * len(params(0))

        abc = ([(SBQ + h * HD, SL_A + h, 1.0) for h in range(4)] + [(SBK + h * HD, SL_A + 4 + h, 1.0) for h in range(4)]
               + [(SWQ + h * HD, SL_B + h, g64q[:, 0:1]) for h in range(4)] + [(SWK + h * HD, SL_B + 4 + h, g64[:, 1:2]) for h in range(2)]
               + [(NQ + h * HD, SL_C + h, g64q[:, 1:2]) for h in range(4)] + [(NKS + h * HD, SL_C + 4 + h, g64[:, 4:5]) for h in range(2)]
               + [(NKW + h * HD, SL_C + 6 + h, g64[:, 5:6]) for h in range(2)])
        def by_head(t):
            return (proj[:, t, NKC:NKC + 4 * HD].rearrange("p (h c d) -> p c h d", c=2, h=2),
                    ps[:, t, 0:4 * HD].rearrange("p (c h d) -> p c h d", c=2, h=2))

        G_X = (0, 0)
        G_POS = (4, 4)
        G_ABC = (5, 4)
        G_LAT = (16, 15)
        G_CMP = (18, 16)
        G_O = (18, 18)
        G_H = (22, 22)
        G_END = (26, 26)
        ABC_OF = [[j for j, (col, _, _) in enumerate(abc) if c0 <= col < c0 + n] for c0, n in CHUNKS]
        NORMED = {2: (SWQ, 6, 0), 3: (NQ, 4, 24), 4: (NKS, 2, 40), 5: (NKW, 2, 48)}
        R_LAT, R_CMP, R_D, R_O, R_X2 = 6, 7, 8, 9, 10

        units = [(kind, h, i, {"B": P * min(i + 1, 2), "cmp": NCMP}.get(kind, P * (i + 1)))
                 for kind in ("A", "B", "cmp", "slc", "win", "D") for h in range(4) for i in range(NT)]
        NU = len(units)
        NSB = 4 * NT
        U_CMP = 2 * NSB
        U_NORMC, U_CMPT = 3, 14
        U_SUMD, U_LAT = 4, 56

        def q_of(kind, h, i):
            c = slice(i * P, (i + 1) * P)
            if kind == "A":
                return heads[0:HD, SL_A + h, c]
            if kind == "B":
                return heads[0:HD, SL_B + h, c]
            if kind == "D":
                return heads[0:MQK, SL_D + h, c]
            return heads[0:HD, SL_C + h, c]

        def k_of(kind, h, i, n):
            if kind == "A":
                return heads[0:HD, SL_A + 4 + h, 0:n]
            if kind == "B":
                return heads[0:HD, SL_B + 4 + h // 2, (i + 1) * P - n:(i + 1) * P]
            if kind == "cmp":
                return kcmpT[:, h // 2, 0:NCMP]
            if kind == "slc":
                return heads[0:HD, SL_C + 4 + h // 2, 0:n]
            if kind == "win":
                return heads[0:HD, SL_C + 6 + h // 2, 0:n]
            return heads[0:MQK, SL_D + 4 + h, 0:n]

        def v_of(kind, h, t):
            if kind == "A":
                return proj[:, t, SBV + h * HD:SBV + (h + 1) * HD]
            if kind == "B":
                return proj[:, t, SWV + (h // 2) * HD:SWV + (h // 2 + 1) * HD]
            if kind == "slc":
                return proj[:, t, NVS + (h // 2) * HD:NVS + (h // 2 + 1) * HD]
            if kind == "win":
                return proj[:, t, NVW + (h // 2) * HD:NVW + (h // 2 + 1) * HD]
            return vlat[:, t, h * HD:(h + 1) * HD]

        def bias_of(kind, h, i, n):
            if kind == "B":
                return gs[:, h, US - n:US]
            if kind == "D":
                return con[:, C_CM + T - n:C_CM + T]
            if kind == "A":
                return con[:, C_SM + T - n:C_SM + T]
            if kind == "cmp":
                u0 = P * (NT - 1 - i) + CMP_L - 1
                return gn[:, h, u0:u0 + CMP_S * (NCMP - 1) + 1:CMP_S]
            return gn[:, h, P * (NT - 1 - i):P * (NT - 1 - i) + n]

        def blocks_of(kind, i, n):
            if kind == "cmp":
                return [(0, NCMP, 0)]
            first = i + 1 - n // P
            return [(b * P, P, first + b) for b in range(n // P)]

        @block.sync
        def _(sp):
            sp.dma_start(x[:, :, :], a["x"].rearrange("b (t p) d -> p (b t) d", p=P)).then_inc(x_in, 16)
            sp.dma_start(con[:, :], consts).then_inc(bias_map_in, 16)
            sp.dma_start(relx[0:BUCKETS, :], a["rel_bias"]).then_inc(bias_map_in, 16)
            sp.dma_start(bmap[:, 0:TN + TS], bias_map).then_inc(bias_map_in, 16)
            with sp.Fori(0, L) as l:
                def load(dst, src, s):
                    sp.dma_start(dst, src).then_inc(s_[s], 16)

                def load_win(c):
                    c0, n = CHUNKS[c]
                    load(win[c % 2][:, :, 0:n], a["w_in"][bass.ds(l, 1)].rearrange("o (p k) n -> p (o k) n", k=KC)[:, :, c0:c0 + n],
                         ("win_a", "win_b")[c % 2])
                enter(sp, l)
                load_win(0)
                load_win(1)
                for dst, src in params(l):
                    load(dst, src, "params")
                for c in range(2, len(CHUNKS)):
                    sp.wait_ge(s_["pj_mm"], NT * (c - 1))
                    load_win(c)
                for c in range(2):
                    load(w1[c * HD:(c + 1) * HD], a["nsa_cmp_w1"][bass.ds(l, 1), c].rearrange("o l d f -> d (o l) f"), "w1_in")
                sp.wait_ge(s_["pv"], NU - 4 * NT)
                load(w_o, a["w_out"][bass.ds(l, 1)].rearrange("o (p k) n -> p (o k) n", k=KC), "wout_in")

                def gate_up_of(e):
                    return [a[n][bass.ds(l, 1), bass.ds(e, 1)].rearrange("a b (p k) f -> p (a b k) f", k=KC)
                            for n in ("moe_w_gate", "moe_w_up")]

                def down_of(e):
                    return a["moe_w_down"][bass.ds(l, 1), bass.ds(e, 1)].rearrange("a b (p c) n -> p (a b c) n", c=2)
                def ring(e, s):
                    g, u = gate_up_of(e)
                    load(ring_g[s], g, f"wg{s}")
                    load(ring_u[s], u, f"wu{s}")
                    load(ring_d[s], down_of(e), f"wd{s}")
                ring(0, 0)
                ring(1, 1)
                sp.wait_ge(s_["pv"], NU)
                ring(2, 2)
                sp.wait_ge(s_["wo_mm"], 2 * NT)
                ring(3, 3)
                sp.wait_ge(scat, 16 * 2 * NT * l + 16 * 2 * NT)
                sp.wait_ge(s_["lg_mm"], 1)
                for s in range(2):
                    load(xe[s], xs_dram[s * S:(s + 1) * S, :], f"xe{s}")
                with sp.Fori(1, NE // 4) as i:
                    for s in range(4):
                        g, u = gate_up_of(4 * i + s)
                        sp.wait_ge(s_["gu_mm"], 4 * i + s - 3)
                        load(ring_g[s], g, f"wg{s}")
                        load(ring_u[s], u, f"wu{s}")
                        sp.wait_ge(s_["dn_mm"], 4 * i + s - 3)
                        load(ring_d[s], down_of(4 * i + s), f"wd{s}")
                sp.wait_ge(s_["dn_mm"], NE)
                sp.wait_ge(s_["xeT_mm"], NE + 1)
                for s in range(2):
                    sp.wait_ge(s_[f"xe{s}"], 16 * (NE // 2 + 1))
                n_over = sp.value_load(overi[0:1, 15:16], min_val=0, max_val=NOVER)
                with sp.If(n_over > 0):
                    with sp.Fori(0, n_over) as k:
                        e = sp.value_load(overi[0:1, bass.ds(k, 1)], min_val=0, max_val=NE - 1)
                        g, u = gate_up_of(e)
                        load(ring_g[0], g, "f_in")
                        load(ring_u[0], u, "f_in")
                        load(ring_d[0], down_of(e), "f_in")
                        load(xe[0], xs_dram[bass.ds(k * S + NE * S, S), :], "f_in")
                        sp.wait_ge(s_["f_end"], k + 1)
                        sp.sem_inc(s_["f_loop"], 1)
                after(sp.drain(), "sp_done")
            sp.wait_ge(layer_open, L + 1)
            sp.dma_start(out.rearrange("b (t p) d -> p (b t) d", p=P), x[:, :, :]).then_inc(out_done, 16)
            sp.wait_ge(out_done, 16)

        @block.tensor
        def _(pe):
            mm = nc.tensor.matmul

            def transposes(srcs, rows, n, on, kp=P):
                tr, ev, bank = (("tr_act", "ev_act", 4), ("tr_dve", "ev_dve", 5))[on]
                if n:
                    pe.wait_ge(s_[ev], n)
                for i, src in enumerate(srcs):
                    ins = nc.tensor.transpose(ps[0:rows, bank, i * kp:(i + 1) * kp], src, con[0:kp, C_ID:C_ID + kp])
                after(ins, tr)

            pe.wait_ge(bias_map_in, 48)
            pe.wait_ge(setup_dve, 1)
            for c in range(3):
                n = min(512, TN + TS - c * 512)
                mm(ps[0:8, c, 0:n], relx[:, :], bmap[:, c * 512:c * 512 + n], start=True, stop=True).then_inc(bias_mm, 1)
            pe.wait_ge(bias_neg, 3)
            with pe.Fori(0, L) as l:
                enter(pe, l)
                pe.wait_ge(s_["xn_rdy"], NT)
                for k in range(KC):
                    transposes([xoc[:, t, k::KC] for t in range(NT)], P, G_X[k % 2] + k // 2, k % 2)
                pe.wait_ge(s_["params"], ALL_PARAMS)
                transposes([cpos[:, :]], P, G_POS[0], 0, kp=CMP_L)
                pe.wait_ge(s_["ev_act"], G_POS[0])
                pe.wait_ge(s_["ev_dve"], G_POS[1])

                def head_groups(c):
                    pe.wait_ge(s_["pj_ev_act"], 2 * c + 2)
                    pe.wait_ge(s_["pj_ev_dve"], 2 * c + 2)
                    if c in NORMED:
                        pe.wait_ge(s_["norms_rdy"], c - 1)
                    for j in ABC_OF[c]:
                        col = abc[j][0]
                        transposes([proj[:, t, col:col + HD] for t in range(NT)], HD, G_ABC[j % 2] + j // 2, j % 2)
                for c, (c0, n) in enumerate(CHUNKS):
                    pe.wait_ge(s_[("win_a", "win_b")[c % 2]], 16 * (c // 2 + 1))
                    for t in range(NT):
                        if c:
                            pe.wait_ge(s_[("pj_ev_act", "pj_ev_dve")[t % 2]], 2 * (c - 1) + t // 2 + 1)
                        for k in range(KC):
                            ins = mm(ps[:, t, 0:n], hTc[:, k, t * P:(t + 1) * P], win[c % 2][:, k, 0:n], start=k == 0, stop=k == KC - 1)
                        after(ins, "pj_mm")
                    if c:
                        head_groups(c - 1)
                pe.wait_ge(s_["pj_ev_act"], 2 * len(CHUNKS))
                pe.wait_ge(s_["pj_ev_dve"], 2 * len(CHUNKS))
                for h in range(2):
                    transposes([proj[:, t, NKC + h * P:NKC + (h + 1) * P] for t in range(NT)], P, G_CMP[1] - 1 + h, 1)
                pe.wait_ge(s_["norms_rdy"], 5)
                transposes([proj[:, t, MCQ:MCQ + QR:2] for t in range(NT)], MQK, G_LAT[0], 0)
                transposes([proj[:, t, MCKV:MCKV + KVR] for t in range(NT)], KVR, G_LAT[0] + 1, 0)
                transposes([proj[:, t, MCQ + 1:MCQ + QR:2] for t in range(NT)], MQK, G_LAT[1] + 2, 1)
                pe.wait_ge(s_["w1_in"], 32)

                def compress(c):
                    r = slice(c * HD, (c + 1) * HD)
                    for j in range(CMP_L):
                        slot = SL_X + 2 * (j // CMP_S)
                        src = heads[r, slot:slot + 2, j:j + CMP_S * (NCMP - 1) + 1:CMP_S]
                        ins = mm(ps[:, 6 + c, 0:2 * NCMP], w1[r, j, :], src, start=j == 0, stop=j == CMP_L - 1)
                    after(ins, "cmp_mm")
                pe.wait_ge(s_["ev_dve"], G_CMP[1] + 1)
                compress(0)
                pe.wait_ge(s_["params"], ALL_PARAMS)
                pe.wait_ge(s_["ev_act"], G_O[0])
                pe.wait_ge(s_["ev_dve"], G_O[1])
                for t in range(NT):
                    if t >= 2:
                        pe.wait_ge(s_["up_ev_act"], t - 1)
                        pe.wait_ge(s_["up_ev_dve"], t - 1)
                    for c in range(2):
                        mm(ps[:, 2 * (t % 2), 0:384], heads[0:MQK, SL_L + c, t * P:(t + 1) * P], w_qup[:, c, :], start=c == 0, stop=c == 1)
                    after(mm(ps[:, 2 * (t % 2) + 1, :], heads[:, SL_L + 2, t * P:(t + 1) * P], w_kvup, start=True, stop=True), "up_mm")
                compress(1)
                pe.wait_ge(s_["cmp_ev"], 2)
                for c in range(2):
                    for h in range(2):
                        ins = mm(ps[0:NCMP, 7, (2 * c + h) * HD:(2 * c + h + 1) * HD], hcmp[:, c, h, 0:NCMP], w_cmp2[:, c, :], start=True, stop=True)
                after(ins, "cmp_out")
                pe.wait_ge(s_["up_ev_act"], NT)
                pe.wait_ge(s_["up_ev_dve"], NT)

                def scores(u):
                    kind, h, i, n = units[u]
                    if u >= 3:
                        pe.wait_ge(s_["logits"], u - 2)
                    after(mm(ps[:, u % 3, 0:n], q_of(kind, h, i), k_of(kind, h, i, n), start=True, stop=True), "scores")

                def turn(u):
                    kind, h, i, n = units[u]
                    if kind == "A":
                        pe.wait_ge(s_["probs_sb"], u + 1)
                    else:
                        pe.wait_ge(s_["probs_sm"], u + 1 - NSB)
                    if u >= 2:
                        pe.wait_ge(s_["probT_ev"], u - 1)
                    for c0, w, _ in blocks_of(kind, i, n):
                        ins = nc.tensor.transpose(ps[0:w, 3 + u % 2, c0:c0 + P], prb[u % 2][:, c0:c0 + w], ident)
                    after(ins, "probT")

                def values(u):
                    kind, h, i, n = units[u]
                    g = u // NT
                    if i == 0 and g >= 2:
                        pe.wait_ge(s_["head_out"], g - 1)
                    pe.wait_ge(s_["probT_ev"], u + 1)
                    bl = blocks_of(kind, i, n)
                    for j, (c0, w, kt) in enumerate(bl):
                        v = vcmp[:, h // 2, :] if kind == "cmp" else v_of(kind, h, kt)
                        ins = mm(ps[:, 5 + g % 2, i * HD:(i + 1) * HD], prT[u % 2][0:w, c0:c0 + P], v, start=j == 0, stop=j == len(bl) - 1)
                    after(ins, "pv")
                for u in range(-2, NU + 1):
                    if u + 2 < NU:
                        scores(u + 2)
                    if 0 <= u < NU:
                        turn(u)
                    if u >= 1:
                        values(u - 1)
                    if u == U_CMPT:
                        pe.wait_ge(s_["cmp_n"], 1)
                        for h in range(2):
                            ins = nc.tensor.transpose(ps[0:HD, 7, h * 32:h * 32 + NCMP], kcmp[:, h, :], con[0:NCMP, C_ID:C_ID + NCMP])
                        after(ins, "cmpT_mm")
                    if u + 2 == U_CMP:
                        pe.wait_ge(s_["cmpT_ev"], 1)
                    if U_LAT <= u < U_LAT + 8:
                        h = u - U_LAT
                        if h == 0:
                            pe.wait_ge(s_["dqk_rdy"], 1)
                        else:
                            pe.wait_ge(s_["lat_ev"], h)
                        for t in range(NT):
                            ins = nc.tensor.transpose(ps[0:MQK, 7, t * P:(t + 1) * P], dqk[h // 4][:, t, h % 4, :], ident)
                        after(ins, "lat_T")
                    if u == U_LAT + 8:
                        pe.wait_ge(s_["lat_ev"], 8)
                pe.wait_ge(s_["o_rdy"], 1)
                for k in range(KC):
                    transposes([xoc[:, t, k::KC] for t in range(NT)], P, G_O[k % 2] + k // 2, k % 2)
                pe.wait_ge(s_["ev_act"], G_H[0])
                pe.wait_ge(s_["ev_dve"], G_H[1])
                pe.wait_ge(s_["wout_in"], 16)
                for j in range(2 * NT):
                    if j >= 4:
                        pe.wait_ge(s_["wo_ev"], j - 3)
                    for k in range(KC):
                        ins = mm(ps[:, j % 4, :], hTc[:, k, j // 2 * P:(j // 2 + 1) * P], w_o[:, k, j % 2 * 512:(j % 2 + 1) * 512], start=k == 0, stop=k == KC - 1)
                    after(ins, "wo_mm")
                pe.wait_ge(s_["xn_rdy"], 2 * NT)
                for k in range(KC):
                    transposes([xoc[:, t, k::KC] for t in range(NT)], P, G_H[k % 2] + k // 2, k % 2)
                pe.wait_ge(s_["ev_act"], G_END[0])
                pe.wait_ge(s_["ev_dve"], G_END[1])
                for t in range(NT):
                    for k in range(KC):
                        ins = mm(ps[:, 0, t * 36:(t + 1) * 36], hTc[:, k, t * P:(t + 1) * P], w_rt[:, k, :], start=k == 0, stop=k == KC - 1)
                after(ins, "lg_mm")
                pe.wait_ge(s_["assign"], 1)
                for t in range(NT):
                    mm(ps[:, 1, t * NE:(t + 1) * NE], con[:, C_TRI:C_TRI + P], rt[:, 9, t, :], start=True, stop=t == 0)
                    for b in range(t):
                        mm(ps[:, 1, t * NE:(t + 1) * NE], ones[:, :], rt[:, 9, b, :], start=False, stop=b == t - 1)
                for t in range(NT):
                    ins = mm(ps[:, 2, 0:NE], ones[:, :], rt[:, 9, t, :], start=t == 0, stop=t == NT - 1)
                after(ins, "pos_mm")

                def turn_x(s):
                    for k in range(KC):
                        ins = nc.tensor.transpose(ps[:, 4 + s, k * S:(k + 1) * S], xe[s][:, k::KC], con[0:S, C_ID:C_ID + S])
                    return ins

                def gate_up(s, ks):
                    for k in ks:
                        ins = mm(ps[0:S, 2 + s % 2, :].rearrange("p (g f) -> p g f", g=2), xeT[s % 2][:, k, :], ring_gu[s][:, :, k, :],
                                 start=k == 0, stop=k == KC - 1)
                    return ins

                def turn_a(b):
                    for c in range(2):
                        ins = nc.tensor.transpose(ps[:, 2 + b, c * S:(c + 1) * S], sg[:, b, c::2], con[0:S, C_ID:C_ID + S])
                    return ins

                def down(s):
                    for hf in range(2):
                        for c in range(2):
                            ins = mm(ps[0:S, (0, 6)[s % 2] + hf, :], aT[:, s % 2, c, :], ring_d[s][:, c, hf * 512:(hf + 1) * 512], start=c == 0, stop=c == 1)
                    return ins

                def expert(e, q, s, first):
                    pe.wait_ge(s_[f"wg{s}"], 16 * q + 16)
                    pe.wait_ge(s_[f"wu{s}"], 16 * q + 16)
                    pe.wait_ge(s_["xeT_ev"], e + 1)
                    gate_up(s, range(3))
                    if not first or s >= 1:
                        pe.wait_ge(s_["a_rdy"], e)
                    gate_up(s, [3])
                    if not first or s >= 1:
                        after(turn_a(1 - s % 2), "aT_mm")
                    pe.wait_ge(s_[f"xe{1 - s % 2}"], 32 * q + 16 * ((s + 1) // 2) + 16)
                    gate_up(s, [4])
                    after(turn_x(1 - s % 2), "xeT_mm")
                    after(gate_up(s, range(5, KC)), "gu_mm")
                    if not first or s >= 1:
                        before = (s - 1) % 4
                        if not first or s >= 3:
                            pe.wait_ge(s_["y_act"], e - 2)
                            pe.wait_ge(s_["y_dve"], e - 2)
                        pe.wait_ge(s_[f"wd{before}"], 16 * q + (16 if s else 0))
                        pe.wait_ge(s_["aT_ev"], e)
                        after(down(before), "dn_mm")
                pe.wait_ge(s_["xe0"], 16)
                after(turn_x(0), "xeT_mm")
                pe.wait_ge(s_["slots_rdy"], 1)
                for s in range(4):
                    expert(s, 0, s, True)
                with pe.Fori(1, NE // 4) as i:
                    for s in range(4):
                        expert(4 * i + s, i, s, False)
                pe.wait_ge(s_["a_rdy"], NE)
                after(turn_a(1), "aT_mm")
                pe.wait_ge(s_["y_act"], NE - 2)
                pe.wait_ge(s_["y_dve"], NE - 2)
                pe.wait_ge(s_["wd3"], 16 * NE // 4)
                pe.wait_ge(s_["aT_ev"], NE)
                after(down(3), "dn_mm")
                n_over = pe.value_load(overi[0:1, 15:16], min_val=0, max_val=NOVER)
                pe.wait_ge(s_["xeT_ev"], NE + 1)
                pe.wait_ge(s_["y_act"], NE)
                pe.wait_ge(s_["y_dve"], NE)
                with pe.If(n_over > 0):
                    with pe.Fori(0, n_over) as k:
                        pe.wait_ge(s_["f_in"], 64 * k + 64)
                        pe.sem_inc(s_["f_step"], 1)
                        after(turn_x(0), "f_T")
                        pe.wait_ge(s_["f_Tev"], k + 1)
                        after(gate_up(0, range(KC)), "f_gu")
                        pe.wait_ge(s_["f_a"], k + 1)
                        pe.sem_inc(s_["f_step"], 1)
                        after(turn_a(0), "f_aT")
                        pe.wait_ge(s_["f_aTev"], k + 1)
                        after(down(0), "f_dn")
                        pe.wait_ge(s_["f_end"], k + 1)
                after(pe.drain(), "pe_done")

        @block.scalar
        def _(act):
            def A(out_, in_, f, **kw):
                return nc.scalar.activation(out_, in_, f, **kw)

            def copy_out(n, dst, src, scale=1.0):
                act.wait_ge(s_["tr_act"], n + 1)
                after(A(dst, src, ACT.Identity, scale=scale), "ev_act")

            def sums_x(rounds):
                for t in range(NT):
                    ins = A(hT[:, t * D:(t + 1) * D], x[:, t, :], ACT.Square, accum_out=ss[:, t:t + 1])
                after(ins, "sum_rdy")
            act.wait_ge(x_in, 16)
            act.wait_ge(bias_map_in, 48)
            with act.Fori(0, L) as l:
                enter(act, l)
                sums_x(1)
                act.wait_ge(s_["params"], ALL_PARAMS)
                for k in range(0, KC, 2):
                    copy_out(G_X[0] + k // 2, hTc[:, k, :], ps[:, 4, :], g_attn[:, k:k + 1])
                copy_out(G_POS[0], cposT[:, :], ps[:, 4, 0:CMP_L])
                act.wait_ge(bias_out, 128)

                def head_groups(c):
                    for j in ABC_OF[c]:
                        if j % 2 == 0:
                            copy_out(G_ABC[0] + j // 2, heads[0:HD, abc[j][1], :], ps[0:HD, 4, :], abc[j][2])
                for c, (c0, n) in enumerate(CHUNKS):
                    for t in (0, 2):
                        act.wait_ge(s_["pj_mm"], NT * c + t + 1)
                        if c0 == NKC:
                            A(*by_head(t), ACT.Identity)
                            skip = 4 * HD
                        else:
                            skip = 0
                        after(A(proj[:, t, c0 + skip:c0 + n], ps[:, t, skip:n], ACT.Identity), "pj_ev_act")
                    if c in NORMED or c == 6:
                        act.wait_ge(s_["pj_ev_dve"], 2 * c + 2)
                        act.wait_ge(s_["pj_ev_act"], 2 * c + 2)
                    if c in NORMED:
                        col, nh, _ = NORMED[c]
                        if c > 2:
                            act.wait_ge(s_["sq_used"], c - 2)
                        after(A(sqh[:, :, 0:nh * HD], proj[:, :, col:col + nh * HD], ACT.Square), "sum_rdy")
                    if c == 6:
                        act.wait_ge(s_["sq_used"], 4)
                        for t in range(NT):
                            A(sqh[:, t, 0:QR], proj[:, t, MCQ:MCQ + QR], ACT.Square, accum_out=ss[:, 56 + t:57 + t])
                            ins = A(sqh[:, t, QR:QR + KVR], proj[:, t, MCKV:MCKV + KVR], ACT.Square, accum_out=ss[:, 60 + t:61 + t])
                        after(ins, "sum_rdy")
                    if c:
                        head_groups(c - 1)
                copy_out(G_LAT[0], heads[0:MQK, SL_L, :], ps[0:MQK, 4, :], g_lq[:, 0:1])
                copy_out(G_LAT[0] + 1, heads[:, SL_L + 2, :], ps[:, 4, :], g_lkv[:, 0:1])
                act.wait_ge(s_["cmp_mm"], 1)

                def hidden(c):
                    return A(hcmp[:, c, :, 0:NCMP], ps[:, 6 + c, 0:2 * NCMP].rearrange("p (h n) -> p h n", h=2), ACT.Gelu_apprx_tanh)
                after(hidden(0), "cmp_ev")
                for t in range(NT):
                    act.wait_ge(s_["up_mm"], t + 1)
                    after(A(dqk[0][:, t], ps[:, 2 * (t % 2), 0:384].rearrange("p (h c) -> p h c", h=4), ACT.Identity), "up_ev_act")
                act.wait_ge(s_["cmp_mm"], 2)
                after(hidden(1), "cmp_ev")
                A(gates[:, :, :], proj[:, :, NG:NG + 12], ACT.Sigmoid)

                def probs(u):
                    kind, h, i, n = units[u]
                    act.wait_ge(s_["logits"], u + 1)
                    if u >= 2:
                        act.wait_ge(s_["probT"], u - 1)
                    if kind == "A":
                        if u >= 2:
                            act.wait_ge(s_["probs_sb"], u - 1)
                        A(prb[u % 2][:, 0:n], lgt[u % 3][:, 0:n], ACT.Sigmoid, scale=HD ** -0.5)
                        after(A(keep[u % 2][:, 0:n], lgt[u % 3][:, 0:n], ACT.Sigmoid, scale=-(HD ** -0.5)), "sig")
                        return
                    after(A(prb[u % 2][:, 0:n], lgt[u % 3][:, 0:n], ACT.Exp, bias=mrow[:, u:u + 1], scale=-1.0, accum_out=den[:, u:u + 1]), "probs_sm")
                    if kind == "B" and i == NT - 1:
                        after(A(esink[:, h * NT:(h + 1) * NT], mrow[:, u - 3:u + 1], ACT.Exp, bias=sink[:, h:h + 1]), "esink_rdy")

                def copy_probs(u):
                    kind, h, i, n = units[u]
                    w, m = (NCMP, P) if kind == "cmp" else (P, n)
                    act.wait_ge(s_["probT"], u + 1)
                    if u >= 2:
                        act.wait_ge(s_["pv"], u - 1)
                    after(A(prT[u % 2][0:w, 0:m], ps[0:w, 3 + u % 2, 0:m], ACT.Identity), "probT_ev")
                for u in range(-1, NU):
                    if u + 1 < NU:
                        probs(u + 1)
                    if u >= 0:
                        copy_probs(u)
                    if U_SUMD <= u < U_SUMD + 8:
                        if u == U_SUMD:
                            act.wait_ge(s_["up_ev_act"], NT)
                            act.wait_ge(s_["up_ev_dve"], NT)
                        h = u - U_SUMD
                        for t in range(NT):
                            c = base + SL_L * T + (h * NT + t) * MQK
                            ins = A(big[:, c:c + MQK], dqk[h // 4][:, t, h % 4, :], ACT.Square, accum_out=ss[:, 8 * t + h:8 * t + h + 1])
                        if h == 7:
                            after(ins, "sum_rdy")
                    if U_LAT <= u < U_LAT + 8:
                        h = u - U_LAT
                        act.wait_ge(s_["lat_T"], h + 1)
                        after(A(heads[0:MQK, SL_D + h, :], ps[0:MQK, 7, :], ACT.Identity, scale=-(MQK ** -0.5) if h < 4 else 1.0), "lat_ev")
                act.wait_ge(s_["head_out"], NU // NT)
                for t in range(NT):
                    for g in range(4):
                        c = t * D + g * 256
                        ins = A(hT[:, c:c + 256], xo[:, c:c + 256], ACT.Square, accum_out=ss[:, 4 * t + g:4 * t + g + 1])
                after(ins, "sum_rdy")
                for k in range(0, KC, 2):
                    copy_out(G_O[0] + k // 2, hTc[:, k, :], ps[:, 4, :], g_out[:, k:k + 1])
                act.wait_ge(s_["wo_ev"], 2 * NT)
                sums_x(2)
                for k in range(0, KC, 2):
                    copy_out(G_H[0] + k // 2, hTc[:, k, :], ps[:, 4, :], g_ffn[:, k:k + 1])
                act.wait_ge(s_["rt_in"], 1)
                after(A(gex[:, :, :], gex[:, :, :], ACT.Exp), "rt_exp")
                act.wait_ge(s_["rt_in"], 2)
                after(A(rsm[:, 6, :], rsm[:, 6, :], ACT.Exp), "rt_exp")

                def output(e, q, s, first):
                    b = s % 2
                    if not first or s >= 2:
                        act.wait_ge(s_[f"yst{b}"], 32 * q + 16 * (s // 2))
                    act.wait_ge(s_["dn_mm"], e + 1)
                    after(A(ye[b][:, 0:512], ps[0:S, (0, 6)[b], :], ACT.Identity), "y_act")
                    act.wait_ge(s_["y_act"], e + 1)
                    act.wait_ge(s_["y_dve"], e + 1)
                    after(act.dma_start(ys_dram[bass.ds(e * S, S), :], ye[b]), f"yst{b}", 16)

                def take_a(b):
                    return A(aT[:, b, :, :], ps[:, 2 + b, 0:2 * S].rearrange("p (c s) -> p c s", c=2), ACT.Identity)

                def expert(e, q, s, first):
                    act.wait_ge(s_["xeT_mm"], e + 1)
                    after(act.dma_start(xe[s % 2], xs_dram[bass.ds(e * S + 2 * S, S), :]), f"xe{s % 2}", 16)
                    if not first or s >= 1:
                        act.wait_ge(s_["aT_mm"], e)
                        after(take_a(1 - s % 2), "aT_ev")
                    act.wait_ge(s_["gu_mm"], e + 1)
                    after(A(sg[:, s % 2, :], ps[0:S, 2 + s % 2, 0:FH], ACT.Silu), "silu_rdy")
                    if not first or s >= 1:
                        output(e - 1, q, s - 1, first)
                for s in range(4):
                    expert(s, 0, s, True)
                with act.Fori(1, NE // 4) as i:
                    for s in range(4):
                        expert(4 * i + s, i, s, False)
                act.wait_ge(s_["aT_mm"], NE)
                after(take_a(1), "aT_ev")
                output(NE - 1, NE // 4 - 1, 3, False)
                n_over = act.value_load(overi[0:1, 15:16], min_val=0, max_val=NOVER)
                act.wait_ge(s_["yst0"], 16 * NE // 2)
                with act.If(n_over > 0):
                    with act.Fori(0, n_over) as k:
                        act.wait_ge(s_["f_gu"], k + 1)
                        after(A(sg[:, 0, :], ps[0:S, 2, 0:FH], ACT.Silu), "f_silu")
                        act.wait_ge(s_["f_aT"], k + 1)
                        after(take_a(0), "f_aTev")
                        act.wait_ge(s_["f_dn"], k + 1)
                        after(A(ye[0][:, 0:512], ps[0:S, 0, :], ACT.Identity), "f_yact")
                        act.wait_ge(s_["f_yact"], k + 1)
                        act.wait_ge(s_["f_ydve"], k + 1)
                        after(act.dma_start(ys_dram[bass.ds(k * S + NE * S, S), :], ye[0]), "f_st", 16)
                        act.wait_ge(s_["f_st"], 16 * k + 16)
                        act.sem_inc(s_["f_end"], 1)
                after(act.drain(), "act_done")

        @block.vector
        def _(dve):
            V = nc.vector
            steps = [0]

            def link(ins):
                steps[0] += 1
                after(ins, "dve_step")
                dve.wait_ge(s_["dve_step"], steps[0])

            def copy_out(n, dst, src, scale=1.0):
                dve.wait_ge(s_["tr_dve"], n + 1)
                after(V.tensor_scalar(dst, src, scale, None, ALU.mult), "ev_dve")

            def mean(dst, src, width):
                return V.tensor_scalar(dst, src, 1.0 / width, EPS, ALU.mult, ALU.add)

            def norm_x(rounds, n):
                dve.wait_ge(s_["sum_rdy"], rounds)
                after(mean(ss[:, 0:NT], ss[:, 0:NT], D), "ms_rdy")
                dve.wait_ge(s_["rs_rdy"], rounds)
                for t in range(NT):
                    after(V.tensor_scalar(xoc[:, t, :], x[:, t, :], rs[:, t:t + 1], None, ALU.mult), "xn_rdy")

            def bc(ap, shape):
                return ap.broadcast_to(shape)

            V.memset(relx[BUCKETS:BUCKETS + 1, :], 1.0)
            V.memset(ones[:, :], 1.0)
            V.memset(neghalf[:, :], -0.5).then_inc(setup_dve, 1)
            for c in range(3):
                n = min(512, TN + TS - c * 512)
                dve.wait_ge(bias_mm, c + 1)
                V.tensor_scalar(sq[0:8, c * 512:c * 512 + n], ps[0:8, c, 0:n], -1.0, None, ALU.mult).then_inc(bias_neg, 1)
            dve.wait_ge(x_in, 16)
            dve.wait_ge(bias_map_in, 48)
            with dve.Fori(0, L) as l:
                steps[0] = 0
                enter(dve, l)
                norm_x(1, 0)
                dve.wait_ge(s_["params"], ALL_PARAMS)
                link(V.tensor_scalar(g64q[:, 0:1], g64[:, 0:1], -(HD ** -0.5), None, ALU.mult))
                link(V.tensor_scalar(g64q[:, 1:2], g64[:, 2:3], -(HD ** -0.5), None, ALU.mult))
                link(V.tensor_scalar(nsink[:, :], sink[:, :], -1.0, None, ALU.mult))
                for k in range(1, KC, 2):
                    copy_out(G_X[1] + k // 2, hTc[:, k, :], ps[:, 5, :], g_attn[:, k:k + 1])
                def head_groups(c):
                    for j in ABC_OF[c]:
                        if j % 2:
                            copy_out(G_ABC[1] + j // 2, heads[0:HD, abc[j][1], :], ps[0:HD, 5, :], abc[j][2])
                for c, (c0, n) in enumerate(CHUNKS):
                    for t in (1, 3):
                        dve.wait_ge(s_["pj_mm"], NT * c + t + 1)
                        if c0 == NKC:
                            V.tensor_copy(*by_head(t))
                            skip = 4 * HD
                        else:
                            skip = 0
                        after(V.tensor_copy(proj[:, t, c0 + skip:c0 + n], ps[:, t, skip:n]), "pj_ev_dve")
                    if c in NORMED:
                        col, nh, r0 = NORMED[c]
                        dve.wait_ge(s_["sum_rdy"], c)
                        sums = ss[:, r0:r0 + NT * nh]
                        ins = V.tensor_reduce(sums.rearrange("p (t h) -> p t h", t=NT), sqh[:, :, 0:nh * HD].rearrange("p t (h c) -> p t h c", c=HD), AX.X, ALU.add)
                        link(ins)
                        after(mean(sums, sums, HD), "ms_rdy")
                        V.memset(den2[:, :], 0.0).then_inc(s_["sq_used"], 1)
                    if c == 6:
                        dve.wait_ge(s_["sum_rdy"], R_LAT)
                        mean(ss[:, 56:60], ss[:, 56:60], QR)
                        after(mean(ss[:, 60:64], ss[:, 60:64], KVR), "ms_rdy")
                    if c:
                        head_groups(c - 1)
                    if c in NORMED:
                        dve.wait_ge(s_["rs_rdy"], c)
                        dve.wait_ge(s_["pj_ev_dve"], 2 * c + 2)
                        v = proj[:, :, col:col + nh * HD].rearrange("p t (h c) -> p t h c", c=HD)
                        r = rs[:, r0:r0 + NT * nh].rearrange("p (t h) -> p t h", t=NT).unsqueeze(3)
                        after(V.tensor_tensor(v, v, bc(r, [P, NT, nh, HD]), ALU.mult), "norms_rdy")
                dve.wait_ge(s_["rs_rdy"], R_LAT)
                for c0, n, r0 in ((MCQ, QR, 56), (MCKV, KVR, 60)):
                    v = proj[:, :, c0:c0 + n]
                    ins = V.tensor_tensor(v, v, bc(rs[:, r0:r0 + NT].unsqueeze(2), [P, NT, n]), ALU.mult)
                after(ins, "norms_rdy")
                dve.wait_ge(s_["ev_act"], G_ABC[0])
                for h in range(2):
                    dve.wait_ge(s_["tr_dve"], G_CMP[1] + h)
                    src = ps[:, 5, :].rearrange("p (b r) -> p b r", r=CMP_S)
                    for half in range(2):
                        dst = heads[:, SL_X + 2 * half + h, :].rearrange("p (b r) -> p b r", r=CMP_S)
                        pos = cposT[:, half * CMP_S:(half + 1) * CMP_S].unsqueeze(1)
                        ins = V.tensor_tensor(dst, src, bc(pos, [P, T // CMP_S, CMP_S]), ALU.add)
                    after(ins, "ev_dve")
                copy_out(G_LAT[1] + 2, heads[0:MQK, SL_L + 1, :], ps[0:MQK, 5, :], g_lq[:, 1:2])
                V.tensor_copy(dqk[1][:, :, :, NOPE:], bc(proj[:, :, MKPE:MKPE + ROPE].unsqueeze(2), [P, NT, 4, ROPE]))
                for t in range(NT):
                    dve.wait_ge(s_["up_mm"], t + 1)
                    kv = ps[:, 2 * (t % 2) + 1, :].rearrange("p (h c) -> p h c", h=4)
                    V.tensor_copy(vlat[:, t, :].rearrange("p (h c) -> p h c", h=4), kv[:, :, NOPE:])
                    after(V.tensor_copy(dqk[1][:, t, :, 0:NOPE], kv[:, :, 0:NOPE]), "up_ev_dve")
                for s in range(2):
                    link(V.memset(left[s][:, T:T + 1], 1.0))
                dve.wait_ge(bias_in, 128)

                def logits(u):
                    kind, h, i, n = units[u]
                    dve.wait_ge(s_["scores"], u + 1)
                    if u >= 3:
                        if units[u - 3][0] == "A":
                            dve.wait_ge(s_["sig"], u - 2)
                        else:
                            dve.wait_ge(s_["probs_sm"], u - 2 - NSB)
                    if kind == "A":
                        after(V.tensor_tensor(lgt[u % 3][:, 0:n], ps[:, u % 3, 0:n], bias_of(kind, h, i, n), ALU.add), "logits")
                        return
                    start = nsink[:, h:h + 1] if kind == "B" else 1e20
                    after(V.tensor_tensor_reduce(out=lgt[u % 3][:, 0:n], in0=ps[:, u % 3, 0:n], in1=bias_of(kind, h, i, n), scale=1.0,
                                                 scalar=start, op0=ALU.add, op1=ALU.min, accum_out=mrow[:, u:u + 1]), "logits")

                def stick(u):
                    kind, h, i, n = units[u]
                    dve.wait_ge(s_["sig"], u + 1)
                    link(V.tensor_tensor_scan(left[u % 2][:, T - n:T][:, ::-1], keep[u % 2][:, 0:n][:, ::-1], keep[u % 2][:, 0:n][:, ::-1], 1.0, ALU.mult, ALU.bypass))
                    after(V.tensor_tensor(prb[u % 2][:, 0:n], prb[u % 2][:, 0:n], left[u % 2][:, T - n + 1:T + 1], ALU.mult), "probs_sb")

                def head_out(g):
                    kind, h = units[g * NT][:2]
                    dve.wait_ge(s_["pv"], NT * g + NT)
                    grp = {"A": 0, "B": 1, "D": 3}.get(kind, 2)
                    src = ps[:, 5 + g % 2, 0:NT * HD].rearrange("p (t c) -> p t c", t=NT)
                    dst = xoc[:, :, grp * 256 + h * HD:grp * 256 + (h + 1) * HD]
                    if kind == "A":
                        after(V.tensor_copy(dst, src), "head_out")
                        return
                    d4 = den[:, NT * g:NT * g + NT]
                    if kind == "B":
                        dve.wait_ge(s_["esink_rdy"], h + 1)
                        link(V.tensor_tensor(d4, d4, esink[:, h * NT:(h + 1) * NT], ALU.add))
                    link(V.tensor_scalar(d4, d4, 1e-30, None, ALU.max))
                    link(V.reciprocal(den2[:, :], d4))
                    if grp == 2:
                        b = ("cmp", "slc", "win").index(kind)
                        link(V.tensor_tensor(den2[:, :], den2[:, :], gates[:, :, 4 * b + h], ALU.mult))
                    f = bc(den2[:, :].unsqueeze(2), [P, NT, HD])
                    if kind in ("slc", "win"):
                        link(V.tensor_tensor(otmp[:, :, :], src, f, ALU.mult))
                        after(V.tensor_tensor(dst, dst, otmp[:, :, :], ALU.add), "head_out")
                        dve.wait_ge(s_["head_out"], g + 1)
                    else:
                        after(V.tensor_tensor(dst, src, f, ALU.mult), "head_out")
                        dve.wait_ge(s_["head_out"], g + 1)
                for u in range(-2, NU + 1):
                    if u + 2 < NU:
                        logits(u + 2)
                    if 0 <= u + 1 < NSB:
                        stick(u + 1)
                    if u >= 1 and u % NT == 0:
                        head_out(u // NT - 1)
                    if u == U_NORMC:
                        dve.wait_ge(s_["cmp_out"], 1)
                        V.tensor_copy(vcmp[:, :, :], ps[0:NCMP, 7, 2 * HD:4 * HD].rearrange("p (h c) -> p h c", h=2))
                        link(V.tensor_copy(kcmp[:, :, :], ps[0:NCMP, 7, 0:2 * HD].rearrange("p (h c) -> p h c", h=2)))
                        link(V.tensor_tensor(csq[:, :, :], kcmp[:, :, :], kcmp[:, :, :], ALU.mult))
                        link(V.tensor_reduce(css[:, 0:2], csq[:, :, :], AX.X, ALU.add))
                        after(mean(css[:, 0:2], css[:, 0:2], HD), "ms_rdy")
                    if u == U_NORMC + 4:
                        dve.wait_ge(s_["rs_rdy"], R_CMP)
                        after(V.tensor_tensor(kcmp[:, :, :], kcmp[:, :, :], bc(css[:, 2:4].unsqueeze(2), [NCMP, 2, HD]), ALU.mult), "cmp_n")
                    if u == U_CMPT:
                        dve.wait_ge(s_["cmpT_mm"], 1)
                        after(V.tensor_scalar(kcmpT[:, :, 0:NCMP], ps[0:HD, 7, 0:64].rearrange("p (h n) -> p h n", h=2)[:, :, 0:NCMP], g64[:, 3:4], None, ALU.mult), "cmpT_ev")
                    if u == U_SUMD + 9:
                        dve.wait_ge(s_["sum_rdy"], 7)
                        after(mean(ss[:, 0:32], ss[:, 0:32], MQK), "ms_rdy")
                dve.wait_ge(s_["sum_rdy"], 8)
                after(mean(ss[:, 0:16], ss[:, 0:16], 256), "ms_rdy")
                dve.wait_ge(s_["rs_rdy"], R_O)
                og = xo[:, :].rearrange("p (g c) -> p g c", c=256)
                after(V.tensor_tensor(og, og, bc(rs[:, 0:16].unsqueeze(2), [P, 16, 256]), ALU.mult), "o_rdy")
                for k in range(1, KC, 2):
                    copy_out(G_O[1] + k // 2, hTc[:, k, :], ps[:, 5, :], g_out[:, k:k + 1])
                for j in range(2 * NT):
                    dve.wait_ge(s_["wo_mm"], j + 1)
                    xs = x[:, j // 2, j % 2 * 512:(j % 2 + 1) * 512]
                    after(V.tensor_tensor(xs, xs, ps[:, j % 4, :], ALU.add), "wo_ev")
                dve.wait_ge(s_["sum_rdy"], 9)
                after(mean(ss[:, 0:NT], ss[:, 0:NT], D), "ms_rdy")
                dve.wait_ge(s_["rs_rdy"], R_X2)
                for t in range(NT):
                    after(V.tensor_scalar(xoc[:, t, :], x[:, t, :], rs[:, t:t + 1], None, ALU.mult), "xn_rdy")
                for k in range(1, KC, 2):
                    copy_out(G_H[1] + k // 2, hTc[:, k, :], ps[:, 5, :], g_ffn[:, k:k + 1])
                TE = [P, NT, NE]
                dve.wait_ge(s_["lg_mm"], 1)
                link(V.tensor_tensor(lg[:, :, :], ps[:, 0, 0:NT * 36].rearrange("p (t n) -> p t n", t=NT), bc(rbias[:, :].unsqueeze(1), [P, NT, 36]), ALU.add))
                gl, el = lg[:, :, 0:NGRP], lg[:, :, NGRP:]

                def r(i):
                    return rsm[:, i, :]

                def b3(ap, n):
                    return bc(ap.unsqueeze(2), [P, NT, n])

                def c3(c, n):
                    return bc(con[:, c:c + n].unsqueeze(1), [P, NT, n])

                def first_best(dst, src, best, at, n):
                    link(V.tensor_reduce(best, src, AX.X, ALU.max))
                    link(V.tensor_tensor(dst, src, b3(best, n), ALU.is_equal))
                    link(V.scalar_tensor_tensor(dst, dst, -1000.0, c3(C_E, n), ALU.mult, ALU.add))
                    link(V.tensor_reduce(at, dst, AX.X, ALU.min))
                    link(V.tensor_tensor(dst, c3(C_IM, n), b3(at, n), ALU.is_equal))
                first_best(goh[:, :, :], gl, r(0), r(1), NGRP)
                after(V.tensor_tensor(gex[:, :, :], gl, b3(r(0), NGRP), ALU.subtract), "rt_in")
                link(V.tensor_scalar(goh[:, :, :], goh[:, :, :], BIG, -BIG, ALU.mult, ALU.add))
                em, oh1, em2, oh2, both, slot, ovf, pick = [rt[:, i] for i in (0, 1, 2, 3, 9, 4, 5, 6)]
                link(V.tensor_tensor(em.rearrange("p t (g e) -> p t g e", g=NGRP), el.rearrange("p t (g e) -> p t g e", g=NGRP),
                                     bc(goh[:, :, :].unsqueeze(3), [P, NT, NGRP, EPG]), ALU.add))
                first_best(oh1, em, r(2), r(3), NE)
                link(V.scalar_tensor_tensor(em2, oh1, -2 * BIG, em, ALU.mult, ALU.add))
                first_best(oh2, em2, r(4), r(5), NE)
                after(V.tensor_tensor(both, oh1, oh2, ALU.add), "assign")
                after(V.tensor_tensor(r(6), r(4), r(2), ALU.subtract), "rt_in")
                dve.wait_ge(s_["rt_exp"], 2)
                V.tensor_scalar(r(7), r(6), 1.0, None, ALU.add)
                link(V.tensor_reduce(r(8), gex[:, :, :], AX.X, ALU.add))
                link(V.tensor_tensor(r(7), r(7), r(8), ALU.mult))
                link(V.reciprocal(r(9), r(7)))
                link(V.tensor_tensor(r(10), r(9), r(6), ALU.mult))
                dve.wait_ge(s_["pos_mm"], 1)
                w = [row[:, i, :] for i in range(6)]
                link(V.tensor_scalar(w[0], ps[:, 2, 0:NE], float(S - 1), None, ALU.add))
                link(V.tensor_copy(rowi[:, :], w[0]))
                link(V.tensor_scalar(rowi[:, :], rowi[:, :], 6, None, ALU.arith_shift_right))
                link(V.tensor_copy(w[1], rowi[:, :]))
                link(V.tensor_scalar(w[1], w[1], -1.0, 0.0, ALU.add, ALU.max))
                link(V.tensor_tensor_scan(w[2], w[1], w[1], 0.0, ALU.add, ALU.bypass))
                link(V.tensor_tensor(w[3], w[2], w[1], ALU.subtract))
                link(V.tensor_scalar(w[4], w[3], float(S), float(S * (NE - 1)), ALU.mult, ALU.add))
                link(V.tensor_tensor(w[4], w[4], con[:, C_E64:C_E64 + NE], ALU.subtract))
                pos = ps[:, 1, 0:NT * NE].rearrange("p (t e) -> p t e", t=NT)
                link(V.tensor_tensor(slot, pos, c3(C_E64, NE), ALU.add))
                link(V.tensor_scalar(ovf, pos, float(S), None, ALU.is_ge))
                link(V.tensor_tensor(ovf, ovf, bc(w[4].unsqueeze(1), TE), ALU.mult))
                link(V.tensor_tensor(slot, slot, ovf, ALU.add))
                for j, oh in enumerate((oh1, oh2)):
                    link(V.tensor_tensor(pick, oh, slot, ALU.mult))
                    link(V.tensor_reduce(slotf[:, j, :], pick, AX.X, ALU.add))
                link(V.tensor_copy(sloti[:, :, :], slotf[:, :, :]))
                TK = [1, 16, NE]
                kk = bc(con[0:1, C_K:C_K + 16].unsqueeze(2), TK)
                link(V.tensor_tensor(over[:, 0], kk, bc(w[3][0:1].unsqueeze(1), TK), ALU.is_ge))
                link(V.tensor_tensor(over[:, 1], kk, bc(w[2][0:1].unsqueeze(1), TK), ALU.is_lt))
                link(V.tensor_tensor(over[:, 0], over[:, 0], over[:, 1], ALU.mult))
                link(V.tensor_tensor(over[:, 0], over[:, 0], bc(con[0:1, C_E:C_E + NE].unsqueeze(1), TK), ALU.mult))
                link(V.tensor_reduce(overf[:, :], over[:, 0], AX.X, ALU.add))
                link(V.tensor_copy(overf[:, 15:16], w[2][0:1, NE - 1:NE]))
                after(V.tensor_copy(overi[:, :], overf[:, :]), "slots_rdy")

                def take_x(s):
                    return V.tensor_tensor(xeT[s], ps[:, 4 + s, :].rearrange("p (k s) -> p k s", k=KC),
                                           bc(g_ffn[:, :].unsqueeze(2), [P, KC, S]), ALU.mult)

                def gate(s):
                    return V.tensor_tensor(sg[:, s, :], sg[:, s, :], ps[0:S, 2 + s, FH:2 * FH], ALU.mult)

                def output(e, q, s, first):
                    b = s % 2
                    if not first or s >= 2:
                        dve.wait_ge(s_[f"yst{b}"], 32 * q + 16 * (s // 2))
                    dve.wait_ge(s_["dn_mm"], e + 1)
                    after(V.tensor_copy(ye[b][:, 512:D], ps[0:S, (1, 7)[b], :]), "y_dve")

                def expert(e, q, s, first):
                    dve.wait_ge(s_["xeT_mm"], e + 2)
                    after(take_x(1 - s % 2), "xeT_ev")
                    dve.wait_ge(s_["silu_rdy"], e + 1)
                    after(gate(s % 2), "a_rdy")
                    if not first or s >= 1:
                        output(e - 1, q, s - 1, first)
                dve.wait_ge(s_["xeT_mm"], 1)
                after(take_x(0), "xeT_ev")
                for s in range(4):
                    expert(s, 0, s, True)
                with dve.Fori(1, NE // 4) as i:
                    for s in range(4):
                        expert(4 * i + s, i, s, False)
                output(NE - 1, NE // 4 - 1, 3, False)
                n_over = dve.value_load(overi[0:1, 15:16], min_val=0, max_val=NOVER)
                dve.wait_ge(s_["yst0"], 16 * NE // 2)
                with dve.If(n_over > 0):
                    with dve.Fori(0, n_over) as k:
                        dve.wait_ge(s_["f_T"], k + 1)
                        after(take_x(0), "f_Tev")
                        dve.wait_ge(s_["f_silu"], k + 1)
                        after(gate(0), "f_a")
                        dve.wait_ge(s_["f_dn"], k + 1)
                        after(V.tensor_copy(ye[0][:, 512:D], ps[0:S, 1, :]), "f_ydve")
                        dve.wait_ge(s_["f_end"], k + 1)
                for t in range(NT):
                    for j in range(2):
                        c = 2 * t + j
                        dve.wait_ge(gath, 16 * 2 * NT * l + 16 * 2 * NT)
                        after(V.scalar_tensor_tensor(x[:, t, :], yg[c], rsm[:, 9 + j, t:t + 1], x[:, t, :], ALU.mult, ALU.add), "comb")
                        dve.wait_ge(s_["comb"], c + 1)
                after(dve.drain(), "dve_done")

        @block.gpsimd
        def _(pool):
            G = nc.gpsimd

            def rsqrt(n, dst, src, rows, cols):
                pool.wait_ge(s_["ms_rdy"], n)
                after(G.tensor_tensor(dst, src, neghalf[0:rows, 0:cols], ALU.pow), "rs_rdy")
            G.memset(zero[:, :], 0.0).then_inc(zeros_rdy, 1)
            pool.wait_ge(setup_dve, 1)
            pool.sem_inc(layer_open, 1)
            pool.wait_ge(bias_neg, 3)
            W = TN + TS
            for h in range(4):
                pool.dma_start(bias_rows[h:h + 1, :, 0:TN], sq[4 + h:5 + h, 0:TN].unsqueeze(1).broadcast_to([1, P, TN])).then_inc(bias_out, 16)
                pool.dma_start(bias_rows[h:h + 1, :, TN:], sq[h:h + 1, TN:TN + TS].unsqueeze(1).broadcast_to([1, P, TS])).then_inc(bias_out, 16)
            pool.wait_ge(bias_out, 128)
            for h in range(4):
                pool.dma_start(gn[:, h, :], bass.AP(bias_rows.tensor, h * P * W + P - 1, [[W - 1, P], [1, UN]])).then_inc(bias_in, 16)
                pool.dma_start(gs[:, h, :], bass.AP(bias_rows.tensor, h * P * W + TN + P - 1, [[W - 1, P], [1, US]])).then_inc(bias_in, 16)
            pool.wait_ge(zeros_rdy, 1)

            def clear(rows, n):
                pool.dma_start(rows.rearrange("(p r) (c w) -> p (r c) w", p=P, w=256), zero[:, :].unsqueeze(1).broadcast_to([P, 4 * n, 256])).then_inc(zeroed, 16)
            parts = [xs_dram[i:min(i + 4 * P, NSLOT // P * P), :] for i in range(0, NSLOT // P * P, 4 * P)]
            parts += [ys_dram[i:min(i + 4 * P, NSLOT // P * P), :] for i in range(NE * S, NSLOT // P * P, 4 * P)]
            for rows in parts:
                clear(rows, rows.shape[0] // P)
            for rows in (xs_dram, ys_dram):
                if NSLOT % P:
                    pool.dma_start(rows[NSLOT // P * P:, :].rearrange("p (c w) -> p c w", w=256), zero[0:NSLOT % P, :].unsqueeze(1).broadcast_to([NSLOT % P, 4, 256])).then_inc(zeroed, 16)
            n_zero = len(parts) + 2 * bool(NSLOT % P)
            with pool.Fori(0, L) as l:
                rsqrt(1, rs[:, 0:NT], ss[:, 0:NT], P, NT)
                for c, (_, nh, r0) in NORMED.items():
                    rsqrt(c, rs[:, r0:r0 + NT * nh], ss[:, r0:r0 + NT * nh], P, NT * nh)
                rsqrt(R_LAT, rs[:, 56:64], ss[:, 56:64], P, 8)
                rsqrt(R_CMP, css[:, 2:4], css[:, 0:2], NCMP, 2)
                rsqrt(R_D, rs[:, 0:32], ss[:, 0:32], P, 32)
                pool.wait_ge(s_["rs_rdy"], R_D)
                step = 0

                def link(ins):
                    after(ins, "rope_step")
                    pool.wait_ge(s_["rope_step"], step + 1)
                rsd = rs[:, 0:32].rearrange("p (t h) -> p t h", t=NT)
                for j in range(2):
                    v = dqk[j]
                    link(G.tensor_tensor(v, v, rsd[:, :, 4 * j:4 * j + 4].unsqueeze(3).broadcast_to([P, NT, 4, MQK]), ALU.mult))
                    step += 1
                    link(G.tensor_tensor(v, v, g_qk[:, j, :].unsqueeze(1).unsqueeze(1).broadcast_to([P, NT, 4, MQK]), ALU.mult))
                    step += 1
                    x1, x2 = v[:, :, :, NOPE:NOPE + HALF], v[:, :, :, NOPE + HALF:]
                    cos, sin = [con[:, c:c + 64].rearrange("p (t f) -> p t f", t=NT).unsqueeze(2).broadcast_to([P, NT, 4, HALF]) for c in (C_COS, C_SIN)]
                    G.tensor_tensor(dtm[0], x1, cos, ALU.mult)
                    G.tensor_tensor(dtm[1], x2, sin, ALU.mult)
                    G.tensor_tensor(dtm[2], x1, sin, ALU.mult)
                    link(G.tensor_tensor(dtm[3], x2, cos, ALU.mult))
                    step += 1
                    G.tensor_tensor(x1, dtm[0], dtm[1], ALU.subtract)
                    ins = G.tensor_tensor(x2, dtm[2], dtm[3], ALU.add)
                    if j == 0:
                        link(ins)
                        step += 1
                after(ins, "dqk_rdy")
                rsqrt(R_O, rs[:, 0:16], ss[:, 0:16], P, 16)
                rsqrt(R_X2, rs[:, 0:NT], ss[:, 0:NT], P, NT)
                pool.wait_ge(zeroed, 16 * n_zero)
                pool.wait_ge(s_["slots_rdy"], 1)
                for t in range(NT):
                    for j in range(2):
                        pool.indirect_dma_start(xs_dram, bass.IndirectOffsetOnAxis(ap=sloti[:, j, t:t + 1], axis=0), xoc[:, t, :], None).then_inc(scat, 16)
                for s in range(2):
                    pool.wait_ge(s_[f"yst{s}"], 16 * NE // 2)
                n_over = pool.value_load(overi[0:1, 15:16], min_val=0, max_val=NOVER)
                with pool.If(n_over > 0):
                    pool.wait_ge(s_["f_end"], n_over)
                for t in range(NT):
                    for j in range(2):
                        pool.indirect_dma_start(yg[2 * t + j], None, ys_dram, bass.IndirectOffsetOnAxis(ap=sloti[:, j, t:t + 1], axis=0)).then_inc(gath, 16)
                pool.wait_ge(s_["comb"], 2 * NT)
                for n in per_layer[:4]:
                    pool.wait_ge(s_[n], 1)
                for n in per_layer[4:] + per_layer[:4]:
                    pool.sem_clear(s_[n])
                pool.sem_inc(layer_open, 1)
    return nc


_INS = ["x", "rel_bias", "attn_norm", "w_in", "swa_q_norm", "swa_k_norm", "swa_sinks", "nsa_q_norm", "nsa_k_norm",
        "nsa_cmp_pos", "nsa_cmp_w1", "nsa_cmp_w2", "mla_q_lat_norm", "mla_w_q_up", "mla_kv_lat_norm", "mla_w_kv_up",
        "mla_q_norm", "mla_k_norm", "out_norm", "w_out", "ffn_norm", "moe_w_group", "moe_b_group", "moe_w_expert",
        "moe_b_expert", "moe_w_gate", "moe_w_up", "moe_w_down"]


def kernel(**inputs):
    import concourse.bacc as _bacc
    from concourse.bass_utils import run_bass_kernel_spmd as _run

    nc = _bacc.Bacc("TRN2", target_bir_lowering=False, num_devices=1)
    arrays, args = {}, {}

    def put(name, v):
        v = np.ascontiguousarray(v)
        arrays["in_" + name] = v
        return nc.dram_tensor("in_" + name, v.shape, mybir.dt.from_np(v.dtype), kind="ExternalInput").ap()
    for name in _INS:
        args[name] = put(name, inputs[name])
    c, m = constants()
    out = nc.dram_tensor("out_0", (1, T, D), F32, kind="ExternalOutput").ap()
    rows = nc.dram_tensor("bias_rows", (4, P, TN + TS), F32, kind="Internal").ap()
    xs = nc.dram_tensor("expert_in", (NSLOT, D), F32, kind="Internal").ap()
    ys = nc.dram_tensor("expert_out", (NSLOT, D), F32, kind="Internal").ap()
    build(nc, args, put("consts", c), put("bias_map", m), out, rows, xs, ys)
    r = _run(nc, [arrays], core_ids=[0])
    return r.results[0]["out_0"]
```

```python
import math
from contextlib import ExitStack

import numpy as np

import concourse.bass as bass
from concourse import mybir

ALU = mybir.AluOpType
ACT = mybir.ActivationFunctionType
AX = mybir.AxisListType
F32 = mybir.dt.float32
I32 = mybir.dt.int32
U32 = mybir.dt.uint32

P = 128
T = 512
NT = T // P
D = 1024
KC = D // P
L = 2
HD = 64
EPS = 1e-6
BIG = 1e30

SBQ, SBK, SBV = 0, 256, 512
SWQ, SWK, SWV = 768, 1024, 1152
NQ, NKC, NVC, NKS, NVS, NKW, NVW, NG = 1280, 1536, 1664, 1792, 1920, 2048, 2176, 2304
MCQ, MCKV, MKPE, COLS = 2316, 2508, 2636, 2668
WCH = 384
CHUNKS = [(c, min(WCH, COLS - c)) for c in range(0, COLS, WCH)]

QR, KVR, NOPE, ROPE = 192, 128, 64, 32
MQK = NOPE + ROPE
HALF = ROPE // 2
CMP_L, CMP_S, CMP_H = 32, 16, 128
NCMP = T // CMP_S - 1
NWIN = 2 * NCMP + 1
BUCKETS = 32

NGRP, EPG, NE = 4, 8, 32
NR = NGRP + NE
FH = 256
S = 64
NOVER = 2 * T // S - 1
NTILE = NE + NOVER
NSLOT = NTILE * S

UN = 896
TN = UN + P - 1
US = 256
TS = US + P - 1

C_ID, C_TRI, C_CM, C_SM, C_COS, C_SIN, C_IM, C_E64, C_E, C_K = np.cumsum([0, P, P, T, T, 64, 64, NE, NE, NE]).tolist()
NCON = C_K + 16

SL_A, SL_B, SL_C, SL_D, SL_X = 0, 8, 14, 22, 30
SL_L = 27
NSL = 34


def t5_bucket(n):
    n = np.maximum(n, 0)
    half = BUCKETS // 2
    nf = np.maximum(n, 1).astype(np.float32)
    large = half + (np.log(nf / np.float32(half)) / np.float32(math.log(1024 / half)) * np.float32(BUCKETS - half)).astype(np.int32)
    return np.where(n < half, n, np.minimum(large, BUCKETS - 1))


def constants():
    c = np.zeros((P, NCON), np.float32)
    p = np.arange(P)[:, None]
    c[:, C_ID:C_ID + P] = np.eye(P)
    c[:, C_TRI:C_TRI + P] = p < np.arange(P)[None]
    dist = p + 384 - np.arange(T)[None]
    c[:, C_CM:C_CM + T] = np.where(dist >= 0, 0, BIG)
    c[:, C_SM:C_SM + T] = np.where(dist > 0, 0, -BIG)
    inv = (np.float32(10000.0) ** (-np.arange(0, ROPE, 2, dtype=np.float32) / np.float32(ROPE))).astype(np.float32)
    ang = (np.arange(T, dtype=np.float32)[:, None] * inv[None]).astype(np.float32).reshape(NT, P, HALF)
    c[:, C_COS:C_COS + 64] = np.cos(ang).transpose(1, 0, 2).reshape(P, 64)
    c[:, C_SIN:C_SIN + 64] = np.sin(ang).transpose(1, 0, 2).reshape(P, 64)
    c[:, C_IM:C_IM + NE] = np.arange(NE) - 1000
    c[:, C_E64:C_E64 + NE] = np.arange(NE) * S
    c[:, C_E:C_E + NE] = np.arange(NE)
    c[:, C_K:C_K + 16] = np.arange(16)
    m = np.zeros((BUCKETS + 1, TN + TS), np.float32)
    dn = T - 1 - np.arange(TN)
    ds = US - 1 - np.arange(TS)
    m[t5_bucket(dn), np.arange(TN)] = 1
    m[t5_bucket(ds), TN + np.arange(TS)] = 1
    m[BUCKETS, :TN] = np.where(dn >= 0, 0, -BIG)
    m[BUCKETS, TN:] = np.where((ds >= 0) & (ds < P), 0, -BIG)
    return c, m


def build(nc, a, consts, bias_map, out, bias_rows, xs_dram, ys_dram):
    with ExitStack() as ctx:
        def sb(name, shape, dt=F32):
            return ctx.enter_context(nc.sbuf_tensor(name, shape, dt))

        def sem(name):
            return ctx.enter_context(nc.semaphore(name))

        con = sb("con", [P, NCON])
        ones = sb("ones", [P, P])
        neghalf = sb("neghalf", [P, 64])
        x = sb("x", [P, NT, D])
        xo = sb("xo", [P, NT * D])
        hT = sb("hT", [P, NT * D])
        big = sb("big", [P, NT * COLS + NSL * T])
        sq = sb("sq", [P, 3584])
        gn = sb("gn", [P, 4, UN])
        gs = sb("gs", [P, 4, US])
        relx = sb("relx", [BUCKETS + 1, 8])
        g_attn, g_out, g_ffn = sb("g_attn", [P, KC]), sb("g_out", [P, KC]), sb("g_ffn", [P, KC])
        g64 = sb("g64", [HD, 6])
        g_lq, g_lkv, g_qk = sb("g_lq", [MQK, 2]), sb("g_lkv", [KVR, 1]), sb("g_qk", [P, 2, MQK])
        sink, nsink = sb("sink", [P, 4]), sb("nsink", [P, 4])
        cpos, cposT = sb("cpos", [CMP_L, P]), sb("cposT", [P, CMP_L])
        zero = sb("zero", [P, 256])
        w_cmp2 = sb("w_cmp2", [P, 2, HD])
        rbias, w_rt = sb("rbias", [P, 36]), sb("w_rt", [P, KC, 36])
        ss, rs = sb("ss", [P, 64]), sb("rs", [P, 64])
        gates = sb("gates", [P, NT, 12])
        hcmp = sb("hcmp", [P, 2, 2, 32])
        kcmp, vcmp = sb("kcmp", [NCMP, 2, HD]), sb("vcmp", [NCMP, 2, HD])
        kcmpT = sb("kcmpT", [HD, 2, 32])
        csq, css = sb("csq", [NCMP, 2, HD]), sb("css", [NCMP, 4])
        mrow, den = sb("mrow", [P, 96]), sb("den", [P, 96])
        den2, esink = sb("den2", [P, 4]), sb("esink", [P, 4 * NT])
        g64q = sb("g64q", [HD, 2])
        otmp = sb("otmp", [P, NT, HD])
        lg = sb("lg", [P, NT, 36])
        rsm = sb("rsm", [P, 12, NT])
        goh, gex = sb("goh", [P, NT, NGRP]), sb("gex", [P, NT, NGRP])
        row, rowi = sb("row", [P, 6, NE]), sb("rowi", [P, NE], I32)
        slotf, sloti = sb("slotf", [P, 2, NT]), sb("sloti", [P, 2, NT], U32)
        overi = sb("overi", [1, 16], I32)
        overf = sb("overf", [1, 16])
        LROWS = [slice(64 * i, 64 * i + NR) for i in range(2)]
        rt = sq[:, 1024:1024 + 10 * NT * NE].rearrange("p (a t e) -> p a t e", a=10, t=NT)
        over = sq[0:1, 0:2 * 16 * NE].rearrange("p (a k e) -> p a k e", a=2, k=16)
        sg = hT[:, 3072:3072 + FH].rearrange("p (i f) -> p i f", i=2)
        aT = hT[:, 3072 + FH:3072 + FH + 4 * S].rearrange("p (i c s) -> p i c s", i=2, c=2)

        ps = ctx.enter_context(nc.psum_tensor("ps", [P, 8, 512], F32))

        ident = con[:, C_ID:C_ID + P]
        hTc = hT[:, :].rearrange("p (k t) -> p k t", k=KC)
        xoc = xo[:, :].rearrange("p (t d) -> p t d", t=NT)
        proj = big[:, 0:NT * COLS].rearrange("p (t c) -> p t c", t=NT)
        heads = big[:, NT * COLS:].rearrange("p (s t) -> p s t", s=NSL)
        base = NT * COLS
        win = [big[:, base + SL_D * T + i * KC * WCH:base + SL_D * T + (i + 1) * KC * WCH].rearrange("p (k n) -> p k n", k=KC) for i in range(2)]
        bmap = big[0:BUCKETS + 1, base + 16 * T:base + 19 * T]
        w_qup = sq[0:MQK, 1536:1536 + 2 * 384].rearrange("p (c n) -> p c n", c=2)
        w_kvup = sq[:, 2304:2304 + 512]
        vlat = sq[:, 0:NT * 256].rearrange("p (t c) -> p t c", t=NT)
        w1 = xo[:, :].rearrange("p (l f) -> p l f", l=CMP_L)
        EW = 3 * KC * FH
        w_o = big[:, EW:EW + KC * D].rearrange("p (k n) -> p k n", k=KC)
        ring_g, ring_u, ring_d, ring_gu = [], [], [], []
        for b in (0, EW + KC * D, 2 * EW + KC * D, EW):
            ring_g.append(big[:, b:b + KC * FH].rearrange("p (k f) -> p k f", k=KC))
            ring_gu.append(big[:, b:b + 2 * KC * FH].rearrange("p (g k f) -> p g k f", g=2, k=KC))
            ring_u.append(big[:, b + KC * FH:b + 2 * KC * FH].rearrange("p (k f) -> p k f", k=KC))
            ring_d.append(big[:, b + 2 * KC * FH:b + EW].rearrange("p (c n) -> p c n", c=2))
        yg = [big[:, i * D:(i + 1) * D] for i in range(8)]
        sqh = sq[:, 0:NT * WCH].rearrange("p (t c) -> p t c", t=NT)
        dqk = [proj[:, :, c:c + 4 * MQK].rearrange("p t (h c) -> p t h c", h=4) for c in (0, 2 * WCH)]
        dtm = [b.rearrange("p (t h c) -> p t h c", t=NT, h=4) for b in
               (big[:, base + (SL_D + 5) * T:base + (SL_D + 5) * T + 256], big[:, base + (SL_D + 5) * T + 256:base + (SL_D + 6) * T],
                big[:, base + (SL_D + 6) * T:base + (SL_D + 6) * T + 256], big[:, base + (SL_D + 6) * T + 256:base + (SL_D + 7) * T])]
        dsq = [big[:, base + SL_L * T + j * 4 * NT * MQK:base + SL_L * T + (j + 1) * 4 * NT * MQK].rearrange("p (t h c) -> p t h c", t=NT, h=4) for j in range(2)]
        lgt = [hT[:, i * T:(i + 1) * T] for i in range(3)]
        prb = [hT[:, (3 + i) * T:(4 + i) * T] for i in range(2)]
        prT = [hT[:, (5 + i) * T:(6 + i) * T] for i in range(2)]
        WROWS = [slice(c * HD, c * HD + NWIN) for c in range(2)]
        hidden = [hT[WROWS[c], 7 * T:7 * T + CMP_H] for c in range(2)]
        oT = [hT[0:HD, 7 * T:8 * T], heads[0:HD, SL_X + 3, :]]
        keep = [heads[:, SL_D + i, :] for i in range(2)]
        left = [big[:, base + (SL_D + 2) * T + i * 520:base + (SL_D + 2) * T + i * 520 + T + 1] for i in range(2)]
        xe = [hT[0:S, i * D:(i + 1) * D] for i in range(2)]
        xeT = [hT[:, 2048 + i * T:2048 + (i + 1) * T].rearrange("p (k s) -> p k s", k=KC) for i in range(2)]
        ye = [sq[:, i * 512:(i + 1) * 512] for i in range(2)]

        kept = ("params_pre win0_pre win1_pre bias_map_in x_sums setup_dve bias_mm bias_neg bias_out bias_in zeros_rdy zeroed layer_open entered "
                "scat out_done").split()
        x_in = [sem(f"x_in{i}") for i in range(NT)]
        gath = [sem(f"gath{i}") for i in range(2 * NT)]
        (params_pre, win0_pre, win1_pre, bias_map_in, x_sums, setup_dve, bias_mm, bias_neg, bias_out, bias_in, zeros_rdy, zeroed, layer_open, entered,
         scat, out_done) = [sem(n) for n in kept]
        per_layer = ("sp_done pe_done act_done dve_done params params_late win_0 win_1 win_a win_b og_rdy sum_x2 w1_in wout_in dve_step sum_rdy ms_rdy rs_rdy xn_rdy "
                     "tr_act tr_dve ev_act ev_dve pj_mm pj_ev_act pj_ev_dve norms_rdy up_mm up_ev_act up_ev_dve "
                     "cmp_mm cmp_ev cmph_mm cmph_ev cmp_out cmp_n cmpT_mm cmpT_ev rope_step dqk_rdy dsq_rdy lat_T lat_ev sq_used scores logits probs_sm sig probs_sb "
                     "probT probT_ev pv oT_rdy oT_mm head_out esink_rdy o_rdy wo_mm wo_ev lgT_mm lgT_ev lg_mm rt_in rt_exp assign pos_mm slots_rdy over_rdy "
                     "wg0 wg1 wg2 wg3 wu0 wu1 wu2 wu3 wd0 wd1 wd2 wd3 xe0 xe1 xeT_mm xeT_ev gu_mm silu_rdy a_rdy aT_mm aT_ev dn_mm y_dve "
                     "yst0 yst1 f_in f_step f_loop f_T f_Tev f_gu f_silu f_a f_aT f_aTev f_dn f_ydve f_st f_end comb").split()
        s_ = {n: sem(n) for n in per_layer}

        def after(ins, s, n=1):
            return ins.then_inc(s_[s], n)

        block = ctx.enter_context(nc.Block())

        def enter(eng, l):
            eng.wait_ge(layer_open, l + 1)
            eng.sem_inc(entered, 1)

        def params(l):
            def of(name):
                return a[name][bass.ds(l, 1)]
            return [
                (g_attn[:, :], of("attn_norm").rearrange("o (p k) -> p (o k)", k=KC)),
                (g_out[:, :], of("out_norm").rearrange("o (p k) -> p (o k)", k=KC)),
                (g64[:, 0:1], of("swa_q_norm").rearrange("o p -> p o")),
                (g64[:, 1:2], of("swa_k_norm").rearrange("o p -> p o")),
                (g64[:, 2:3], of("nsa_q_norm").rearrange("o p -> p o")),
                (g64[:, 3:4], of("nsa_k_norm")[:, 0].rearrange("o p -> p o")),
                (g64[:, 4:5], of("nsa_k_norm")[:, 1].rearrange("o p -> p o")),
                (g64[:, 5:6], of("nsa_k_norm")[:, 2].rearrange("o p -> p o")),
                (g_lq[:, :], of("mla_q_lat_norm").rearrange("o (p k) -> p (o k)", k=2)),
                (g_lkv[:, :], of("mla_kv_lat_norm").rearrange("o p -> p o")),
                (g_qk[:, 0, :], of("mla_q_norm").broadcast_to([P, MQK])),
                (g_qk[:, 1, :], of("mla_k_norm").broadcast_to([P, MQK])),
                (sink[:, :], of("swa_sinks").broadcast_to([P, 4])),
                (cpos[:, 0:HD], of("nsa_cmp_pos")[:, 0].rearrange("o l d -> (o l) d")),
                (cpos[:, HD:], of("nsa_cmp_pos")[:, 1].rearrange("o l d -> (o l) d")),
                (w_cmp2[:, :, :], of("nsa_cmp_w2").rearrange("o c f d -> f (o c) d")),
                (rbias[:, 0:NGRP], of("moe_b_group").broadcast_to([P, NGRP])),
                (rbias[:, NGRP:], of("moe_b_expert").broadcast_to([P, NE])),
                (w_rt[:, :, 0:NGRP], of("moe_w_group").rearrange("o (p k) n -> p (o k) n", k=KC)),
                (w_rt[:, :, NGRP:], of("moe_w_expert").rearrange("o (p k) n -> p (o k) n", k=KC)),
            ]

        def late_params(l):
            def of(name):
                return a[name][bass.ds(l, 1)]
            return [
                (g_ffn[:, :], of("ffn_norm").rearrange("o (p k) -> p (o k)", k=KC)),
                (w_qup, of("mla_w_q_up").rearrange("o (p c) n -> p (o c) n", c=2)),
                (w_kvup, of("mla_w_kv_up").rearrange("o p n -> p (o n)")),
            ]
        ALL_PARAMS = 16 * len(params(0))
        LATE_PARAMS = 16 * len(late_params(0))

        abc = ([(SBQ + h * HD, SL_A + h, 1.0) for h in range(4)] + [(SBK + h * HD, SL_A + 4 + h, 1.0) for h in range(4)]
               + [(SWQ + h * HD, SL_B + h, g64q[:, 0:1]) for h in range(4)] + [(SWK + h * HD, SL_B + 4 + h, g64[:, 1:2]) for h in range(2)]
               + [(NQ + h * HD, SL_C + h, g64q[:, 1:2]) for h in range(4)] + [(NKS + h * HD, SL_C + 4 + h, g64[:, 4:5]) for h in range(2)]
               + [(NKW + h * HD, SL_C + 6 + h, g64[:, 5:6]) for h in range(2)])
        def by_group(ap):
            return ap[:, 32:48].rearrange("p (t g) -> p t g", t=NT)[:, :, 0:3]

        def by_head(t):
            return (proj[:, t, NKC:NKC + 4 * HD].rearrange("p (h c d) -> p c h d", c=2, h=2),
                    ps[:, t, 0:4 * HD].rearrange("p (c h d) -> p c h d", c=2, h=2))

        G_X = (0, 0)
        G_POS = (4, 4)
        G_ABC = (5, 4)
        G_LAT = (16, 15)
        G_CMP = (18, 14)
        G_O = (18, 18)
        G_H = (22, 22)
        G_END = (26, 26)
        def group_of(j):
            return G_ABC[j % 2] + j // 2 + (2 if j % 2 and G_ABC[1] + j // 2 >= G_CMP[1] else 0)
        ABC_OF = [[j for j, (col, _, _) in enumerate(abc) if c0 <= col < c0 + n] for c0, n in CHUNKS]
        NORMED = {2: (SWQ, 6, 0), 3: (NQ, 4, 24), 4: (NKS, 2, 40), 5: (NKW, 2, 48)}
        R_LAT, R_CMP, R_D, R_G, R_O, R_X2 = 6, 7, 8, 9, 10, 11

        units = [(kind, h, i, {"B": P * min(i + 1, 2), "cmp": NCMP}.get(kind, P * (i + 1)))
                 for kind in ("A", "B", "cmp", "slc", "win", "D") for h in range(4) for i in range(NT)]
        NU = len(units)
        NSB = 4 * NT
        GROUP_SUMS = ((22, 4), (38, 8), (86, 20))
        U_CMP = 2 * NSB
        U_NORMC, U_CMPT = 3, 14
        U_SUMD, U_LAT = 4, 56

        def q_of(kind, h, i):
            c = slice(i * P, (i + 1) * P)
            if kind == "A":
                return heads[0:HD, SL_A + h, c]
            if kind == "B":
                return heads[0:HD, SL_B + h, c]
            if kind == "D":
                return heads[0:MQK, SL_D + h, c]
            return heads[0:HD, SL_C + h, c]

        def k_of(kind, h, i, n):
            if kind == "A":
                return heads[0:HD, SL_A + 4 + h, 0:n]
            if kind == "B":
                return heads[0:HD, SL_B + 4 + h // 2, (i + 1) * P - n:(i + 1) * P]
            if kind == "cmp":
                return kcmpT[:, h // 2, 0:NCMP]
            if kind == "slc":
                return heads[0:HD, SL_C + 4 + h // 2, 0:n]
            if kind == "win":
                return heads[0:HD, SL_C + 6 + h // 2, 0:n]
            return heads[0:MQK, SL_D + 4 + h, 0:n]

        def v_of(kind, h, t):
            if kind == "A":
                return proj[:, t, SBV + h * HD:SBV + (h + 1) * HD]
            if kind == "B":
                return proj[:, t, SWV + (h // 2) * HD:SWV + (h // 2 + 1) * HD]
            if kind == "slc":
                return proj[:, t, NVS + (h // 2) * HD:NVS + (h // 2 + 1) * HD]
            if kind == "win":
                return proj[:, t, NVW + (h // 2) * HD:NVW + (h // 2 + 1) * HD]
            return vlat[:, t, h * HD:(h + 1) * HD]

        def bias_of(kind, h, i, n):
            if kind == "B":
                return gs[:, h, US - n:US]
            if kind == "D":
                return con[:, C_CM + T - n:C_CM + T]
            if kind == "A":
                return con[:, C_SM + T - n:C_SM + T]
            if kind == "cmp":
                u0 = P * (NT - 1 - i) + CMP_L - 1
                return gn[:, h, u0:u0 + CMP_S * (NCMP - 1) + 1:CMP_S]
            return gn[:, h, P * (NT - 1 - i):P * (NT - 1 - i) + n]

        def blocks_of(kind, i, n):
            if kind == "cmp":
                return [(0, NCMP, 0)]
            first = i + 1 - n // P
            return [(b * P, P, first + b) for b in range(n // P)]

        @block.sync
        def _(sp):
            def win_rows(l, c):
                c0, n = CHUNKS[c]
                return a["w_in"][bass.ds(l, 1)].rearrange("o (p k) n -> p (o k) n", k=KC)[:, :, c0:c0 + n]

            def load_params(l):
                for dst, src in params(l):
                    sp.dma_start(dst, src).then_inc(params_pre, 16)
            for t in range(NT):
                sp.dma_start(x[:, t, :], a["x"][0, t * P:(t + 1) * P, :]).then_inc(x_in[t], 16)
            sp.dma_start(con[:, :], consts).then_inc(bias_map_in, 16)
            sp.dma_start(relx[0:BUCKETS, :], a["rel_bias"]).then_inc(bias_map_in, 16)
            sp.dma_start(bmap[:, 0:TN + TS], bias_map).then_inc(bias_map_in, 16)
            sp.dma_start(win[0], win_rows(0, 0)).then_inc(win0_pre, 16)
            load_params(0)
            sp.dma_start(win[1], win_rows(0, 1)).then_inc(win1_pre, 16)
            with sp.Fori(0, L) as l:
                def load(dst, src, s):
                    sp.dma_start(dst, src).then_inc(s_[s], 16)

                def load_win(c):
                    load(win[c % 2][:, :, 0:CHUNKS[c][1]], win_rows(l, c), ("win_a", "win_b")[c % 2])
                enter(sp, l)
                for dst, src in late_params(l):
                    load(dst, src, "params_late")
                sp.wait_ge(params_pre, ALL_PARAMS * l + ALL_PARAMS)
                sp.sem_inc(s_["params"], 1)
                sp.wait_ge(win0_pre, 16 * l + 16)
                sp.sem_inc(s_["win_0"], 1)
                sp.wait_ge(win1_pre, 16 * l + 16)
                sp.sem_inc(s_["win_1"], 1)
                for c in range(2, len(CHUNKS)):
                    sp.wait_ge(s_["pj_mm"], NT * (c - 1))
                    load_win(c)
                for c in range(2):
                    load(w1[c * HD:(c + 1) * HD], a["nsa_cmp_w1"][bass.ds(l, 1), c].rearrange("o l d f -> d (o l) f"), "w1_in")
                sp.wait_ge(s_["pv"], NU - 4 * NT)
                load(w_o, a["w_out"][bass.ds(l, 1)].rearrange("o (p k) n -> p (o k) n", k=KC), "wout_in")

                def gate_up_of(e):
                    return [a[n][bass.ds(l, 1), bass.ds(e, 1)].rearrange("a b (p k) f -> p (a b k) f", k=KC)
                            for n in ("moe_w_gate", "moe_w_up")]

                def down_of(e):
                    return a["moe_w_down"][bass.ds(l, 1), bass.ds(e, 1)].rearrange("a b (c p) n -> p (a b c) n", c=2)
                def ring(e, s):
                    g, u = gate_up_of(e)
                    load(ring_g[s], g, f"wg{s}")
                    load(ring_u[s], u, f"wu{s}")
                    load(ring_d[s], down_of(e), f"wd{s}")
                ring(0, 0)
                ring(1, 1)
                sp.wait_ge(s_["pv"], NU)
                ring(2, 2)
                sp.wait_ge(s_["wo_mm"], 2 * NT)
                ring(3, 3)
                sp.wait_ge(scat, 16 * 2 * NT * l + 16 * 2 * NT)
                sp.wait_ge(s_["lg_mm"], 1)
                for s in range(2):
                    load(xe[s], xs_dram[s * S:(s + 1) * S, :], f"xe{s}")
                with sp.If(l < L - 1):
                    load_params(L - 1)
                with sp.Fori(1, NE // 4) as i:
                    for s in range(4):
                        g, u = gate_up_of(4 * i + s)
                        sp.wait_ge(s_["gu_mm"], 4 * i + s - 3)
                        load(ring_g[s], g, f"wg{s}")
                        load(ring_u[s], u, f"wu{s}")
                        sp.wait_ge(s_["dn_mm"], 4 * i + s - 3)
                        load(ring_d[s], down_of(4 * i + s), f"wd{s}")
                sp.wait_ge(s_["dn_mm"], NE)
                sp.wait_ge(s_["xeT_mm"], NE + 1)
                for s in range(2):
                    sp.wait_ge(s_[f"xe{s}"], 16 * (NE // 2 + 1))
                sp.wait_ge(s_["over_rdy"], 1)
                n_over = sp.value_load(overi[0:1, 15:16], min_val=0, max_val=NOVER)
                with sp.If(n_over > 0):
                    with sp.Fori(0, n_over) as k:
                        e = sp.value_load(overi[0:1, bass.ds(k, 1)], min_val=0, max_val=NE - 1)
                        g, u = gate_up_of(e)
                        load(ring_g[0], g, "f_in")
                        load(ring_u[0], u, "f_in")
                        load(ring_d[0], down_of(e), "f_in")
                        load(xe[0], xs_dram[bass.ds(k * S + NE * S, S), :], "f_in")
                        sp.wait_ge(s_["f_end"], k + 1)
                        sp.sem_inc(s_["f_loop"], 1)
                with sp.If(l < L - 1):
                    sp.wait_ge(s_["comb"], 2 * NT - 2)
                    sp.dma_start(win[0], win_rows(L - 1, 0)).then_inc(win0_pre, 16)
                    sp.dma_start(win[1], win_rows(L - 1, 1)).then_inc(win1_pre, 16)
                with sp.If(l > L - 2):
                    for t in range(NT):
                        sp.wait_ge(s_["comb"], 2 * t + 2)
                        sp.dma_start(out[0, t * P:(t + 1) * P, :], x[:, t, :]).then_inc(out_done, 16)
                after(sp.drain(), "sp_done")
            sp.wait_ge(layer_open, L + 1)
            sp.wait_ge(out_done, 16 * NT)

        @block.tensor
        def _(pe):
            mm = nc.tensor.matmul

            def transposes(srcs, rows, n, on, kp=P, step=0):
                tr, ev, bank = (("tr_act", "ev_act", 4), ("tr_dve", "ev_dve", 5))[on]
                bank += 2 * (step % 2)
                if n - (step > 0) > 0:
                    pe.wait_ge(s_[ev], n - (step > 0))
                for i, src in enumerate(srcs):
                    ins = nc.tensor.transpose(ps[0:rows, bank, i * kp:(i + 1) * kp], src, con[0:kp, C_ID:C_ID + kp])
                after(ins, tr)

            pe.wait_ge(bias_map_in, 48)
            pe.wait_ge(setup_dve, 1)
            for c in range(3):
                n = min(512, TN + TS - c * 512)
                mm(ps[0:8, c, 0:n], relx[:, :], bmap[:, c * 512:c * 512 + n], start=True, stop=True).then_inc(bias_mm, 1)
            pe.wait_ge(bias_neg, 3)
            with pe.Fori(0, L) as l:
                enter(pe, l)
                pe.wait_ge(s_["xn_rdy"], NT)
                for k in range(KC):
                    transposes([xoc[:, t, k::KC] for t in range(NT)], P, G_X[k % 2] + k // 2, k % 2, step=k // 2)
                pe.wait_ge(s_["params"], 1)
                transposes([cpos[:, :]], P, G_POS[0], 0, kp=CMP_L)
                pe.wait_ge(s_["ev_act"], G_POS[0])
                pe.wait_ge(s_["ev_dve"], G_POS[1])

                def head_groups(c):
                    pe.wait_ge(s_["pj_ev_act"], 2 * c + 2)
                    pe.wait_ge(s_["pj_ev_dve"], 2 * c + 2)
                    if c in NORMED:
                        pe.wait_ge(s_["norms_rdy"], c - 1)
                    for j in ABC_OF[c]:
                        col = abc[j][0]
                        transposes([proj[:, t, col:col + HD] for t in range(NT)], HD, group_of(j), j % 2)
                for c, (c0, n) in enumerate(CHUNKS):
                    if c == 6:
                        for h in range(2):
                            transposes([proj[:, t, NKC + h * P:NKC + (h + 1) * P] for t in range(NT)], P, G_CMP[1] + h, 1, step=h)
                    if c < 2:
                        pe.wait_ge(s_[("win_0", "win_1")[c]], 1)
                    else:
                        pe.wait_ge(s_[("win_a", "win_b")[c % 2]], 16 * (c // 2))
                    for t in range(NT):
                        if c:
                            pe.wait_ge(s_[("pj_ev_act", "pj_ev_dve")[t % 2]], 2 * (c - 1) + t // 2 + 1)
                        for k in range(KC):
                            ins = mm(ps[:, t, 0:n], hTc[:, k, t * P:(t + 1) * P], win[c % 2][:, k, 0:n], start=k == 0, stop=k == KC - 1)
                        after(ins, "pj_mm")
                    if c:
                        head_groups(c - 1)
                pe.wait_ge(s_["w1_in"], 32)

                pe.wait_ge(s_["ev_dve"], G_CMP[1] + 2)
                for j in range(CMP_L):
                    c0 = base + (SL_X + 2 * (j // CMP_S)) * T + j
                    for c in range(2):
                        r = slice(c * HD, (c + 1) * HD)
                        ins = mm(ps[WROWS[c], 6 + c, 0:CMP_H], big[r, c0:c0 + CMP_S * (NWIN - 1) + 1:CMP_S], w1[r, j, :], start=j == 0, stop=j == CMP_L - 1)
                after(ins, "cmp_mm")
                pe.wait_ge(s_["norms_rdy"], 5)
                transposes([proj[:, t, MCQ:MCQ + QR:2] for t in range(NT)], MQK, G_LAT[0], 0)
                transposes([proj[:, t, MCKV:MCKV + KVR] for t in range(NT)], KVR, G_LAT[0] + 1, 0)
                transposes([proj[:, t, MCQ + 1:MCQ + QR:2] for t in range(NT)], MQK, G_LAT[1] + 2, 1)
                pe.wait_ge(s_["params_late"], LATE_PARAMS)
                pe.wait_ge(s_["ev_act"], G_O[0])
                pe.wait_ge(s_["ev_dve"], G_O[1])
                for t in range(NT):
                    if t >= 2:
                        pe.wait_ge(s_["up_ev_act"], t - 1)
                        pe.wait_ge(s_["up_ev_dve"], t - 1)
                    for c in range(2):
                        mm(ps[:, 2 * (t % 2), 0:384], heads[0:MQK, SL_L + c, t * P:(t + 1) * P], w_qup[:, c, :], start=c == 0, stop=c == 1)
                    after(mm(ps[:, 2 * (t % 2) + 1, :], heads[:, SL_L + 2, t * P:(t + 1) * P], w_kvup, start=True, stop=True), "up_mm")
                pe.wait_ge(s_["up_ev_act"], NT)
                pe.wait_ge(s_["up_ev_dve"], NT)

                def scores(u):
                    kind, h, i, n = units[u]
                    if u >= 3:
                        pe.wait_ge(s_["logits"], u - 2)
                    after(mm(ps[:, u % 3, 0:n], q_of(kind, h, i), k_of(kind, h, i, n), start=True, stop=True), "scores")

                def turn(u):
                    kind, h, i, n = units[u]
                    if kind == "A":
                        pe.wait_ge(s_["probs_sb"], u + 1)
                    else:
                        pe.wait_ge(s_["probs_sm"], u + 1 - NSB)
                    if u >= 2:
                        pe.wait_ge(s_["probT_ev"], u - 1)
                    for c0, w, _ in blocks_of(kind, i, n):
                        ins = nc.tensor.transpose(ps[0:w, 3 + u % 2, c0:c0 + P], prb[u % 2][:, c0:c0 + w], ident)
                    after(ins, "probT")

                def values(u):
                    kind, h, i, n = units[u]
                    g = u // NT
                    if i == 0 and g >= 2:
                        pe.wait_ge(s_["head_out"], g - 1)
                    pe.wait_ge(s_["probT_ev"], u + 1)
                    bl = blocks_of(kind, i, n)
                    for j, (c0, w, kt) in enumerate(bl):
                        v = vcmp[:, h // 2, :] if kind == "cmp" else v_of(kind, h, kt)
                        ins = mm(ps[0:HD, 5 + g % 2, i * P:(i + 1) * P], v, prT[u % 2][0:w, c0:c0 + P], start=j == 0, stop=j == len(bl) - 1)
                    after(ins, "pv")

                def turn_back(g):
                    pe.wait_ge(s_["oT_rdy"], g + 1)
                    for t in range(NT):
                        ins = nc.tensor.transpose(ps[:, 5 + g % 2, t * HD:(t + 1) * HD], oT[g % 2][:, t * P:(t + 1) * P], con[0:HD, C_ID:C_ID + HD])
                    after(ins, "oT_mm")
                for u in range(-2, NU + 3):
                    if u + 2 < NU:
                        scores(u + 2)
                    if 0 <= u < NU:
                        turn(u)
                    if 1 <= u <= NU:
                        values(u - 1)
                    if u >= NT + 2 and u % NT == 2:
                        turn_back(u // NT - 1)
                    if u == -1:
                        pe.wait_ge(s_["cmp_ev"], 1)
                        for c in range(2):
                            ins = nc.tensor.transpose(ps[:, 6 + c, CMP_H:CMP_H + NWIN], hidden[c], con[WROWS[c], C_ID + c * HD:C_ID + c * HD + NWIN])
                        after(ins, "cmph_mm")
                    if u == 1:
                        pe.wait_ge(s_["cmph_ev"], 1)
                        for c in range(2):
                            for h in range(2):
                                ins = mm(ps[0:NCMP, 7, (2 * c + h) * HD:(2 * c + h + 1) * HD], hcmp[:, c, h, 0:NCMP], w_cmp2[:, c, :], start=True, stop=True)
                        after(ins, "cmp_out")
                    if u == U_CMPT:
                        pe.wait_ge(s_["cmp_n"], 1)
                        for h in range(2):
                            ins = nc.tensor.transpose(ps[0:HD, 7, h * 32:h * 32 + NCMP], kcmp[:, h, :], con[0:NCMP, C_ID:C_ID + NCMP])
                        after(ins, "cmpT_mm")
                    if u + 2 == U_CMP:
                        pe.wait_ge(s_["cmpT_ev"], 1)
                    if U_LAT <= u < U_LAT + 8:
                        h = u - U_LAT
                        if h == 0:
                            pe.wait_ge(s_["dqk_rdy"], 1)
                        else:
                            pe.wait_ge(s_["lat_ev"], h)
                        for t in range(NT):
                            ins = nc.tensor.transpose(ps[0:MQK, 7, t * P:(t + 1) * P], dqk[h // 4][:, t, h % 4, :], ident)
                        after(ins, "lat_T")
                    if u == U_LAT + 8:
                        pe.wait_ge(s_["lat_ev"], 8)
                pe.wait_ge(s_["og_rdy"], 1)
                pe.wait_ge(s_["o_rdy"], 1)
                for k in range(KC):
                    transposes([xoc[:, t, k::KC] for t in range(NT)], P, G_O[k % 2] + k // 2, k % 2, step=k // 2)
                pe.wait_ge(s_["ev_act"], G_H[0])
                pe.wait_ge(s_["ev_dve"], G_H[1])
                pe.wait_ge(s_["wout_in"], 16)
                for j in range(2 * NT):
                    if j >= 4:
                        pe.wait_ge(s_["wo_ev"], j - 3)
                    for k in range(KC):
                        ins = mm(ps[:, j % 4, :], hTc[:, k, j // 2 * P:(j // 2 + 1) * P], w_o[:, k, j % 2 * 512:(j % 2 + 1) * 512], start=k == 0, stop=k == KC - 1)
                    after(ins, "wo_mm")
                pe.wait_ge(s_["xn_rdy"], 2 * NT)
                for k in range(KC + 2):
                    if k < KC:
                        transposes([xoc[:, t, k::KC] for t in range(NT)], P, G_H[k % 2] + k // 2, k % 2, step=k // 2)
                    if k >= 2:
                        j = k - 2
                        pe.wait_ge(s_[("ev_act", "ev_dve")[j % 2]], G_H[j % 2] + j // 2 + 1)
                        ins = mm(ps[LROWS[j % 2], j % 2, :], w_rt[:, j, :], hTc[:, j, :], start=j < 2, stop=j >= KC - 2)
                        if j >= KC - 2:
                            after(ins, "lgT_mm")
                pe.wait_ge(s_["lgT_ev"], 2)
                for i in range(2):
                    for t in range(NT):
                        ins = nc.tensor.transpose(ps[:, 2 + i, t * NR:(t + 1) * NR], sq[LROWS[i], t * P:(t + 1) * P], con[LROWS[i], C_ID + 64 * i:C_ID + 64 * i + NR])
                after(ins, "lg_mm")
                pe.wait_ge(s_["assign"], 1)
                for b in range(NT):
                    mm(ps[:, 2, 0:NE], ones[:, :], rt[:, 9, b, :], start=b == 0, stop=b == NT - 1)
                mm(ps[:, 1, 0:NT * NE], con[:, C_TRI:C_TRI + P], rt[:, 9], start=True, stop=False)
                for b in range(NT - 1):
                    ins = mm(ps[:, 1, (b + 1) * NE:NT * NE].rearrange("p (t e) -> p t e", e=NE), ones[:, :],
                             rt[:, 9, b, :].unsqueeze(1).broadcast_to([P, NT - 1 - b, NE]), start=False, stop=b == NT - 2)
                after(ins, "pos_mm")

                def turn_x(s):
                    for k in range(KC):
                        ins = nc.tensor.transpose(ps[:, 4 + s, k * S:(k + 1) * S], xe[s][:, k::KC], con[0:S, C_ID:C_ID + S])
                    return ins

                def gate_up(s, ks):
                    for k in ks:
                        for c in range(2):
                            ins = mm(ps[c * S:(c + 1) * S, 2 + s % 2, 0:FH].rearrange("p (g f) -> p g f", g=2), xeT[s % 2][:, k, :],
                                     ring_gu[s][:, :, k, c * P:(c + 1) * P], start=k == 0, stop=k == KC - 1)
                    return ins

                def turn_a(b):
                    return nc.tensor.transpose(ps[:, 2 + b, FH:FH + P], sg[:, b, :], ident)

                def down(s):
                    for c in range(2):
                        for hf in range(2):
                            ins = mm(ps[hf * S:(hf + 1) * S, (0, 6)[s % 2], :], aT[:, s % 2, c, :], ring_d[s][:, c, hf * 512:(hf + 1) * 512], start=c == 0, stop=c == 1)
                    return ins

                def expert(e, q, s, first):
                    pe.wait_ge(s_[f"wg{s}"], 16 * q + 16)
                    pe.wait_ge(s_[f"wu{s}"], 16 * q + 16)
                    pe.wait_ge(s_["xeT_ev"], e + 1)
                    gate_up(s, range(3))
                    if not first or s >= 1:
                        pe.wait_ge(s_["a_rdy"], e)
                    gate_up(s, [3])
                    if not first or s >= 1:
                        after(turn_a(1 - s % 2), "aT_mm")
                    pe.wait_ge(s_[f"xe{1 - s % 2}"], 32 * q + 16 * ((s + 1) // 2) + 16)
                    gate_up(s, [4])
                    after(turn_x(1 - s % 2), "xeT_mm")
                    after(gate_up(s, range(5, KC)), "gu_mm")
                    if not first or s >= 1:
                        before = (s - 1) % 4
                        if not first or s >= 3:
                            pe.wait_ge(s_["y_dve"], e - 2)
                        pe.wait_ge(s_[f"wd{before}"], 16 * q + (16 if s else 0))
                        pe.wait_ge(s_["aT_ev"], e)
                        after(down(before), "dn_mm")
                pe.wait_ge(s_["xe0"], 16)
                after(turn_x(0), "xeT_mm")
                pe.wait_ge(s_["slots_rdy"], 1)
                for s in range(4):
                    expert(s, 0, s, True)
                with pe.Fori(1, NE // 4) as i:
                    for s in range(4):
                        expert(4 * i + s, i, s, False)
                pe.wait_ge(s_["a_rdy"], NE)
                after(turn_a(1), "aT_mm")
                pe.wait_ge(s_["y_dve"], NE - 2)
                pe.wait_ge(s_["wd3"], 16 * NE // 4)
                pe.wait_ge(s_["aT_ev"], NE)
                after(down(3), "dn_mm")
                pe.wait_ge(s_["over_rdy"], 1)
                n_over = pe.value_load(overi[0:1, 15:16], min_val=0, max_val=NOVER)
                pe.wait_ge(s_["xeT_ev"], NE + 1)
                pe.wait_ge(s_["y_dve"], NE)
                with pe.If(n_over > 0):
                    with pe.Fori(0, n_over) as k:
                        pe.wait_ge(s_["f_in"], 64 * k + 64)
                        pe.sem_inc(s_["f_step"], 1)
                        after(turn_x(0), "f_T")
                        pe.wait_ge(s_["f_Tev"], k + 1)
                        after(gate_up(0, range(KC)), "f_gu")
                        pe.wait_ge(s_["f_a"], k + 1)
                        pe.sem_inc(s_["f_step"], 1)
                        after(turn_a(0), "f_aT")
                        pe.wait_ge(s_["f_aTev"], k + 1)
                        after(down(0), "f_dn")
                        pe.wait_ge(s_["f_end"], k + 1)
                after(pe.drain(), "pe_done")

        @block.scalar
        def _(act):
            def A(out_, in_, f, **kw):
                return nc.scalar.activation(out_, in_, f, **kw)

            def copy_out(n, dst, src, scale=1.0):
                act.wait_ge(s_["tr_act"], n + 1)
                after(A(dst, src, ACT.Identity, scale=scale), "ev_act")

            def sum_x(t, squares):
                return A(squares[:, t * D:(t + 1) * D], x[:, t, :], ACT.Square, accum_out=ss[:, t:t + 1])
            for t in range(NT):
                act.wait_ge(x_in[t], 16)
                ins = sum_x(t, hT)
            ins.then_inc(x_sums, 1)
            act.wait_ge(bias_map_in, 48)
            with act.Fori(0, L) as l:
                enter(act, l)
                act.wait_ge(s_["params"], 1)
                for k in range(0, KC, 2):
                    copy_out(G_X[0] + k // 2, hTc[:, k, :], ps[:, 4 + k % 4, :], g_attn[:, k:k + 1])
                copy_out(G_POS[0], cposT[:, :], ps[:, 4, 0:CMP_L])
                act.wait_ge(bias_out, 128)

                def head_groups(c):
                    for j in ABC_OF[c]:
                        if j % 2 == 0:
                            copy_out(group_of(j), heads[0:HD, abc[j][1], :], ps[0:HD, 4, :], abc[j][2])
                for c, (c0, n) in enumerate(CHUNKS):
                    for t in (0, 2):
                        act.wait_ge(s_["pj_mm"], NT * c + t + 1)
                        if c0 == NKC:
                            A(*by_head(t), ACT.Identity)
                            skip = 4 * HD
                        else:
                            skip = 0
                        after(A(proj[:, t, c0 + skip:c0 + n], ps[:, t, skip:n], ACT.Identity), "pj_ev_act")
                    if c in NORMED or c == 6:
                        act.wait_ge(s_["pj_ev_dve"], 2 * c + 2)
                        act.wait_ge(s_["pj_ev_act"], 2 * c + 2)
                    if c in NORMED:
                        col, nh, _ = NORMED[c]
                        if c > 2:
                            act.wait_ge(s_["sq_used"], c - 2)
                        after(A(sqh[:, :, 0:nh * HD], proj[:, :, col:col + nh * HD], ACT.Square), "sum_rdy")
                    if c:
                        head_groups(c - 1)
                    if c == 6:
                        act.wait_ge(s_["sq_used"], 4)
                        for t in range(NT):
                            A(sqh[:, t, 0:QR], proj[:, t, MCQ:MCQ + QR], ACT.Square, accum_out=ss[:, 56 + t:57 + t])
                            ins = A(sqh[:, t, QR:QR + KVR], proj[:, t, MCKV:MCKV + KVR], ACT.Square, accum_out=ss[:, 60 + t:61 + t])
                        after(ins, "sum_rdy")
                copy_out(G_LAT[0], heads[0:MQK, SL_L, :], ps[0:MQK, 4, :], g_lq[:, 0:1])
                copy_out(G_LAT[0] + 1, heads[:, SL_L + 2, :], ps[:, 4, :], g_lkv[:, 0:1])
                act.wait_ge(s_["cmp_mm"], 1)

                for c in range(2):
                    ins = A(hidden[c], ps[WROWS[c], 6 + c, 0:CMP_H], ACT.Gelu_apprx_tanh)
                after(ins, "cmp_ev")
                for t in range(NT):
                    act.wait_ge(s_["up_mm"], t + 1)
                    after(A(dqk[0][:, t], ps[:, 2 * (t % 2), 0:384].rearrange("p (h c) -> p h c", h=4), ACT.Identity), "up_ev_act")
                A(gates[:, :, :], proj[:, :, NG:NG + 12], ACT.Sigmoid)

                def probs(u):
                    kind, h, i, n = units[u]
                    act.wait_ge(s_["logits"], u + 1)
                    if u >= 2:
                        act.wait_ge(s_["probT"], u - 1)
                    if kind == "A":
                        if u >= 2:
                            act.wait_ge(s_["probs_sb"], u - 1)
                        A(prb[u % 2][:, 0:n], lgt[u % 3][:, 0:n], ACT.Sigmoid, scale=HD ** -0.5)
                        after(A(keep[u % 2][:, 0:n], lgt[u % 3][:, 0:n], ACT.Sigmoid, scale=-(HD ** -0.5)), "sig")
                        return
                    after(A(prb[u % 2][:, 0:n], lgt[u % 3][:, 0:n], ACT.Exp, bias=mrow[:, u:u + 1], scale=-1.0, accum_out=den[:, u:u + 1]), "probs_sm")
                    if kind == "B" and i == NT - 1:
                        after(A(esink[:, h * NT:(h + 1) * NT], mrow[:, u - 3:u + 1], ACT.Exp, bias=sink[:, h:h + 1]), "esink_rdy")

                def copy_probs(u):
                    kind, h, i, n = units[u]
                    w, m = (NCMP, P) if kind == "cmp" else (P, n)
                    act.wait_ge(s_["probT"], u + 1)
                    if u >= 2:
                        act.wait_ge(s_["pv"], u - 1)
                    after(A(prT[u % 2][0:w, 0:m], ps[0:w, 3 + u % 2, 0:m], ACT.Identity), "probT_ev")
                def sum_group(t, g, squares):
                    c = t * D + g * 256
                    return A(squares, xo[:, c:c + 256], ACT.Square, accum_out=ss[:, 32 + 4 * t + g:33 + 4 * t + g])
                for u in range(-1, NU + 2):
                    if u + 1 < NU:
                        probs(u + 1)
                    if u > NT and u % NT == 1:
                        g = u // NT - 1
                        act.wait_ge(s_["pv"], NT * g + NT)
                        after(A(oT[g % 2], ps[0:HD, 5 + g % 2, :], ACT.Identity), "oT_rdy")
                    if 0 <= u < NU:
                        copy_probs(u)
                    if u == 0:
                        act.wait_ge(s_["cmph_mm"], 1)
                        for c in range(2):
                            ins = A(hcmp[:, c].rearrange("p h n -> p (h n)")[:, 0:NWIN], ps[:, 6 + c, CMP_H:CMP_H + NWIN], ACT.Identity)
                        after(ins, "cmph_ev")
                    for g, (u0, done) in enumerate(GROUP_SUMS):
                        if u0 <= u < u0 + NT:
                            if u == u0:
                                act.wait_ge(s_["head_out"], done)
                            ins = sum_group(u - u0, g, heads[:, SL_X + u % 2, 0:256])
                            if u == GROUP_SUMS[-1][0] + NT - 1:
                                after(ins, "sum_rdy")
                    if U_LAT <= u < U_LAT + 8:
                        h = u - U_LAT
                        act.wait_ge(s_["lat_T"], h + 1)
                        after(A(heads[0:MQK, SL_D + h, :], ps[0:MQK, 7, :], ACT.Identity, scale=-(MQK ** -0.5) if h < 4 else 1.0), "lat_ev")
                act.wait_ge(s_["head_out"], NU // NT)
                for t in range(NT):
                    ins = sum_group(t, 3, hT[:, 3 * T + t * 256:3 * T + (t + 1) * 256])
                after(ins, "sum_rdy")
                for k in range(0, KC, 2):
                    copy_out(G_O[0] + k // 2, hTc[:, k, :], ps[:, 4 + k % 4, :], g_out[:, k:k + 1])
                for t in range(NT):
                    act.wait_ge(s_["wo_ev"], 2 * t + 2)
                    after(sum_x(t, xo), "sum_x2")
                act.wait_ge(s_["params_late"], LATE_PARAMS)
                for k in range(0, KC, 2):
                    copy_out(G_H[0] + k // 2, hTc[:, k, :], ps[:, 4 + k % 4, :], g_ffn[:, k:k + 1])
                act.wait_ge(s_["lgT_mm"], 1)
                after(A(sq[LROWS[0], 0:T], ps[LROWS[0], 0, :], ACT.Identity), "lgT_ev")
                act.wait_ge(s_["rt_in"], 1)
                after(A(gex[:, :, :], gex[:, :, :], ACT.Exp), "rt_exp")
                act.wait_ge(s_["rt_in"], 2)
                after(A(rsm[:, 6, :], rsm[:, 6, :], ACT.Exp), "rt_exp")

                def store(slot, buf, s):
                    for hf in range(2):
                        after(act.dma_start(ys_dram[bass.ds(slot, S), hf * 512:(hf + 1) * 512], ye[buf][hf * S:(hf + 1) * S, :]), s, 16)

                def output(e, q, s, first):
                    act.wait_ge(s_["y_dve"], e + 1)
                    store(e * S, s % 2, f"yst{s % 2}")

                def take_a(b):
                    return A(aT[:, b, :, :], ps[:, 2 + b, FH:FH + P].rearrange("p (c s) -> p c s", c=2), ACT.Identity)

                def expert(e, q, s, first):
                    act.wait_ge(s_["xeT_mm"], e + 1)
                    after(act.dma_start(xe[s % 2], xs_dram[bass.ds(e * S + 2 * S, S), :]), f"xe{s % 2}", 16)
                    if not first or s >= 1:
                        act.wait_ge(s_["aT_mm"], e)
                        after(take_a(1 - s % 2), "aT_ev")
                    act.wait_ge(s_["gu_mm"], e + 1)
                    after(A(sg[:, s % 2, :], ps[:, 2 + s % 2, 0:P], ACT.Silu), "silu_rdy")
                    if not first or s >= 1:
                        output(e - 1, q, s - 1, first)
                for s in range(4):
                    expert(s, 0, s, True)
                with act.Fori(1, NE // 4) as i:
                    for s in range(4):
                        expert(4 * i + s, i, s, False)
                act.wait_ge(s_["aT_mm"], NE)
                after(take_a(1), "aT_ev")
                output(NE - 1, NE // 4 - 1, 3, False)
                act.wait_ge(s_["over_rdy"], 1)
                n_over = act.value_load(overi[0:1, 15:16], min_val=0, max_val=NOVER)
                act.wait_ge(s_["yst0"], 32 * NE // 2)
                with act.If(n_over > 0):
                    with act.Fori(0, n_over) as k:
                        act.wait_ge(s_["f_gu"], k + 1)
                        after(A(sg[:, 0, :], ps[:, 2, 0:P], ACT.Silu), "f_silu")
                        act.wait_ge(s_["f_aT"], k + 1)
                        after(take_a(0), "f_aTev")
                        act.wait_ge(s_["f_ydve"], k + 1)
                        store(k * S + NE * S, 0, "f_st")
                        act.wait_ge(s_["f_st"], 32 * k + 32)
                        act.sem_inc(s_["f_end"], 1)
                for t in range(NT):
                    act.wait_ge(s_["comb"], 2 * t + 2)
                    sum_x(t, hT)
                after(act.drain(), "act_done")

        @block.vector
        def _(dve):
            V = nc.vector
            steps = [0]

            def link(ins):
                steps[0] += 1
                after(ins, "dve_step")
                dve.wait_ge(s_["dve_step"], steps[0])

            def copy_out(n, dst, src, scale=1.0):
                dve.wait_ge(s_["tr_dve"], n + 1)
                after(V.tensor_scalar(dst, src, scale, None, ALU.mult), "ev_dve")

            def mean(dst, src, width):
                return V.tensor_scalar(dst, src, 1.0 / width, EPS, ALU.mult, ALU.add)

            def norm_tile(t):
                after(V.tensor_scalar(xoc[:, t, :], x[:, t, :], rs[:, t:t + 1], None, ALU.mult), "xn_rdy")

            def norm_x(rounds):
                after(mean(ss[:, 0:NT], ss[:, 0:NT], D), "ms_rdy")
                dve.wait_ge(s_["rs_rdy"], rounds)
                for t in range(NT):
                    norm_tile(t)

            def bc(ap, shape):
                return ap.broadcast_to(shape)

            V.memset(relx[BUCKETS:BUCKETS + 1, :], 1.0)
            V.memset(ones[:, :], 1.0)
            V.memset(neghalf[:, :], -0.5).then_inc(setup_dve, 1)
            for c in range(3):
                n = min(512, TN + TS - c * 512)
                dve.wait_ge(bias_mm, c + 1)
                V.tensor_scalar(sq[0:8, c * 512:c * 512 + n], ps[0:8, c, 0:n], -1.0, None, ALU.mult).then_inc(bias_neg, 1)
            for t in range(NT):
                dve.wait_ge(x_in[t], 16)
            dve.wait_ge(x_sums, 1)
            dve.wait_ge(bias_map_in, 48)
            with dve.Fori(0, L) as l:
                steps[0] = 0
                enter(dve, l)
                norm_x(1)
                dve.wait_ge(s_["params"], 1)
                link(V.tensor_scalar(g64q[:, 0:1], g64[:, 0:1], -(HD ** -0.5), None, ALU.mult))
                link(V.tensor_scalar(g64q[:, 1:2], g64[:, 2:3], -(HD ** -0.5), None, ALU.mult))
                link(V.tensor_scalar(nsink[:, :], sink[:, :], -1.0, None, ALU.mult))
                for k in range(1, KC, 2):
                    copy_out(G_X[1] + k // 2, hTc[:, k, :], ps[:, 4 + k % 4, :], g_attn[:, k:k + 1])
                def head_groups(c):
                    for j in ABC_OF[c]:
                        if j % 2:
                            copy_out(group_of(j), heads[0:HD, abc[j][1], :], ps[0:HD, 5, :], abc[j][2])
                for c, (c0, n) in enumerate(CHUNKS):
                    if c == 6:
                        dve.wait_ge(s_["ev_act"], G_ABC[0])
                        for h in range(2):
                            dve.wait_ge(s_["tr_dve"], G_CMP[1] + h + 1)
                            src = ps[:, 5 + 2 * h, :].rearrange("p (b r) -> p b r", r=CMP_S)
                            for half in range(2):
                                dst = heads[:, SL_X + 2 * half + h, :].rearrange("p (b r) -> p b r", r=CMP_S)
                                pos = cposT[:, half * CMP_S:(half + 1) * CMP_S].unsqueeze(1)
                                ins = V.tensor_tensor(dst, src, bc(pos, [P, T // CMP_S, CMP_S]), ALU.add)
                            after(ins, "ev_dve")
                    for t in (1, 3):
                        dve.wait_ge(s_["pj_mm"], NT * c + t + 1)
                        if c0 == NKC:
                            V.tensor_copy(*by_head(t))
                            skip = 4 * HD
                        else:
                            skip = 0
                        after(V.tensor_copy(proj[:, t, c0 + skip:c0 + n], ps[:, t, skip:n]), "pj_ev_dve")
                    if c in NORMED:
                        col, nh, r0 = NORMED[c]
                        dve.wait_ge(s_["sum_rdy"], c - 1)
                        sums = ss[:, r0:r0 + NT * nh]
                        ins = V.tensor_reduce(sums.rearrange("p (t h) -> p t h", t=NT), sqh[:, :, 0:nh * HD].rearrange("p t (h c) -> p t h c", c=HD), AX.X, ALU.add)
                        link(ins)
                        after(mean(sums, sums, HD), "ms_rdy")
                        V.memset(den2[:, :], 0.0).then_inc(s_["sq_used"], 1)
                    if c:
                        head_groups(c - 1)
                    if c == 6:
                        dve.wait_ge(s_["sum_rdy"], R_LAT - 1)
                        mean(ss[:, 56:60], ss[:, 56:60], QR)
                        after(mean(ss[:, 60:64], ss[:, 60:64], KVR), "ms_rdy")
                    if c in NORMED:
                        dve.wait_ge(s_["rs_rdy"], c)
                        dve.wait_ge(s_["pj_ev_dve"], 2 * c + 2)
                        v = proj[:, :, col:col + nh * HD].rearrange("p t (h c) -> p t h c", c=HD)
                        r = rs[:, r0:r0 + NT * nh].rearrange("p (t h) -> p t h", t=NT).unsqueeze(3)
                        after(V.tensor_tensor(v, v, bc(r, [P, NT, nh, HD]), ALU.mult), "norms_rdy")
                dve.wait_ge(s_["rs_rdy"], R_LAT)
                for c0, n, r0 in ((MCQ, QR, 56), (MCKV, KVR, 60)):
                    v = proj[:, :, c0:c0 + n]
                    ins = V.tensor_tensor(v, v, bc(rs[:, r0:r0 + NT].unsqueeze(2), [P, NT, n]), ALU.mult)
                after(ins, "norms_rdy")
                copy_out(G_LAT[1] + 2, heads[0:MQK, SL_L + 1, :], ps[0:MQK, 5, :], g_lq[:, 1:2])
                V.tensor_copy(dqk[1][:, :, :, NOPE:], bc(proj[:, :, MKPE:MKPE + ROPE].unsqueeze(2), [P, NT, 4, ROPE]))
                for t in range(NT):
                    dve.wait_ge(s_["up_mm"], t + 1)
                    kv = ps[:, 2 * (t % 2) + 1, :].rearrange("p (h c) -> p h c", h=4)
                    V.tensor_copy(vlat[:, t, :].rearrange("p (h c) -> p h c", h=4), kv[:, :, NOPE:])
                    after(V.tensor_copy(dqk[1][:, t, :, 0:NOPE], kv[:, :, 0:NOPE]), "up_ev_dve")
                for s in range(2):
                    link(V.memset(left[s][:, T:T + 1], 1.0))
                dve.wait_ge(bias_in, 128)

                def logits(u):
                    kind, h, i, n = units[u]
                    dve.wait_ge(s_["scores"], u + 1)
                    if u >= 3:
                        if units[u - 3][0] == "A":
                            dve.wait_ge(s_["sig"], u - 2)
                        else:
                            dve.wait_ge(s_["probs_sm"], u - 2 - NSB)
                    if kind == "A":
                        after(V.tensor_tensor(lgt[u % 3][:, 0:n], ps[:, u % 3, 0:n], bias_of(kind, h, i, n), ALU.add), "logits")
                        return
                    start = nsink[:, h:h + 1] if kind == "B" else 1e20
                    after(V.tensor_tensor_reduce(out=lgt[u % 3][:, 0:n], in0=ps[:, u % 3, 0:n], in1=bias_of(kind, h, i, n), scale=1.0,
                                                 scalar=start, op0=ALU.add, op1=ALU.min, accum_out=mrow[:, u:u + 1]), "logits")

                def stick(u):
                    kind, h, i, n = units[u]
                    dve.wait_ge(s_["sig"], u + 1)
                    link(V.tensor_tensor_scan(left[u % 2][:, T - n:T][:, ::-1], keep[u % 2][:, 0:n][:, ::-1], keep[u % 2][:, 0:n][:, ::-1], 1.0, ALU.mult, ALU.bypass))
                    after(V.tensor_tensor(prb[u % 2][:, 0:n], prb[u % 2][:, 0:n], left[u % 2][:, T - n + 1:T + 1], ALU.mult), "probs_sb")

                def head_out(g):
                    kind, h = units[g * NT][:2]
                    dve.wait_ge(s_["oT_mm"], g + 1)
                    grp = {"A": 0, "B": 1, "D": 3}.get(kind, 2)
                    src = ps[:, 5 + g % 2, 0:NT * HD].rearrange("p (t c) -> p t c", t=NT)
                    dst = xoc[:, :, grp * 256 + h * HD:grp * 256 + (h + 1) * HD]
                    if kind == "A":
                        after(V.tensor_copy(dst, src), "head_out")
                        return
                    d4 = den[:, NT * g:NT * g + NT]
                    if kind == "B":
                        dve.wait_ge(s_["esink_rdy"], h + 1)
                        link(V.tensor_tensor(d4, d4, esink[:, h * NT:(h + 1) * NT], ALU.add))
                    link(V.tensor_scalar(d4, d4, 1e-30, None, ALU.max))
                    link(V.reciprocal(den2[:, :], d4))
                    if grp == 2:
                        b = ("cmp", "slc", "win").index(kind)
                        link(V.tensor_tensor(den2[:, :], den2[:, :], gates[:, :, 4 * b + h], ALU.mult))
                    f = bc(den2[:, :].unsqueeze(2), [P, NT, HD])
                    if kind in ("slc", "win"):
                        link(V.tensor_tensor(otmp[:, :, :], src, f, ALU.mult))
                        after(V.tensor_tensor(dst, dst, otmp[:, :, :], ALU.add), "head_out")
                        dve.wait_ge(s_["head_out"], g + 1)
                    else:
                        after(V.tensor_tensor(dst, src, f, ALU.mult), "head_out")
                        dve.wait_ge(s_["head_out"], g + 1)
                for u in range(-2, NU + 4):
                    if u + 2 < NU:
                        logits(u + 2)
                    if 0 <= u + 1 < NSB:
                        stick(u + 1)
                    if u >= NT + 3 and u % NT == 3:
                        head_out(u // NT - 1)
                    if u == U_NORMC:
                        dve.wait_ge(s_["cmp_out"], 1)
                        V.tensor_copy(vcmp[:, :, :], ps[0:NCMP, 7, 2 * HD:4 * HD].rearrange("p (h c) -> p h c", h=2))
                        link(V.tensor_copy(kcmp[:, :, :], ps[0:NCMP, 7, 0:2 * HD].rearrange("p (h c) -> p h c", h=2)))
                        link(V.tensor_tensor(csq[:, :, :], kcmp[:, :, :], kcmp[:, :, :], ALU.mult))
                        link(V.tensor_reduce(css[:, 0:2], csq[:, :, :], AX.X, ALU.add))
                        after(mean(css[:, 0:2], css[:, 0:2], HD), "ms_rdy")
                    if u == U_NORMC + 4:
                        dve.wait_ge(s_["rs_rdy"], R_CMP)
                        after(V.tensor_tensor(kcmp[:, :, :], kcmp[:, :, :], bc(css[:, 2:4].unsqueeze(2), [NCMP, 2, HD]), ALU.mult), "cmp_n")
                    if u == U_CMPT:
                        dve.wait_ge(s_["cmpT_mm"], 1)
                        after(V.tensor_scalar(kcmpT[:, :, 0:NCMP], ps[0:HD, 7, 0:64].rearrange("p (h n) -> p h n", h=2)[:, :, 0:NCMP], g64[:, 3:4], None, ALU.mult), "cmpT_ev")
                    if u == GROUP_SUMS[-1][0] + NT + 1:
                        dve.wait_ge(s_["sum_rdy"], 6)
                        m = by_group(ss)
                        after(mean(m, m, 256), "ms_rdy")
                    if U_SUMD <= u < U_SUMD + 8:
                        t, j = divmod(u - U_SUMD, 2)
                        if t == 0:
                            dve.wait_ge(s_["dsq_rdy"], j + 1)
                        link(V.tensor_reduce(ss[:, 8 * t + 4 * j:8 * t + 4 * j + 4], dsq[j][:, t], AX.X, ALU.add))
                    if u == U_SUMD + 8:
                        after(mean(ss[:, 0:32], ss[:, 0:32], MQK), "ms_rdy")
                dve.wait_ge(s_["sum_rdy"], 7)
                after(mean(ss[:, 35:48:4], ss[:, 35:48:4], 256), "ms_rdy")
                dve.wait_ge(s_["rs_rdy"], R_O)
                og = xoc[:, :, 768:]
                after(V.tensor_tensor(og, og, bc(rs[:, 35:48:4].unsqueeze(2), [P, NT, 256]), ALU.mult), "o_rdy")
                for k in range(1, KC, 2):
                    copy_out(G_O[1] + k // 2, hTc[:, k, :], ps[:, 4 + k % 4, :], g_out[:, k:k + 1])
                for j in range(2 * NT):
                    dve.wait_ge(s_["wo_mm"], j + 1)
                    xs = x[:, j // 2, j % 2 * 512:(j % 2 + 1) * 512]
                    after(V.tensor_tensor(xs, xs, ps[:, j % 4, :], ALU.add), "wo_ev")
                    if j == 2 * NT - 3:
                        dve.wait_ge(s_["sum_x2"], NT - 1)
                        after(mean(ss[:, 0:NT - 1], ss[:, 0:NT - 1], D), "ms_rdy")
                    if j == 2 * NT - 2:
                        dve.wait_ge(s_["rs_rdy"], R_X2)
                        for t in range(NT - 1):
                            norm_tile(t)
                dve.wait_ge(s_["sum_x2"], NT)
                after(mean(ss[:, NT - 1:NT], ss[:, NT - 1:NT], D), "ms_rdy")
                dve.wait_ge(s_["rs_rdy"], R_X2 + 1)
                norm_tile(NT - 1)
                dve.wait_ge(s_["params_late"], LATE_PARAMS)
                for k in range(1, KC, 2):
                    copy_out(G_H[1] + k // 2, hTc[:, k, :], ps[:, 4 + k % 4, :], g_ffn[:, k:k + 1])
                dve.wait_ge(s_["lgT_mm"], 2)
                after(V.tensor_copy(sq[LROWS[1], 0:T], ps[LROWS[1], 1, :]), "lgT_ev")
                TE = [P, NT, NE]
                dve.wait_ge(s_["lg_mm"], 1)
                part = [ps[:, 2 + i, 0:NT * NR].rearrange("p (t n) -> p t n", t=NT) for i in range(2)]
                link(V.tensor_tensor(lg[:, :, :], part[0], bc(rbias[:, :].unsqueeze(1), [P, NT, NR]), ALU.add))
                link(V.tensor_tensor(lg[:, :, :], lg[:, :, :], part[1], ALU.add))
                gl, el = lg[:, :, 0:NGRP], lg[:, :, NGRP:]

                def r(i):
                    return rsm[:, i, :]

                def b3(ap, n):
                    return bc(ap.unsqueeze(2), [P, NT, n])

                def c3(c, n):
                    return bc(con[:, c:c + n].unsqueeze(1), [P, NT, n])

                def first_best(dst, src, best, at, n):
                    link(V.tensor_reduce(best, src, AX.X, ALU.max))
                    link(V.tensor_tensor(dst, src, b3(best, n), ALU.is_equal))
                    link(V.scalar_tensor_tensor(dst, dst, -1000.0, c3(C_E, n), ALU.mult, ALU.add))
                    link(V.tensor_reduce(at, dst, AX.X, ALU.min))
                    link(V.tensor_tensor(dst, c3(C_IM, n), b3(at, n), ALU.is_equal))
                first_best(goh[:, :, :], gl, r(0), r(1), NGRP)
                after(V.tensor_tensor(gex[:, :, :], gl, b3(r(0), NGRP), ALU.subtract), "rt_in")
                link(V.tensor_scalar(goh[:, :, :], goh[:, :, :], BIG, -BIG, ALU.mult, ALU.add))
                em, oh1, oh2, em2, both, slot, ovf = [rt[:, i] for i in (0, 1, 2, 3, 9, 4, 5)]
                picks = rt[:, 6:8]
                link(V.tensor_tensor(em.rearrange("p t (g e) -> p t g e", g=NGRP), el.rearrange("p t (g e) -> p t g e", g=NGRP),
                                     bc(goh[:, :, :].unsqueeze(3), [P, NT, NGRP, EPG]), ALU.add))
                first_best(oh1, em, r(2), r(3), NE)
                link(V.scalar_tensor_tensor(em2, oh1, -2 * BIG, em, ALU.mult, ALU.add))
                first_best(oh2, em2, r(4), r(5), NE)
                after(V.tensor_tensor(both, oh1, oh2, ALU.add), "assign")
                after(V.tensor_tensor(r(6), r(4), r(2), ALU.subtract), "rt_in")
                dve.wait_ge(s_["rt_exp"], 2)
                V.tensor_scalar(r(7), r(6), 1.0, None, ALU.add)
                link(V.tensor_reduce(r(8), gex[:, :, :], AX.X, ALU.add))
                link(V.tensor_tensor(r(7), r(7), r(8), ALU.mult))
                link(V.reciprocal(r(9), r(7)))
                link(V.tensor_tensor(r(10), r(9), r(6), ALU.mult))
                dve.wait_ge(s_["pos_mm"], 1)
                w = [row[:, i, :] for i in range(6)]
                link(V.tensor_scalar(w[0], ps[:, 2, 0:NE], float(S - 1), None, ALU.add))
                link(V.tensor_copy(rowi[:, :], w[0]))
                link(V.tensor_scalar(rowi[:, :], rowi[:, :], 6, None, ALU.arith_shift_right))
                link(V.tensor_copy(w[1], rowi[:, :]))
                link(V.tensor_scalar(w[1], w[1], -1.0, 0.0, ALU.add, ALU.max))
                link(V.tensor_tensor_scan(w[2], w[1], w[1], 0.0, ALU.add, ALU.bypass))
                link(V.tensor_tensor(w[3], w[2], w[1], ALU.subtract))
                link(V.tensor_scalar(w[4], w[3], float(S), float(S * (NE - 1)), ALU.mult, ALU.add))
                link(V.tensor_tensor(w[4], w[4], con[:, C_E64:C_E64 + NE], ALU.subtract))
                pos = ps[:, 1, 0:NT * NE].rearrange("p (t e) -> p t e", t=NT)
                link(V.tensor_tensor(slot, pos, c3(C_E64, NE), ALU.add))
                link(V.tensor_scalar(ovf, pos, float(S), None, ALU.is_ge))
                link(V.tensor_tensor(ovf, ovf, bc(w[4].unsqueeze(1), TE), ALU.mult))
                link(V.tensor_tensor(slot, slot, ovf, ALU.add))
                link(V.tensor_tensor(picks, rt[:, 1:3], bc(slot.unsqueeze(1), [P, 2, NT, NE]), ALU.mult))
                link(V.tensor_reduce(slotf[:, :, :], picks, AX.X, ALU.add))
                after(V.tensor_copy(sloti[:, :, :], slotf[:, :, :]), "slots_rdy")
                TK = [1, 16, NE]
                kk = bc(con[0:1, C_K:C_K + 16].unsqueeze(2), TK)
                link(V.tensor_tensor(over[:, 0], kk, bc(w[3][0:1].unsqueeze(1), TK), ALU.is_ge))
                link(V.tensor_tensor(over[:, 1], kk, bc(w[2][0:1].unsqueeze(1), TK), ALU.is_lt))
                link(V.tensor_tensor(over[:, 0], over[:, 0], over[:, 1], ALU.mult))
                link(V.tensor_tensor(over[:, 0], over[:, 0], bc(con[0:1, C_E:C_E + NE].unsqueeze(1), TK), ALU.mult))
                link(V.tensor_reduce(overf[:, :], over[:, 0], AX.X, ALU.add))
                link(V.tensor_copy(overf[:, 15:16], w[2][0:1, NE - 1:NE]))
                after(V.tensor_copy(overi[:, :], overf[:, :]), "over_rdy")

                def take_x(s):
                    return V.tensor_tensor(xeT[s], ps[:, 4 + s, :].rearrange("p (k s) -> p k s", k=KC),
                                           bc(g_ffn[:, :].unsqueeze(2), [P, KC, S]), ALU.mult)

                def gate(s):
                    return V.tensor_tensor(sg[:, s, :], sg[:, s, :], ps[:, 2 + s, P:2 * P], ALU.mult)

                def output(e, q, s, first):
                    b = s % 2
                    if not first or s >= 2:
                        dve.wait_ge(s_[f"yst{b}"], 64 * q + 32 * (s // 2))
                    dve.wait_ge(s_["dn_mm"], e + 1)
                    after(V.tensor_copy(ye[b], ps[:, (0, 6)[b], :]), "y_dve")

                def expert(e, q, s, first):
                    dve.wait_ge(s_["xeT_mm"], e + 2)
                    after(take_x(1 - s % 2), "xeT_ev")
                    dve.wait_ge(s_["silu_rdy"], e + 1)
                    after(gate(s % 2), "a_rdy")
                    if not first or s >= 1:
                        output(e - 1, q, s - 1, first)
                dve.wait_ge(s_["xeT_mm"], 1)
                after(take_x(0), "xeT_ev")
                for s in range(4):
                    expert(s, 0, s, True)
                with dve.Fori(1, NE // 4) as i:
                    for s in range(4):
                        expert(4 * i + s, i, s, False)
                output(NE - 1, NE // 4 - 1, 3, False)
                dve.wait_ge(s_["over_rdy"], 1)
                n_over = dve.value_load(overi[0:1, 15:16], min_val=0, max_val=NOVER)
                dve.wait_ge(s_["yst0"], 32 * NE // 2)
                with dve.If(n_over > 0):
                    with dve.Fori(0, n_over) as k:
                        dve.wait_ge(s_["f_T"], k + 1)
                        after(take_x(0), "f_Tev")
                        dve.wait_ge(s_["f_silu"], k + 1)
                        after(gate(0), "f_a")
                        dve.wait_ge(s_["f_dn"], k + 1)
                        after(V.tensor_copy(ye[0], ps[:, 0, :]), "f_ydve")
                        dve.wait_ge(s_["f_end"], k + 1)
                for t in range(NT):
                    for j in range(2):
                        c = 2 * t + j
                        dve.wait_ge(gath[c], 16 * l + 16)
                        after(V.scalar_tensor_tensor(x[:, t, :], yg[c], rsm[:, 9 + j, t:t + 1], x[:, t, :], ALU.mult, ALU.add), "comb")
                        dve.wait_ge(s_["comb"], c + 1)
                after(dve.drain(), "dve_done")

        @block.gpsimd
        def _(pool):
            G = nc.gpsimd

            def rsqrt(n, dst, src, rows, cols):
                pool.wait_ge(s_["ms_rdy"], n)
                after(G.tensor_tensor(dst, src, neghalf[0:rows, 0:cols], ALU.pow), "rs_rdy")
            G.memset(zero[:, :], 0.0).then_inc(zeros_rdy, 1)
            pool.wait_ge(setup_dve, 1)
            pool.sem_inc(layer_open, 1)
            parts = [xs_dram[i:min(i + 4 * P, NSLOT // P * P), :] for i in range(0, NSLOT // P * P, 4 * P)]
            parts += [ys_dram[i:min(i + 4 * P, NSLOT // P * P), :] for i in range(NE * S, NSLOT // P * P, 4 * P)]
            n_zero = len(parts) + 2 * bool(NSLOT % P)
            with pool.Fori(0, L) as l:
                rsqrt(1, rs[:, 0:NT], ss[:, 0:NT], P, NT)
                with pool.If(l < 1):
                    pool.wait_ge(bias_neg, 3)
                    W = TN + TS
                    for h in range(4):
                        pool.dma_start(bias_rows[h:h + 1, :, 0:TN], sq[4 + h:5 + h, 0:TN].unsqueeze(1).broadcast_to([1, P, TN])).then_inc(bias_out, 16)
                        pool.dma_start(bias_rows[h:h + 1, :, TN:], sq[h:h + 1, TN:TN + TS].unsqueeze(1).broadcast_to([1, P, TS])).then_inc(bias_out, 16)
                    pool.wait_ge(bias_out, 128)
                    for h in range(4):
                        pool.dma_start(gn[:, h, :], bass.AP(bias_rows.tensor, h * P * W + P - 1, [[W - 1, P], [1, UN]])).then_inc(bias_in, 16)
                        pool.dma_start(gs[:, h, :], bass.AP(bias_rows.tensor, h * P * W + TN + P - 1, [[W - 1, P], [1, US]])).then_inc(bias_in, 16)
                for c, (_, nh, r0) in NORMED.items():
                    rsqrt(c, rs[:, r0:r0 + NT * nh], ss[:, r0:r0 + NT * nh], P, NT * nh)
                rsqrt(R_LAT, rs[:, 56:64], ss[:, 56:64], P, 8)
                pool.wait_ge(s_["up_ev_act"], NT)
                pool.wait_ge(s_["up_ev_dve"], NT)
                for j in range(2):
                    if j:
                        pool.wait_ge(s_["cmp_mm"], 1)
                    after(G.tensor_tensor(dsq[j], dqk[j], dqk[j], ALU.mult), "dsq_rdy")
                rsqrt(R_CMP, css[:, 2:4], css[:, 0:2], NCMP, 2)
                rsqrt(R_D, rs[:, 0:32], ss[:, 0:32], P, 32)
                pool.wait_ge(s_["rs_rdy"], R_D)
                step = 0

                def link(ins):
                    after(ins, "rope_step")
                    pool.wait_ge(s_["rope_step"], step + 1)
                rsd = rs[:, 0:32].rearrange("p (t h) -> p t h", t=NT)
                for j in range(2):
                    v = dqk[j]
                    link(G.tensor_tensor(v, v, rsd[:, :, 4 * j:4 * j + 4].unsqueeze(3).broadcast_to([P, NT, 4, MQK]), ALU.mult))
                    step += 1
                    link(G.tensor_tensor(v, v, g_qk[:, j, :].unsqueeze(1).unsqueeze(1).broadcast_to([P, NT, 4, MQK]), ALU.mult))
                    step += 1
                    x1, x2 = v[:, :, :, NOPE:NOPE + HALF], v[:, :, :, NOPE + HALF:]
                    cos, sin = [con[:, c:c + 64].rearrange("p (t f) -> p t f", t=NT).unsqueeze(2).broadcast_to([P, NT, 4, HALF]) for c in (C_COS, C_SIN)]
                    G.tensor_tensor(dtm[0], x1, cos, ALU.mult)
                    G.tensor_tensor(dtm[1], x2, sin, ALU.mult)
                    G.tensor_tensor(dtm[2], x1, sin, ALU.mult)
                    link(G.tensor_tensor(dtm[3], x2, cos, ALU.mult))
                    step += 1
                    G.tensor_tensor(x1, dtm[0], dtm[1], ALU.subtract)
                    ins = G.tensor_tensor(x2, dtm[2], dtm[3], ALU.add)
                    if j == 0:
                        link(ins)
                        step += 1
                after(ins, "dqk_rdy")
                with pool.If(l < 1):
                    pool.wait_ge(zeros_rdy, 1)

                    def clear(rows, n):
                        pool.dma_start(rows.rearrange("(p r) (c w) -> p (r c) w", p=P, w=256), zero[:, :].unsqueeze(1).broadcast_to([P, 4 * n, 256])).then_inc(zeroed, 16)
                    for rows in parts:
                        clear(rows, rows.shape[0] // P)
                    for rows in (xs_dram, ys_dram):
                        if NSLOT % P:
                            pool.dma_start(rows[NSLOT // P * P:, :].rearrange("p (c w) -> p c w", w=256), zero[0:NSLOT % P, :].unsqueeze(1).broadcast_to([NSLOT % P, 4, 256])).then_inc(zeroed, 16)
                pool.wait_ge(s_["ms_rdy"], R_G)
                after(G.tensor_tensor(by_group(rs), by_group(ss), by_group(neghalf), ALU.pow), "rs_rdy")
                pool.wait_ge(s_["rs_rdy"], R_G)
                og = xo[:, :].rearrange("p (t g c) -> p t g c", t=NT, g=4)[:, :, 0:3, :]
                after(G.tensor_tensor(og, og, by_group(rs).unsqueeze(3).broadcast_to([P, NT, 3, 256]), ALU.mult), "og_rdy")
                rsqrt(R_O, rs[:, 35:48:4], ss[:, 35:48:4], P, NT)
                rsqrt(R_X2, rs[:, 0:NT - 1], ss[:, 0:NT - 1], P, NT - 1)
                rsqrt(R_X2 + 1, rs[:, NT - 1:NT], ss[:, NT - 1:NT], P, 1)
                pool.wait_ge(zeroed, 16 * n_zero)
                pool.wait_ge(s_["slots_rdy"], 1)
                for t in range(NT):
                    for j in range(2):
                        pool.indirect_dma_start(xs_dram, bass.IndirectOffsetOnAxis(ap=sloti[:, j, t:t + 1], axis=0), xoc[:, t, :], None).then_inc(scat, 16)
                for s in range(2):
                    pool.wait_ge(s_[f"yst{s}"], 32 * NE // 2)
                pool.wait_ge(s_["over_rdy"], 1)
                n_over = pool.value_load(overi[0:1, 15:16], min_val=0, max_val=NOVER)
                with pool.If(n_over > 0):
                    pool.wait_ge(s_["f_end"], n_over)
                for t in range(NT):
                    for j in range(2):
                        pool.indirect_dma_start(yg[2 * t + j], None, ys_dram, bass.IndirectOffsetOnAxis(ap=sloti[:, j, t:t + 1], axis=0)).then_inc(gath[2 * t + j], 16)
                pool.wait_ge(s_["comb"], 2 * NT)
                for n in per_layer[:4]:
                    pool.wait_ge(s_[n], 1)
                first = s_[per_layer[0]].num
                pool.sem_clear(range(first, first + len(per_layer)))
                pool.sem_inc(layer_open, 1)
    return nc


_INS = ["x", "rel_bias", "attn_norm", "w_in", "swa_q_norm", "swa_k_norm", "swa_sinks", "nsa_q_norm", "nsa_k_norm",
        "nsa_cmp_pos", "nsa_cmp_w1", "nsa_cmp_w2", "mla_q_lat_norm", "mla_w_q_up", "mla_kv_lat_norm", "mla_w_kv_up",
        "mla_q_norm", "mla_k_norm", "out_norm", "w_out", "ffn_norm", "moe_w_group", "moe_b_group", "moe_w_expert",
        "moe_b_expert", "moe_w_gate", "moe_w_up", "moe_w_down"]


def kernel(**inputs):
    import concourse.bacc as _bacc
    from concourse.bass_utils import run_bass_kernel_spmd as _run

    nc = _bacc.Bacc("TRN2", target_bir_lowering=False, num_devices=1)
    arrays, args = {}, {}

    def put(name, v):
        v = np.ascontiguousarray(v)
        arrays["in_" + name] = v
        return nc.dram_tensor("in_" + name, v.shape, mybir.dt.from_np(v.dtype), kind="ExternalInput").ap()
    for name in _INS:
        args[name] = put(name, inputs[name])
    c, m = constants()
    out = nc.dram_tensor("out_0", (1, T, D), F32, kind="ExternalOutput").ap()
    rows = nc.dram_tensor("bias_rows", (4, P, TN + TS), F32, kind="Internal").ap()
    xs = nc.dram_tensor("expert_in", (NSLOT, D), F32, kind="Internal").ap()
    ys = nc.dram_tensor("expert_out", (NSLOT, D), F32, kind="Internal").ap()
    build(nc, args, put("consts", c), put("bias_map", m), out, rows, xs, ys)
    r = _run(nc, [arrays], core_ids=[0])
    return r.results[0]["out_0"]
```
